# Optimizing a Trainium2 kernel written in Bass

```python
import math
import jax
import jax.numpy as jnp
from jax import lax
import numpy as np

D_MODEL = 1024
BATCH = 1
SEQ = 512
DEPTH = 2

GRID_W = 64
CTX_LEN = 256
EPS = 1e-6
F32 = jnp.float32
HEAD_DIM = 64
GROUP_W = D_MODEL // 2
D_FF = 256 * ((8 * D_MODEL // 3 + 255) // 256)
N_MOD = 9

NA_HEADS = GROUP_W // HEAD_DIM
NA_WIN_R = 8
NA_WIN_C = 16
NA_QBLK = 16
NA_STRIP = NA_QBLK + NA_WIN_C

SSD_HEADS = GROUP_W // HEAD_DIM
SSD_P = HEAD_DIM
SSD_GROUPS = 2
SSD_STATE = 128
SSD_CONV = 4
SSD_CHUNK = 128
SSD_CONV_CH = GROUP_W + 2 * SSD_GROUPS * SSD_STATE

LRU_W = GROUP_W
LRU_BLOCKS = LRU_W // HEAD_DIM
LRU_BS = LRU_W // LRU_BLOCKS
LRU_CONV = 4
LRU_C = 8.0

DIFF_HEADS = GROUP_W // (2 * HEAD_DIM)
DIFF_QBLK = 128
ROPE_BASE = 10000.0

AB_SPLITS = (GROUP_W, GROUP_W, GROUP_W, GROUP_W, SSD_CONV_CH, 2 * SSD_HEADS)
AB_IN = sum(AB_SPLITS)
CD_SPLITS = (LRU_W, LRU_W, GROUP_W, GROUP_W, GROUP_W)
CD_IN = sum(CD_SPLITS)

kernel_name = 'hybrid_na_ssd_rglru_diffattn_prefix_dit'

def _split(u, sizes):
    return jnp.split(u, [int(s) for s in np.cumsum(sizes)[:-1]], axis=-1)

def rms_norm(x, g):
    xf = x.astype(F32)
    y = xf * lax.rsqrt(jnp.mean(xf * xf, axis=-1, keepdims=True) + EPS)
    return (y * g.astype(F32)).astype(x.dtype)

def _modulate(h, g, m, k):
    return (rms_norm(h, g) * (1 + m[:, :, 3 * k + 1]) + m[:, :, 3 * k]).astype(h.dtype)

def swiglu(h, w1, w3, w2):
    return (jax.nn.silu(h @ w1) * (h @ w3)) @ w2

def _half_ffn(h, g, m, k, w1, w3, w2):
    y = swiglu(_modulate(h, g, m, k), w1, w3, w2)
    return h + (0.5 * m[:, :, 3 * k + 2] * y).astype(h.dtype)

def dwconv_centred(x, w, b):
    K, C = w.shape
    left = K // 2
    y = lax.conv_general_dilated(x, w[:, None, :].astype(x.dtype), window_strides=(1,),
                                 padding=[(left, K - 1 - left)],
                                 dimension_numbers=('NWC', 'WIO', 'NWC'), feature_group_count=C)
    return y + b.astype(x.dtype)

def axial_rope(L, d):
    t = jnp.arange(L)
    row = (t // GRID_W).astype(F32)
    col = (t % GRID_W).astype(F32)
    n = d // 4
    inv = ROPE_BASE ** (-jnp.arange(n, dtype=F32) / n)
    ang = jnp.concatenate([row[:, None] * inv, col[:, None] * inv], axis=-1)
    return jnp.cos(ang), jnp.sin(ang)

def apply_rope(x, cos, sin):
    L = x.shape[1]
    shp = (1, L) + (1,) * (x.ndim - 3) + (cos.shape[-1],)
    cs, sn = cos.reshape(shp), sin.reshape(shp)
    xr = x.astype(F32).reshape(x.shape[:-1] + (-1, 2))
    x1, x2 = xr[..., 0], xr[..., 1]
    out = jnp.stack([x1 * cs - x2 * sn, x1 * sn + x2 * cs], axis=-1)
    return out.reshape(x.shape).astype(x.dtype)

def softmax_attn(q, k, v):
    s = jnp.einsum('bqhd,bkhd->bhqk', q, k, preferred_element_type=F32) * (q.shape[-1] ** -0.5)
    p = jax.nn.softmax(s, axis=-1)
    return jnp.einsum('bhqk,bkhd->bqhd', p, v.astype(F32)).astype(q.dtype)

def neighborhood_attention(q, k, v, kc, vc, rpb):
    Bsz, S, H, d = q.shape
    rows = S // GRID_W
    kr = min(NA_WIN_R, rows)
    ncb = GRID_W // NA_QBLK
    scale = d ** -0.5
    qcols = jnp.arange(GRID_W).reshape(ncb, NA_QBLK)
    qc0 = jnp.clip(qcols - NA_WIN_C // 2, 0, GRID_W - NA_WIN_C)
    strip0 = jnp.clip(jnp.arange(ncb) * NA_QBLK - NA_WIN_C // 2, 0, GRID_W - NA_STRIP)
    strip_cols = strip0[:, None] + jnp.arange(NA_STRIP)[None, :]
    kcol = strip_cols[:, None, :]
    col_in = (kcol >= qc0[..., None]) & (kcol < qc0[..., None] + NA_WIN_C)
    dc = jnp.clip(kcol - qcols[..., None] + NA_WIN_C - 1, 0, 2 * NA_WIN_C - 2)
    mask = col_in[None, None, :, :, None, :]

    def row_block(args):
        q_row, r = args
        r0 = jnp.clip(r - kr // 2, 0, rows - kr)
        k_rows = lax.dynamic_slice_in_dim(k, r0 * GRID_W, kr * GRID_W, axis=1).reshape(Bsz, kr, GRID_W, H, d)
        v_rows = lax.dynamic_slice_in_dim(v, r0 * GRID_W, kr * GRID_W, axis=1).reshape(Bsz, kr, GRID_W, H, d)
        k_s = jnp.take(k_rows, strip_cols, axis=2)
        v_s = jnp.take(v_rows, strip_cols, axis=2)
        qb = q_row.reshape(Bsz, ncb, NA_QBLK, H, d)
        dr = r0 + jnp.arange(kr) - r + NA_WIN_R - 1
        bias = rpb[:, dr[:, None, None, None], dc[None]].transpose(0, 2, 3, 1, 4)
        s_lat = jnp.einsum('bnqhd,bknshd->bhnqks', qb, k_s, preferred_element_type=F32) * scale + bias[None].astype(F32)
        s_lat = jnp.where(mask, s_lat, -jnp.inf).reshape(Bsz, H, ncb, NA_QBLK, kr * NA_STRIP)
        s_ctx = jnp.einsum('bnqhd,bchd->bhnqc', qb, kc, preferred_element_type=F32) * scale
        p = jax.nn.softmax(jnp.concatenate([s_lat, s_ctx], axis=-1), axis=-1)
        p_lat = p[..., :kr * NA_STRIP].reshape(Bsz, H, ncb, NA_QBLK, kr, NA_STRIP)
        p_ctx = p[..., kr * NA_STRIP:]
        o = (jnp.einsum('bhnqks,bknshd->bnqhd', p_lat, v_s.astype(F32))
             + jnp.einsum('bhnqc,bchd->bnqhd', p_ctx, vc.astype(F32)))
        return o.reshape(Bsz, GRID_W, H, d).astype(q.dtype)

    q_rows = jnp.moveaxis(q.reshape(Bsz, rows, GRID_W, H, d), 1, 0)
    o = lax.map(row_block, (q_rows, jnp.arange(rows)))
    return jnp.moveaxis(o, 0, 1).reshape(Bsz, S, H, d)

def ssd_scan(x, dt, A, Bm, Cm, h0):
    Bsz, L, H, P = x.shape
    G, N = Bm.shape[2], Bm.shape[3]
    R = H // G
    Q = SSD_CHUNK
    nc = L // Q
    x = x.astype(F32).reshape(Bsz, nc, Q, G, R, P)
    dt = dt.reshape(Bsz, nc, Q, G, R)
    Bm = Bm.astype(F32).reshape(Bsz, nc, Q, G, N)
    Cm = Cm.astype(F32).reshape(Bsz, nc, Q, G, N)
    a_cs = jnp.cumsum(dt * A.reshape(G, R), axis=2).transpose(0, 1, 3, 4, 2)
    tri = jnp.tril(jnp.ones((Q, Q), dtype=bool))
    decay_in = jnp.exp(jnp.where(tri, a_cs[..., :, None] - a_cs[..., None, :], -jnp.inf))
    xdt = x * dt[..., None]
    cb = jnp.einsum('bcign,bcjgn->bcgij', Cm, Bm)
    y_diag = jnp.einsum('bcgij,bcgrij,bcjgrp->bcigrp', cb, decay_in, xdt)
    decay_end = jnp.exp(a_cs[..., -1:] - a_cs)
    states = jnp.einsum('bcjgn,bcgrj,bcjgrp->bcgrpn', Bm, decay_end, xdt)
    chunk_decay = jnp.exp(a_cs[..., -1])

    def step(h, inp):
        s, dcy = inp
        return h * dcy[..., None, None] + s, h

    h_last, h_start = lax.scan(step, h0.astype(F32).reshape(Bsz, G, R, P, N),
                               (jnp.moveaxis(states, 1, 0), jnp.moveaxis(chunk_decay, 1, 0)))
    h_start = jnp.moveaxis(h_start, 0, 1)
    y_off = jnp.einsum('bcign,bcgrpn,bcgri->bcigrp', Cm, h_start, jnp.exp(a_cs))
    y = (y_diag + y_off).reshape(Bsz, L, H, P)
    return y, h_last.reshape(Bsz, H, P, N)

def ssd_branch(xbc, dt_raw, conv_w, conv_b, dt_bias, a_log, d_skip, h0_f, h0_b):
    Bsz, L, _ = xbc.shape
    xbc = jax.nn.silu(dwconv_centred(xbc, conv_w, conv_b))
    xs, bm, cm = _split(xbc, (GROUP_W, SSD_GROUPS * SSD_STATE, SSD_GROUPS * SSD_STATE))
    xs = xs.reshape(Bsz, L, SSD_HEADS, SSD_P)
    bm = bm.reshape(Bsz, L, SSD_GROUPS, SSD_STATE)
    cm = cm.reshape(Bsz, L, SSD_GROUPS, SSD_STATE)
    dt = jax.nn.softplus(dt_raw.astype(F32).reshape(Bsz, L, 2, SSD_HEADS) + dt_bias.astype(F32))
    A = -jnp.exp(a_log.astype(F32))
    flip = lambda t: jnp.flip(t, axis=1)
    y_f, hf = ssd_scan(xs, dt[:, :, 0], A[0], bm, cm, h0_f)
    y_b, hb = ssd_scan(flip(xs), flip(dt[:, :, 1]), A[1], flip(bm), flip(cm), h0_b)
    y = y_f + flip(y_b) + d_skip.astype(F32)[:, None] * xs.astype(F32)
    return y, hf, hb

def rglru_scan(x, wa, ba, wx, bx, lam, h0):
    Bsz, L, W = x.shape
    xf = x.astype(F32)
    xb = xf.reshape(Bsz, L, LRU_BLOCKS, LRU_BS)
    r = jax.nn.sigmoid(jnp.einsum('blnd,nde->blne', xb, wa.astype(F32)).reshape(Bsz, L, W) + ba.astype(F32))
    i = jax.nn.sigmoid(jnp.einsum('blnd,nde->blne', xb, wx.astype(F32)).reshape(Bsz, L, W) + bx.astype(F32))
    log_a = -LRU_C * r * jax.nn.softplus(-lam.astype(F32))
    a = jnp.exp(log_a)
    b = jnp.sqrt(-jnp.expm1(2 * log_a)) * (i * xf)
    b = b.at[:, 0].add(a[:, 0] * h0)

    def combine(u, v):
        return u[0] * v[0], v[0] * u[1] + v[1]

    _, h = lax.associative_scan(combine, (a, b), axis=1)
    return h, h[:, -1]

def rglru_bidir(x, wa, ba, wx, bx, lam, h0_f, h0_b):
    h_f, last_f = rglru_scan(x, wa[0], ba[0], wx[0], bx[0], lam[0], h0_f)
    h_b, last_b = rglru_scan(jnp.flip(x, axis=1), wa[1], ba[1], wx[1], bx[1], lam[1], h0_b)
    return h_f + jnp.flip(h_b, axis=1), last_f, last_b

def diff_attn_core(qb, k, v, lam):
    s = jnp.einsum('bqhtd,bkhtd->bhtqk', qb, k, preferred_element_type=F32) * (qb.shape[-1] ** -0.5)
    p = jax.nn.softmax(s, axis=-1)
    w = p[:, :, 0] - lam * p[:, :, 1]
    return jnp.einsum('bhqk,bkhe->bqhe', w, v.astype(F32))

def mixer_ab(hx, hc, w_in, w_out, q_g, k_g, rpb, conv_w, conv_b, dt_bias, a_log, d_skip, norm_g, with_ctx):
    Bsz, S, _ = hx.shape
    Lc = hc.shape[1]
    q, k, v, z, xbc, dt = _split(hx @ w_in, AB_SPLITS)
    q_c, k_c, v_c, z_c, xbc_c, dt_c = _split(hc @ w_in, AB_SPLITS)

    def heads(q, k, v):
        shp = (Bsz, q.shape[1], NA_HEADS, HEAD_DIM)
        return rms_norm(q.reshape(shp), q_g), rms_norm(k.reshape(shp), k_g), v.reshape(shp)

    q, k, v = heads(q, k, v)
    q_c, k_c, v_c = heads(q_c, k_c, v_c)
    o_na = neighborhood_attention(q, k, v, k_c, v_c, rpb)

    zeros = jnp.zeros((Bsz, SSD_HEADS, SSD_P, SSD_STATE), F32)
    y_c, hf_c, hb_c = ssd_branch(xbc_c, dt_c, conv_w, conv_b, dt_bias, a_log, d_skip, zeros, zeros)
    y_s, _, _ = ssd_branch(xbc, dt, conv_w, conv_b, dt_bias, a_log, d_skip, hf_c, hb_c)

    def gated(y, zz):
        return rms_norm(y.reshape(Bsz, y.shape[1], GROUP_W) * jax.nn.silu(zz.astype(F32)), norm_g).astype(hx.dtype)

    y = jnp.concatenate([o_na.reshape(Bsz, S, GROUP_W), gated(y_s, z)], axis=-1) @ w_out
    yc = None
    if with_ctx:
        o_c = softmax_attn(q_c, k_c, v_c)
        yc = jnp.concatenate([o_c.reshape(Bsz, Lc, GROUP_W), gated(y_c, z_c)], axis=-1) @ w_out
    return y, yc

def mixer_cd(hx, hc, w_in, w_out, conv_w, conv_b, wa, ba, wx, bx, lam_p, q_g, k_g, diff_lam, subln_g, lam_init, with_ctx):
    Bsz, S, _ = hx.shape
    Lc = hc.shape[1]
    gate, xr, q, k, v = _split(hx @ w_in, CD_SPLITS)
    gate_c, xr_c, q_c, k_c, v_c = _split(hc @ w_in, CD_SPLITS)

    xr_c = dwconv_centred(xr_c, conv_w, conv_b)
    xr = dwconv_centred(xr, conv_w, conv_b)
    zeros = jnp.zeros((Bsz, LRU_W), F32)
    h_c, hf_c, hb_c = rglru_bidir(xr_c, wa, ba, wx, bx, lam_p, zeros, zeros)
    h, _, _ = rglru_bidir(xr, wa, ba, wx, bx, lam_p, hf_c, hb_c)
    out_c = (jax.nn.gelu(gate.astype(F32)) * h).astype(hx.dtype)

    lam = (jnp.exp(jnp.sum(diff_lam[0].astype(F32) * diff_lam[1].astype(F32)))
           - jnp.exp(jnp.sum(diff_lam[2].astype(F32) * diff_lam[3].astype(F32))) + lam_init)

    def heads(q, k, v):
        L = q.shape[1]
        shp = (Bsz, L, DIFF_HEADS, 2, HEAD_DIM)
        return (rms_norm(q.reshape(shp), q_g), rms_norm(k.reshape(shp), k_g),
                v.reshape(Bsz, L, DIFF_HEADS, 2 * HEAD_DIM))

    q, k, v = heads(q, k, v)
    q_c, k_c, v_c = heads(q_c, k_c, v_c)
    cos, sin = axial_rope(S, HEAD_DIM)
    q = apply_rope(q, cos, sin)
    k = apply_rope(k, cos, sin)
    k_all = jnp.concatenate([k_c, k], axis=1)
    v_all = jnp.concatenate([v_c, v], axis=1)
    nb = S // DIFF_QBLK
    q_blocks = jnp.moveaxis(q.reshape(Bsz, nb, DIFF_QBLK, DIFF_HEADS, 2, HEAD_DIM), 1, 0)
    o = lax.map(lambda qb: diff_attn_core(qb, k_all, v_all, lam), q_blocks)
    o = jnp.moveaxis(o, 0, 1).reshape(Bsz, S, DIFF_HEADS, 2 * HEAD_DIM)
    o = (rms_norm(o, subln_g) * (1 - lam_init)).reshape(Bsz, S, GROUP_W).astype(hx.dtype)
    y = jnp.concatenate([out_c, o], axis=-1) @ w_out
    yc = None
    if with_ctx:
        oc = diff_attn_core(q_c, k_c, v_c, lam)
        oc = (rms_norm(oc, subln_g) * (1 - lam_init)).reshape(Bsz, Lc, GROUP_W).astype(hc.dtype)
        oc_lru = (jax.nn.gelu(gate_c.astype(F32)) * h_c).astype(hc.dtype)
        yc = jnp.concatenate([oc_lru, oc], axis=-1) @ w_out
    return y, yc

def setup_inputs(seed: int = 0) -> dict:
    key = jax.random.key(seed)
    ks = list(jax.random.split(key, 40))
    cnt = [0]

    def nk():
        cnt[0] += 1
        return ks[cnt[0] - 1]

    def nrm(shape, s):
        return jax.random.normal(nk(), shape, F32) * s

    D = D_MODEL
    NE = (DEPTH + 1) // 2
    NO = DEPTH // 2
    x = nrm((BATCH, SEQ, D), 1.0)
    c = nrm((BATCH, D), 1.0)
    ctx = nrm((BATCH, CTX_LEN, D), 1.0)
    c_ctx = nrm((D,), 1.0)
    w_mod = nrm((DEPTH, D, N_MOD * D), 0.5 * D ** -0.5)
    b_mod = nrm((DEPTH, N_MOD * D), 0.01)
    norm_g = 1.0 + nrm((DEPTH, 3, D), 0.02)
    ffn_w1 = nrm((DEPTH, 2, D, D_FF), D ** -0.5)
    ffn_w3 = nrm((DEPTH, 2, D, D_FF), D ** -0.5)
    ffn_w2 = nrm((DEPTH, 2, D_FF, D), D_FF ** -0.5)
    ab_w_in = nrm((NE, D, AB_IN), D ** -0.5)
    ab_w_out = nrm((NE, 2 * GROUP_W, D), (2 * GROUP_W) ** -0.5)
    na_q_g = 1.0 + nrm((NE, HEAD_DIM), 0.02)
    na_k_g = 1.0 + nrm((NE, HEAD_DIM), 0.02)
    na_rpb = nrm((NE, NA_HEADS, 2 * NA_WIN_R - 1, 2 * NA_WIN_C - 1), 0.2)
    ssd_conv_w = nrm((NE, SSD_CONV, SSD_CONV_CH), SSD_CONV ** -0.5)
    ssd_conv_b = nrm((NE, SSD_CONV_CH), 0.01)
    dt0 = jnp.exp(jax.random.uniform(nk(), (NE, 2, SSD_HEADS), F32, math.log(1e-3), math.log(1e-1)))
    ssd_dt_bias = dt0 + jnp.log(-jnp.expm1(-dt0))
    ssd_a_log = jnp.log(jax.random.uniform(nk(), (NE, 2, SSD_HEADS), F32, 1.0, 16.0))
    ssd_d = 1.0 + nrm((NE, SSD_HEADS), 0.1)
    ssd_norm_g = 1.0 + nrm((NE, GROUP_W), 0.02)
    cd_w_in = nrm((NO, D, CD_IN), D ** -0.5)
    cd_w_out = nrm((NO, 2 * GROUP_W, D), (2 * GROUP_W) ** -0.5)
    lru_conv_w = nrm((NO, LRU_CONV, LRU_W), LRU_CONV ** -0.5)
    lru_conv_b = nrm((NO, LRU_W), 0.01)
    lru_wa = nrm((NO, 2, LRU_BLOCKS, LRU_BS, LRU_BS), LRU_BS ** -0.5)
    lru_ba = nrm((NO, 2, LRU_W), 0.1)
    lru_wx = nrm((NO, 2, LRU_BLOCKS, LRU_BS, LRU_BS), LRU_BS ** -0.5)
    lru_bx = nrm((NO, 2, LRU_W), 0.1)
    u = jax.random.uniform(nk(), (NO, 2, LRU_W), F32, 0.9, 0.999) ** (1.0 / LRU_C)
    lru_lambda = jnp.log(u) - jnp.log1p(-u)
    diff_q_g = 1.0 + nrm((NO, HEAD_DIM), 0.02)
    diff_k_g = 1.0 + nrm((NO, HEAD_DIM), 0.02)
    diff_lambda = nrm((NO, 4, HEAD_DIM), 0.1)
    diff_subln_g = 1.0 + nrm((NO, 2 * HEAD_DIM), 0.02)
    return {'x': x, 'c': c, 'ctx': ctx, 'c_ctx': c_ctx, 'w_mod': w_mod, 'b_mod': b_mod, 'norm_g': norm_g,
            'ffn_w1': ffn_w1, 'ffn_w3': ffn_w3, 'ffn_w2': ffn_w2, 'ab_w_in': ab_w_in, 'ab_w_out': ab_w_out,
            'na_q_g': na_q_g, 'na_k_g': na_k_g, 'na_rpb': na_rpb, 'ssd_conv_w': ssd_conv_w,
            'ssd_conv_b': ssd_conv_b, 'ssd_dt_bias': ssd_dt_bias, 'ssd_a_log': ssd_a_log, 'ssd_d': ssd_d,
            'ssd_norm_g': ssd_norm_g, 'cd_w_in': cd_w_in, 'cd_w_out': cd_w_out, 'lru_conv_w': lru_conv_w,
            'lru_conv_b': lru_conv_b, 'lru_wa': lru_wa, 'lru_ba': lru_ba, 'lru_wx': lru_wx, 'lru_bx': lru_bx,
            'lru_lambda': lru_lambda, 'diff_q_g': diff_q_g, 'diff_k_g': diff_k_g, 'diff_lambda': diff_lambda,
            'diff_subln_g': diff_subln_g}

def reference(x, c, ctx, c_ctx, w_mod, b_mod, norm_g, ffn_w1, ffn_w3, ffn_w2, ab_w_in, ab_w_out,
              na_q_g, na_k_g, na_rpb, ssd_conv_w, ssd_conv_b, ssd_dt_bias, ssd_a_log, ssd_d, ssd_norm_g,
              cd_w_in, cd_w_out, lru_conv_w, lru_conv_b, lru_wa, lru_ba, lru_wx, lru_bx, lru_lambda,
              diff_q_g, diff_k_g, diff_lambda, diff_subln_g):
    Bsz = x.shape[0]
    sc = jax.nn.silu(c.astype(F32))
    scc = jax.nn.silu(c_ctx.astype(F32))
    xc = ctx
    for i in range(DEPTH):
        last = i == DEPTH - 1
        j = i // 2
        m = (sc @ w_mod[i].astype(F32) + b_mod[i].astype(F32)).reshape(Bsz, 1, N_MOD, D_MODEL)
        mc = (scc @ w_mod[i].astype(F32) + b_mod[i].astype(F32)).reshape(1, 1, N_MOD, D_MODEL)
        x = _half_ffn(x, norm_g[i, 0], m, 0, ffn_w1[i, 0], ffn_w3[i, 0], ffn_w2[i, 0])
        xc = _half_ffn(xc, norm_g[i, 0], mc, 0, ffn_w1[i, 0], ffn_w3[i, 0], ffn_w2[i, 0])
        hx = _modulate(x, norm_g[i, 1], m, 1)
        hc = _modulate(xc, norm_g[i, 1], mc, 1)
        if i % 2 == 0:
            y, yc = mixer_ab(hx, hc, ab_w_in[j], ab_w_out[j], na_q_g[j], na_k_g[j], na_rpb[j],
                             ssd_conv_w[j], ssd_conv_b[j], ssd_dt_bias[j], ssd_a_log[j], ssd_d[j],
                             ssd_norm_g[j], not last)
        else:
            lam_init = 0.8 - 0.6 * math.exp(-0.3 * i)
            y, yc = mixer_cd(hx, hc, cd_w_in[j], cd_w_out[j], lru_conv_w[j], lru_conv_b[j], lru_wa[j],
                             lru_ba[j], lru_wx[j], lru_bx[j], lru_lambda[j], diff_q_g[j], diff_k_g[j],
                             diff_lambda[j], diff_subln_g[j], lam_init, not last)
        x = x + (m[:, :, 5] * y).astype(x.dtype)
        x = _half_ffn(x, norm_g[i, 2], m, 2, ffn_w1[i, 1], ffn_w3[i, 1], ffn_w2[i, 1])
        if not last:
            xc = xc + (mc[:, :, 5] * yc).astype(xc.dtype)
            xc = _half_ffn(xc, norm_g[i, 2], mc, 2, ffn_w1[i, 1], ffn_w3[i, 1], ffn_w2[i, 1])
    return x


_drawn_inputs = setup_inputs


def setup_inputs(seed=0):
    import zlib

    import numpy as np

    out = dict(_drawn_inputs(seed))
    spreads = {}
    factors = {'norm_g': 4.285,
     'na_q_g': 8.0,
     'na_k_g': 8.0,
     'na_rpb': 8.0,
     'ssd_conv_b': 8.0,
     'ssd_d': 56.112,
     'ssd_norm_g': 8.0,
     'lru_conv_b': 4.282,
     'lru_ba': 8.0,
     'lru_bx': 4.475,
     'diff_q_g': 8.0,
     'diff_k_g': 8.0,
     'diff_lambda': 2.77,
     'diff_subln_g': 64.0}
    for name, (base, spread) in spreads.items():
        noise = np.random.default_rng([zlib.crc32(name.encode()), seed]).standard_normal(out[name].shape)
        drawn = base * np.exp(spread * noise) if base else spread * noise
        out[name] = jnp.asarray(drawn.astype(out[name].dtype))
    for name, factor in factors.items():
        out[name] = (out[name] * factor).astype(out[name].dtype)
    return out
```

```python
from contextlib import ExitStack

import numpy as np

import concourse.bass as bass
import concourse.mybir as mybir
from concourse.alu_op_type import AluOpType as ALU

F32 = mybir.dt.float32
F32R = mybir.dt.float32r
ACT = mybir.ActivationFunctionType
AX = mybir.AxisListType

P = 128
D = 1024
NLAT, NCTX = 512, 256
T = NLAT + NCTX
KC = D // P
DFF = 2816
FC = DFF // P
FH = FC // 2
NMT = 9 * KC
EPS = 1e-6
HD = 64
NT = T // P
LT = NLAT // P
GRID_W, ROWS = 64, 8
SEGS = ((0, NLAT, 0), (NLAT, T, 1))
LSEG = ((0, NLAT, 0),)
STRIP0 = (0, 8, 24, 32)
STRIP_OFF = (0, 8, 8, 16)
RPB_PAD = 32
RPB_ROW = 31
RPB_HEAD = 15 * 31
RPB_RUN = 7 * RPB_ROW + 32 + 16
RPB_LEN = RPB_PAD + 8 * RPB_HEAD + 48
LAM_INIT = 0.8 - 0.6 * float(np.exp(-0.3))
FWD_SEQ = (4, 5, 0, 1, 2, 3)
BWD_SEQ = (5, 4, 3, 2, 1, 0)

AB_IN_T, AB_OUT_T, CD_IN_T, CD_OUT_T = 24, 8, 20, 8
UP, DOWN = 2 * FH, KC
FFN_T = 2 * (UP + DOWN)
BASE = {}
_t = 0
for _name, _n in (("ffn0", FFN_T), ("ab_in", AB_IN_T), ("ab_out", AB_OUT_T), ("ffn1", FFN_T),
                  ("ffn2", FFN_T), ("cd_in", CD_IN_T), ("cd_out", CD_OUT_T), ("ffn3", FFN_T)):
    BASE[_name] = _t
    _t += _n
N_TILES = _t

PCOL = {}
_c = 0
for _name, _n in (("bmod", 2 * NMT), ("normg", 6 * KC), ("naqg", 1), ("nakg", 1), ("scw", 32), ("scb", 8),
                  ("dtb", 16), ("alog", 16), ("ssdd", 4), ("ssdg", 4), ("lcw", 16), ("lcb", 4), ("lba", 8),
                  ("lbx", 8), ("lam", 8), ("dqg", 1), ("dkg", 1), ("subg", 1), ("dlam", 256), ("cc", 16)):
    PCOL[_name] = (_c, _c + _n)
    _c += _n
NPAR = _c
CCOL = {n: (i * P, (i + 1) * P) for i, n in enumerate(("ident", "ones", "blk", "trif", "trib", "swap"))}
NCON = 6 * P


def build(nc, dr, upto=99):
    ctx = ExitStack()
    with ctx:
        arena0 = 2048

        def at(name, shape, word, dt=F32):
            return nc.alloc_sbuf_tensor_at(name, shape, dt, offset=arena0 + 4 * word)

        w = 0
        x = at("x", [P, KC, T], w); w += KC * T
        XH = w
        xh = at("xh", [P, KC, T], w, F32R); w += KC * T
        XL = w
        xl = at("xl", [P, KC, T], w, F32R); w += KC * T
        H = w
        hh = at("hh", [P, FH, T], w, F32R); w += FH * T
        hl = at("hl", [P, FH, T], w, F32R); w += FH * T
        MR = w
        mraw = at("mraw", [P, 3, D], w); w += 3 * D
        raw = [at(f"raw{s}", [P, FH * P], w + s * FH * P) for s in range(2)]; w += 2 * FH * P
        wh = [at(f"wh{s}", [P, FH * P], w + s * FH * P, F32R) for s in range(2)]; w += 2 * FH * P
        wl = [at(f"wl{s}", [P, FH * P], w + s * FH * P, F32R) for s in range(2)]; w += 2 * FH * P
        TB = w
        tmp = [at(f"tmp{s}", [P, T], w + s * T) for s in range(4)]; w += 4 * T + 32
        g1s, hf = tmp[0], tmp[1]
        vn = (tmp[0], tmp[1])
        yn = (tmp[2], tmp[3])
        SQ = w
        sq = [at(f"sq{s}", [P, T], w + s * T) for s in range(2)]; w += 2 * T
        ssq = at("ssq", [P, T], w); w += T
        rstd = at("rstd", [P, T], w); w += T
        con = at("con", [P, NCON], w); w += NCON
        par = at("par", [P, NPAR], w); w += (NPAR + 7) // 8 * 8
        M = at("M", [P, 2 * NMT, 2], w); w += 4 * NMT
        modA = at("modA", [P, 6, KC, 2], w); w += 6 * KC * 2
        modG = at("modG", [P, 6, KC, 2], w); w += 6 * KC * 2
        sc = at("sc", [P, KC, 2], w); w += 2 * KC
        eps = at("eps", [P, 1], w); w += 8
        mcol = at("mcol", [P, 3, 2], w); w += 8
        FREE = w
        LIMIT = (229368 - arena0) // 4

        def cst(n):
            return con[:, CCOL[n][0]:CCOL[n][1]]

        def pr(n):
            return par[:, PCOL[n][0]:PCOL[n][1]]

        mini = [at(f"mini{s}", [P, 4, D], H + s * 4 * D) for s in range(4)]
        scb0 = at("scb0", [P, 2, D], MR)
        scb = at("scb", [P, 2, D], SQ)

        w = H
        kq = at("kq", [P, 8, T], w); w += 8 * T
        zs = at("zs", [P, 4, T], w); w += 4 * T
        cv = at("cv", [P, 8, T], w); w += 8 * T
        VT0 = w
        vT = at("vT", [P, 4, T], w); w += 4 * T
        assert w <= MR + 3 * D
        ABX = w
        pad = [at(f"pad{s}", [P, 774], TB + s * 776) for s in range(2)]
        cb = [at(f"cb{s}", [P, 771], TB + (2 + s) * 776) for s in range(2)]
        vsa = at("vsa", [P, 6, 512], XH + 4 * T)
        vsb = at("vsb", [P, 4, 512], XL + 4 * T)
        nsS = [at(f"nsS{s}", [P, 512], VT0 + s * 512) for s in range(2)]
        nsP = [at(f"nsP{s}", [P, 512], VT0 + 1024 + s * 512) for s in range(2)]
        nsT = [at(f"nsT{s}", [P, 512], VT0 + 2048 + s * 512) for s in range(2)]
        rb = at("rb", [P, 8, RPB_RUN], SQ)
        bm = [at(f"bm{s}", [P, 512], TB + s * 512) for s in range(2)]
        namask = at("namask", [P, 3, 256], TB + 1024)
        onorm = [at(f"onorm{s}", [P, 512], TB + 1792 + s * 512) for s in range(2)]
        vst = [at(f"vst{s}", [P, 512], ABX + s * 512) for s in range(2)]
        nst = at("nst", [P, 4, 8], TB + 2816)
        xst = at("xst", [P, NT, 512], H)
        bst = at("bst", [P, NT, 256], H + 3072)
        xw = [at(f"xw{s}", [P, 512], H + 4608 + s * 512) for s in range(2)]
        hm = at("hm", [P, 512], H + 5632)
        hsa = at("hsa", [P, 6, 512], XH + 4 * T)
        hsb = at("hsb", [P, 4, 512], XL + 4 * T)
        hst = [[hsa[:, s, :] for s in range(5)], [hsa[:, 5, :]] + [hsb[:, s, :] for s in range(4)]]
        gy = at("gy", [P, 4, T], VT0)
        SET = (TB, SQ)
        sL = [[at(f"sL{s}{d}", [P, 512], SET[s] + 512 * d) for d in range(2)] for s in range(2)]
        sE = [[at(f"sE{s}{d}", [P, 512], SET[s] + 1024 + 512 * d) for d in range(2)] for s in range(2)]
        xdt = [[at(f"xdt{s}{d}", [P, 256], SET[s] + 2048 + 256 * d) for d in range(2)] for s in range(2)]
        cbm = [[at(f"cbm{s}{d}", [P, 128], SET[s] + 2560 + 128 * d) for d in range(2)] for s in range(2)]
        sqg = [at(f"sqg{s}", [P, T], SQ + s * T) for s in range(2)]
        lng, rsg = at("lng", [P, T], TB), at("rsg", [P, T], TB + T)
        vg = [at(f"vg{s}", [P, T], TB + (2 + s) * T) for s in range(2)]

        w = H
        k2 = at("k2", [P, 4, T], w); w += 4 * T
        q2 = at("q2", [P, 4, NLAT], w); w += 4 * NLAT
        LR = w
        vT2 = at("vT2", [P, 4, T], w); w += 4 * T
        vtok = at("vtok", [P, NT, 512], w); w += NT * 512
        xc = at("xc", [P, 4, T], w); w += 4 * T
        gate = at("gate", [P, 4, NLAT], w); w += 4 * NLAT
        hsum = at("hsum", [P, 4, NLAT], w); w += 4 * NLAT
        rope = at("rope", [P, 2, NLAT], w); w += 2 * NLAT
        assert w <= MR + 3 * D
        lruw = at("lruw", [P, 16, P], SQ)
        lR, lA, lI, lX = ([at(f"{n}{d}", [P, T], (LR, XH + 4 * T)[d] + q * T) for d in range(2)]
                          for q, n in enumerate(("lR", "lA", "lI", "lX")))
        pb = [at(f"pb{s}", [P, T], TB + s * T) for s in range(2)]
        wb, wtb = at("wb", [P, T], TB + 2 * T), at("wtb", [P, T], TB + 3 * T)
        ovb = [at(f"ovb{s}", [P, 512], TB + s * T) for s in range(2)]

        fw = [FREE]

        def small(name, shape, dt=F32):
            n = 1
            for s_ in shape[1:]:
                n *= s_
            t_ = at(name, shape, fw[0], dt)
            fw[0] += (n + 7) // 8 * 8
            assert fw[0] <= LIMIT, (name, fw[0], LIMIT)
            return t_

        assert FREE <= LIMIT
        wdt, wdh, wdl = small("wdt", [P, P]), small("wdh", [P, P], F32R), small("wdl", [P, P], F32R)
        TH = [P, NT, 16]
        dtu, dte, dts, dt2, dtp, dt, dA, ea = (small(n, TH) for n in ("dtu", "dte", "dts", "dt2", "dtp", "dt", "dA", "ea"))
        acs, tm, dend, cdec = (small(n, TH) for n in ("acs", "tm", "dend", "cdec"))
        qg8 = small("qg8", [P, 2])

        G = [ctx.enter_context(nc.psum_tensor(f"G{s}", [P, 1024], F32)) for s in range(2)]
        NP = ctx.enter_context(nc.psum_tensor("NP", [P, 1024], F32))
        B67 = ctx.enter_context(nc.psum_tensor("B67", [P, 1024], F32))
        B6, B7 = B67[:, 0:512], B67[:, 512:1024]

        def sem(name):
            return ctx.enter_context(nc.semaphore(name))

        con_landed, x_landed, out_stored = sem("con_landed"), sem("x_landed"), sem("out_stored")
        raw_landed = [sem("raw_landed0"), sem("raw_landed1")]
        hi_done, lo_done, mm_done = sem("hi_done"), sem("lo_done"), sem("mm_done")
        psum_free = [sem("psum_free0"), sem("psum_free1")]
        h_hi, h_ready = sem("h_hi"), sem("h_ready")
        mini_landed = [sem(f"mini_landed{s}") for s in range(4)]
        mini_mm, mini_dot, mini_set = sem("mini_mm"), sem("mini_dot"), sem("mini_set")
        mod_landed, mod_dot, mod_prod, mod_sum, mod_set = (sem("mod_landed"), sem("mod_dot"), sem("mod_prod"),
                                                           sem("mod_sum"), sem("mod_set"))
        scb0_landed, scb0_ready, scb_landed, scb_ready = (sem("scb0_landed"), sem("scb0_ready"), sem("scb_landed"),
                                                          sem("scb_ready"))
        sc_ready, eps_set, prep_done = sem("sc_ready"), sem("eps_set"), sem("prep_done")
        sq_done, ssq_acc, norm_sum, norm_ln, rstd_ready = (sem("sq_done"), sem("ssq_acc"), sem("norm_sum"),
                                                           sem("norm_ln"), sem("rstd_ready"))
        v_ready, aff_done, xn_hi, xn_ready = sem("v_ready"), sem("aff_done"), sem("xn_hi"), sem("xn_ready")

        fw[0] = FREE
        t1b = [small(f"t1b{s}", [P, NLAT]) for s in range(2)]
        t2b = small("t2b", [P, NLAT])
        coef = small("coef", [P, 8, 8])
        dl = small("dl", [P, 8])
        dg = small("dg", [P, 4])
        st2 = small("st2", [P, 2, 8])
        qg2 = small("qg2", [P, 2])
        fw[0] = FREE
        onq = [at(f"onq{s}", [P, 512], SQ + 2048 + 512 * s) for s in range(2)]
        onq += [small(f"onq{s + 2}", [P, 512]) for s in range(2)]
        junk = small("junk", [P, P])

        wdt_landed, wdt_hi, wdt_lo, dt_mm, dt_abs, dt_exp, dt_set, dve_chain = (
            sem(n) for n in ("wdt_landed", "wdt_hi", "wdt_lo", "dt_mm", "dt_abs", "dt_exp", "dt_set", "dve_chain"))
        qg_set, kq_sq, kq_sum, kq_ln, kq_rs, kq_done = (sem(n) for n in ("qg_set", "kq_sq", "kq_sum", "kq_ln", "kq_rs", "kq_done"))
        pad_zero, conv_tap, conv_done, cv_ready = (sem(n) for n in ("pad_zero", "conv_tap", "conv_done", "cv_ready"))
        rb_landed, mask_landed, bm_zero, bm_ready = (sem(n) for n in ("rb_landed", "mask_landed", "bm_zero", "bm_ready"))
        vst_ready = sem("vst_ready")
        vt_done, vs_ready, s_done, na_biased, nmax_ready, p_ready, tr_done, pt_ready, pv_done, rinv_ready, o_read = (
            sem(n) for n in ("vt_done", "vs_ready", "s_done", "na_biased", "nmax_ready", "p_ready", "tr_done", "pt_ready",
                             "pv_done", "rinv_ready", "o_read"))
        ot_done, cat_hi, na_cat = sem("ot_done"), sem("cat_hi"), sem("na_cat")
        tk_done, tk_ready, acs_mm, acs_set, tm_set, dend_set, dw_set, xw_ready, st_mm, hm_set, h_set = (
            sem(n) for n in ("tk_done", "tk_ready", "acs_mm", "acs_set", "tm_set", "dend_set", "dw_set", "xw_ready",
                             "st_mm", "hm_set", "h_set"))
        r_mm, d_ready, l_ready, e_ready, m_ready, xdt_ready, y_mm, y_read, gz_done = (
            sem(n) for n in ("r_mm", "d_ready", "l_ready", "e_ready", "m_ready", "xdt_ready", "y_mm", "y_read", "gz_done"))
        cb_set, gsq_done, gn_sum, gn_ln, gn_rs, vg_ready, gcat_hi, ssd_cat = (
            sem(n) for n in ("cb_set", "gsq_done", "gn_sum", "gn_ln", "gn_rs", "vg_ready", "gcat_hi", "ssd_cat"))

        names = ("rope_landed lruw_landed coef_abs coef_exp coef_set dl_set dl_exp dlam_set dg_set v2_done v2_ready rope_mm "
                 "t1_ready t2_set rope_done gate_mm gate_sig lru_a lru_t lru_a2 lru_m lru_ix lru_q lru_b scan_c scan_l "
                 "lru_h lru_o lru_hi cd_cat s2_done max2_ready p2_ready rinv2 w_part w_done tr2_done wt_ready pv2_done "
                 "ss_ready ss_ln rr_ready on_done oq_done ov_ready oq_hi cd_cat2")
        (rope_landed, lruw_landed, coef_abs, coef_exp, coef_set, dl_set, dl_exp, dlam_set, dg_set, v2_done, v2_ready, rope_mm,
         t1_ready, t2_set, rope_done, gate_mm, gate_sig, lru_a, lru_t, lru_a2, lru_m, lru_ix, lru_q, lru_b, scan_c, scan_l,
         lru_h, lru_o, lru_hi, cd_cat, s2_done, max2_ready, p2_ready, rinv2, w_part, w_done, tr2_done, wt_ready, pv2_done,
         ss_ready, ss_ln, rr_ready, on_done, oq_done, ov_ready, oq_hi, cd_cat2) = (sem(n) for n in names.split())
        CD, CDO = BASE["cd_in"], BASE["cd_out"]
        NA2 = 16
        SCHED = []
        for p_ in range(4):
            SCHED += [("gates", p_), ("act", p_), ("att", 4 * p_), ("att", 4 * p_ + 1), ("root", p_), ("att", 4 * p_ + 2),
                      ("out", p_), ("att", 4 * p_ + 3)]
        SCHED += [("att", NA2), ("att", NA2 + 1)]

        AB = BASE["ab_in"]
        ABO = BASE["ab_out"]
        NU = 40

        def strip(ap, n, width, c0):
            return ap.rearrange("p (r w) -> p r w", w=GRID_W)[:, :, c0:c0 + width]

        def vtile(g):
            return vsa[:, g, :] if g < 6 else vsb[:, g - 6, :]

        def heads(col, n, width):
            return col.unsqueeze(2).to_broadcast([P, n, width])

        block = ctx.enter_context(nc.Block())

        @block.sync
        def _(sp):
            def load(t, slot, n, src, nk):
                if not (isinstance(t, int) and t < 2):
                    sp.wait_ge(lo_done, t - 1)
                sp.dma_start(raw[slot][:, 0:nk * P], src).then_inc(raw_landed[slot], 16)

            def load_tiles(base, count, dram, nk, row0=0):
                with sp.Fori(0, count // 2) as i:
                    for s in range(2):
                        src = dram[bass.ds(i * 2 + (row0 + s), 1)].rearrange("a p n -> (a p) n")
                        if base == 0:
                            sp.wait_ge(lo_done, i * 2 + (s + 1))
                            src = dram[bass.ds(i * 2 + (row0 + s + 2), 1)].rearrange("a p n -> (a p) n")
                            sp.dma_start(raw[s][:, 0:nk * P], src).then_inc(raw_landed[s], 16)
                        else:
                            load(i * 2 + (base + s), s, None, src, nk)

            def load_ffn(f, base):
                for h in range(2):
                    b = base + h * (UP + DOWN)
                    r = (f * 2 + h) * UP
                    if b == 0:
                        load_tiles(0, UP - 2, dr["w13"], KC, r)
                    else:
                        load_tiles(b, UP, dr["w13"], KC, r)
                    load_tiles(b + UP, DOWN, dr["w2"], FH, (f * 2 + h) * DOWN)

            sp.dma_start(par[:], dr["par"]).then_inc(con_landed, 16)
            sp.dma_start(con[:], dr["con"]).then_inc(con_landed, 16)
            sp.dma_start(scb0[:], dr["ccb"]).then_inc(scb0_landed, 16)
            sp.dma_start(x[:], dr["x"]).then_inc(x_landed, 16)
            sp.dma_start(wdt[:], dr["wdt"]).then_inc(wdt_landed, 16)
            for s in range(2):
                sp.dma_start(raw[s][:, 0:D], dr["w13"][s]).then_inc(raw_landed[s], 16)
            for b in range(6):
                if b == 4:
                    sp.wait_ge(mini_mm, 1)
                if b == 5:
                    sp.wait_ge(mini_dot, 8)
                src = dr["wmk"][2 * b:2 * b + 4] if b % 2 == 0 else dr["wmn"][4 * b:4 * b + 4]
                sp.dma_start(mini[b % 4][:], src.rearrange("t p n -> p t n")).then_inc(mini_landed[b % 4], 16)
            load_ffn(0, BASE["ffn0"])
            fin = BASE["ffn0"] + FFN_T
            if upto >= 1:
                load_tiles(AB, AB_IN_T, dr["abin"], KC)
                sp.wait_ge(kq_done, 8)
                for r in range(ROWS):
                    base = dr["rpb"]
                    src = bass.AP(tensor=base.tensor, offset=RPB_PAD + (7 - r) * RPB_ROW - 1,
                                  ap=[[RPB_LEN, 16], [RPB_HEAD, 8], [1, RPB_RUN]])
                    sp.dma_start(rb[16 * r:16 * r + 16, :, :], src).then_inc(rb_landed, 16)
                sp.wait_ge(cv_ready, 8)
                sp.dma_start(namask[:], dr["mask"]).then_inc(mask_landed, 16)
                load_tiles(ABO, AB_OUT_T, dr["about"], KC)
                fin = ABO + AB_OUT_T
            if upto >= 2:
                load_ffn(1, BASE["ffn1"])
                load_ffn(2, BASE["ffn2"])
                fin = BASE["ffn2"] + FFN_T if upto == 2 else N_TILES
            if upto >= 3:
                load_tiles(CD, 2, dr["cdin"], KC)
                sp.wait_ge(psum_free[0], CD // 2)
                sp.wait_ge(psum_free[1], CD // 2)
                sp.dma_start(rope[:], dr["rope"]).then_inc(rope_landed, 16)
                load_tiles(CD + 2, CD_IN_T - 2, dr["cdin"], KC, 2)
                sp.wait_ge(kq_done, 16)
                sp.dma_start(lruw[:].rearrange("p a n -> p (a n)"), dr["lruw"]).then_inc(lruw_landed, 16)
                load_tiles(CDO, CD_OUT_T, dr["cdout"], KC)
                load_ffn(3, BASE["ffn3"])
            for s in range(2):
                sp.wait_ge(psum_free[s], fin // 2)
            sp.dma_start(dr["out"], x[:, :, 0:NLAT] if upto >= 3 else x[:]).then_inc(out_stored, 16)
            sp.wait_ge(out_stored, 16)

        @block.tensor
        def _(pe):
            def gemm(t, slot, n, nk, rh, rl, segs, ready=None):
                pe.wait_ge(lo_done, t + 1)
                if not (isinstance(n, int) and n == 0):
                    pe.wait_ge(psum_free[slot], n)
                for k in range(nk):
                    if ready is not None:
                        ready(k)
                    W, L = wh[slot][:, k * P:(k + 1) * P], wl[slot][:, k * P:(k + 1) * P]
                    for a, b, _s in segs:
                        pe.matmul(G[slot][:, a:b], W, rh[:, k, a:b], start=(k == 0), stop=False)
                    for a, b, _s in segs:
                        pe.matmul(G[slot][:, a:b], W, rl[:, k, a:b], start=False, stop=False)
                    for a, b, _s in segs:
                        mm = pe.matmul(G[slot][:, a:b], L, rh[:, k, a:b], start=False, stop=(k == nk - 1))
                mm.then_inc(mm_done, 1)

            def norm(n, segs):
                pe.wait_ge(ssq_acc, 8 * (n + 1))
                for a, b, _s in segs:
                    mm = pe.matmul(NP[:, a:b], cst("ones"), ssq[:, a:b], start=True, stop=True)
                mm.then_inc(norm_sum, 1)

            def ffn(f, n, base, segs):
                for h in range(2):
                    b = base + h * (UP + DOWN)
                    hb = (2 * f + h) * FH

                    def xn(k):
                        pe.wait_ge(xn_ready, 8 * n + k + 1)

                    def hid(k):
                        pe.wait_ge(h_ready, hb + k + 1)

                    def pair(i):
                        for s in range(2):
                            gemm(i * 2 + (b + s), s, i + b // 2, KC, xh, xl, segs, xn if s == 0 else None)

                    if b == 0:
                        pair(0)
                    with pe.Fori(int(b == 0), FH) as i:
                        pair(i)
                    d = b + UP
                    with pe.Fori(0, DOWN // 2) as i:
                        for s in range(2):
                            gemm(i * 2 + (d + s), s, i + d // 2, FH, hh, hl, segs, hid if s == 0 else None)

            def ab_in_pe():
                b = AB
                for c in range(AB_IN_T):
                    gemm(b + c, c % 2, (b + c) // 2, KC, xh, xl, SEGS,
                         (lambda k: pe.wait_ge(xn_ready, 8 + k + 1)) if c == 0 else None)
                    i = c - 5
                    if 0 <= i < 8:
                        pe.wait_ge(kq_sq, i + 1)
                        if i:
                            pe.wait_ge(kq_ln, i)
                        for a, e, _s in SEGS:
                            mm = pe.matmul(NP[:, a:e], cst("blk"), sq[i % 2][:, a:e], start=True, stop=True)
                        mm.then_inc(kq_sum, 1)
                    if c == 11:
                        pe.wait_ge(wdt_lo, 1)
                        for tt in range(NT):
                            o = B6[:, 16 * tt:16 * tt + 16]
                            for k in range(KC):
                                tk = slice(P * tt, P * tt + P)
                                wk = slice(16 * k, 16 * k + 16)
                                pe.matmul(o, xh[:, k, tk], wdh[:, wk], start=(k == 0), stop=False)
                                pe.matmul(o, xl[:, k, tk], wdh[:, wk], start=False, stop=False)
                                mm = pe.matmul(o, xh[:, k, tk], wdl[:, wk], start=False, stop=(k == KC - 1))
                        mm.then_inc(dt_mm, 1)

            def na_pe():
                for s in range(2):
                    pe.wait_ge(psum_free[s], ABO // 2)
                pe.wait_ge(dt_abs, 1)
                for g in range(10):
                    if g >= 2:
                        pe.wait_ge(vs_ready, g - 1)
                    if g < 8:
                        pe.wait_ge(vst_ready, g + 1)
                    bank = (B6, B7)[g % 2]
                    for c in range(4):
                        src = (vst[g % 2][:, P * c:P * c + P] if g < 8
                               else vT[:, c, NLAT + P * (g - 8):NLAT + P * (g - 7)])
                        mm = pe.transpose(bank[:, P * c:P * c + P], src, cst("ident"))
                    mm.then_inc(vt_done, 1)

                def scores(u):
                    h, bank = u % 8, G[0][:, 512 * (u % 2):512 * (u % 2) + 512]
                    hp = slice(64 * (h % 2), 64 * (h % 2) + 64)
                    kk, qq = kq[hp, h // 2, :], kq[hp, 4 + h // 2, :]
                    if 2 <= u < 34:
                        pe.wait_ge(na_biased, u - 1)
                    if u >= 34:
                        pe.wait_ge(p_ready, u - 1)
                    if u < 32:
                        n = u // 8
                        q = qq[:, P * n:P * n + P]
                        pe.matmul(bank[:, 0:256].rearrange("p (r c) -> p r c", c=32), q,
                                  strip(kk[:, 0:NLAT], 8, 32, STRIP0[n]), start=True, stop=True)
                        mm = pe.matmul(bank[:, 256:512], q, kk[:, NLAT:T], start=True, stop=True)
                    else:
                        for w_ in range(2):
                            mm = pe.matmul(bank[:, 256 * w_:256 * w_ + 256], qq[:, NLAT + P * w_:NLAT + P * w_ + P],
                                           kk[:, NLAT:T], start=True, stop=True)
                    mm.then_inc(s_done, 1)

                def turn(u):
                    pe.wait_ge(p_ready, u + 1)
                    if u >= 2:
                        pe.wait_ge(pt_ready, u - 1)
                    for c in range(4):
                        mm = pe.transpose(G[1][:, 512 * (u % 2) + P * c:512 * (u % 2) + P * c + P],
                                          nsP[u % 2][:, P * c:P * c + P], cst("ident"))
                    mm.then_inc(tr_done, 1)

                def values(u):
                    h = u % 8
                    o = NP[:, 512 * (u % 2):512 * (u % 2) + 128]
                    pe.wait_ge(pt_ready, u + 1)
                    if u >= 2:
                        pe.wait_ge(o_read, u - 1)
                    for c in range(4):
                        if u < 32:
                            g, w_, first, last = (2 * (u // 8) + c if c < 2 else 6 + c), 0, c == 0, c == 3
                        else:
                            g, w_, first, last = 8 + c % 2, c // 2, c % 2 == 0, c % 2 == 1
                        mm = pe.matmul(o[:, 64 * w_:64 * w_ + 64], nsT[u % 2][:, P * c:P * c + P],
                                       vtile(g)[:, 64 * h:64 * h + 64], start=first, stop=last)
                    mm.then_inc(pv_done, 1)

                def turn_out(gi):
                    pe.wait_ge(o_read, min(8 * gi + 8, NU))
                    if gi >= 2:
                        pe.wait_ge(na_cat, gi - 1)
                    else:
                        pe.wait_ge(vs_ready, 10)
                    for c in range(4):
                        mm = pe.transpose((B6, B7)[gi % 2][:, P * c:P * c + P], onorm[gi % 2][:, P * c:P * c + P],
                                          cst("ident"))
                    mm.then_inc(ot_done, 1)

                pe.wait_ge(kq_done, 8)
                for it in range(NU + 4):
                    if it < NU:
                        scores(it)
                    if 0 <= it - 2 < NU:
                        turn(it - 2)
                    if 0 <= it - 3 < NU:
                        values(it - 3)
                    if it >= 12 and (it - 12) % 8 == 0 and (it - 12) // 8 < 4:
                        turn_out((it - 12) // 8)
                turn_out(4)
                turn_out(5)

            def ssd_pe():
                pe.wait_ge(cv_ready, 8)
                for q in range(9):
                    if q < 2:
                        pe.wait_ge(na_cat, 5 + q)
                    else:
                        pe.wait_ge(tk_ready, q - 1)
                    for c in range(4):
                        tt = q if q < 6 else 2 * (q - 6) + c // 2
                        src = cv[:, c if q < 6 else 4 + c % 2, P * tt:P * tt + P]
                        mm = pe.transpose((B6, B7)[q % 2][:, P * c:P * c + P], src, cst("ident"))
                    mm.then_inc(tk_done, 1)
                pe.wait_ge(dt_set, 1)
                pe.wait_ge(o_read, NU)
                aout = NP[:, 0:96].rearrange("p (t c) -> p t c", c=16)
                pe.matmul(aout[:, :, 0:8], cst("trif"), dA[:, :, 0:8], start=True, stop=True)
                pe.matmul(aout[:, :, 8:16], cst("trib"), dA[:, :, 8:16], start=True, stop=True)
                pe.matmul(NP[:, 512:608], cst("ones"), dA[:].rearrange("p t c -> p (t c)"), start=True, stop=True
                          ).then_inc(acs_mm, 1)
                pe.wait_ge(tk_ready, 9)
                pe.wait_ge(pt_ready, NU)
                for s in range(5):
                    for d in range(2):
                        e = 2 * s + d
                        tt = (FWD_SEQ, BWD_SEQ)[d][s]
                        pe.wait_ge(xw_ready, e + 1)
                        if s:
                            pe.wait_ge(h_set, e - 1)
                        for g in range(2):
                            mm = pe.matmul(G[1][:, 512 * d + 256 * g:512 * d + 256 * g + 256],
                                           bst[:, tt, P * g:P * g + P], xw[e % 2][:, 256 * g:256 * g + 256],
                                           start=True, stop=True)
                        mm.then_inc(st_mm, 1)

                def prep_y(u):
                    tt, g, st = u // 2, u % 2, u % 2
                    if u < 2:
                        if u == 0:
                            pe.wait_ge(tk_ready, 9)
                            pe.wait_ge(p_ready, NU)
                        else:
                            pe.wait_ge(h_set, 10)
                    else:
                        pe.wait_ge(e_ready, u - 1)
                        pe.wait_ge(cb_set, 2 * (u - 1))
                    tk = slice(P * tt, P * tt + P)
                    pe.matmul((B6, B7)[st][:, 0:P], cv[:, 4 + g, tk], cv[:, 6 + g, tk], start=True, stop=True)
                    for d in range(2):
                        for hh_ in range(4):
                            col = 8 * d + 4 * g + hh_
                            mm = pe.matmul(G[st][:, 512 * d + P * hh_:512 * d + P * hh_ + P],
                                           dA[:, tt, col:col + 1].to_broadcast([P, P]), cst(("trif", "trib")[d]),
                                           start=True, stop=True)
                    mm.then_inc(r_mm, 1)

                def y(u):
                    tt, g, st = u // 2, u % 2, u % 2
                    pe.wait_ge(m_ready, 4 * (u + 1))
                    pe.wait_ge(xdt_ready, 2 * (u + 1))
                    if u == 0:
                        pe.wait_ge(tm_set, 1)
                        pe.wait_ge(dend_set, 2)
                        pe.wait_ge(h_set, 10)
                    if g == 0 and tt >= 2:
                        pe.wait_ge(y_read, tt - 1)
                    for hh_ in range(4):
                        h = 4 * g + hh_
                        o = NP[64 * (h % 2):64 * (h % 2) + 64, 512 * (tt % 2) + P * (h // 2):512 * (tt % 2) + P * (h // 2) + P]
                        terms = [(xdt[st][d][:, 64 * hh_:64 * hh_ + 64], sL[st][d]) for d in range(2)]
                        for d in range(2):
                            pos = (FWD_SEQ, BWD_SEQ)[d].index(tt)
                            if pos:
                                terms.append((hst[d][pos - 1][:, 64 * h:64 * h + 64], sE[st][d]))
                        for q, (lh, rh_) in enumerate(terms):
                            mm = pe.matmul(o, lh, rh_[:, P * hh_:P * hh_ + P], start=(q == 0), stop=(q == len(terms) - 1))
                    mm.then_inc(y_mm, 1)

                prep_y(0)
                for u in range(12):
                    if u + 1 < 12:
                        prep_y(u + 1)
                    y(u)
                pe.wait_ge(y_read, 6)
                for c in range(4):
                    pe.wait_ge(gsq_done, c + 1)
                    for a, e, _s in SEGS:
                        mm = pe.matmul(NP[:, a:e], cst("ones"), sqg[c % 2][:, a:e], start=(c == 0), stop=(c == 3))
                    mm.then_inc(gn_sum, 1)

            def ab_out_pe():
                def ready(k):
                    if k == 0:
                        pe.wait_ge(na_cat, 6)
                    if k >= 4:
                        pe.wait_ge(ssd_cat, k - 3)
                pe.wait_ge(e_ready, 12)
                for c in range(AB_OUT_T):
                    gemm(ABO + c, c % 2, (ABO + c) // 2, KC, xh, xl, SEGS, ready if c == 0 else None)

            def ab_pe():
                norm(1, SEGS)
                ab_in_pe()
                na_pe()
                ssd_pe()
                ab_out_pe()

            def cd_in_pe():
                for c in range(CD_IN_T):
                    gemm(CD + c, c % 2, (CD + c) // 2, KC, xh, xl, LSEG if 8 <= c < 12 or c >= 16 else SEGS,
                         (lambda k: pe.wait_ge(xn_ready, 32 + k + 1)) if c == 0 else None)
                    if 4 <= c < 7:
                        for tt in (2 * c - 8, 2 * c - 7):
                            if tt >= 2:
                                pe.wait_ge(v2_ready, tt - 1)
                            if tt == 0:
                                for s in range(2):
                                    pe.wait_ge(psum_free[s], (CD + 4) // 2)
                            for q in range(4):
                                mm = pe.transpose((B6, B7)[tt % 2][:, P * q:P * q + P], vT2[:, q, P * tt:P * tt + P],
                                                  cst("ident"))
                            mm.then_inc(v2_done, 1)
                    i = c - 5
                    if 0 <= i < 8:
                        pe.wait_ge(kq_sq, 8 + i + 1)
                        pe.wait_ge(kq_ln, 8 + i)
                        for a, e, _s in (SEGS if i < 4 else LSEG):
                            mm = pe.matmul(NP[:, a:e], cst("blk"), sq[i % 2][:, a:e], start=True, stop=True)
                        mm.then_inc(kq_sum, 1)
                    i = c - 7
                    if 0 <= i < 8:
                        pe.wait_ge(kq_done, 8 + i + 1)
                        if i < 2:
                            pe.wait_ge(v2_ready, 6)
                        else:
                            pe.wait_ge(t2_set, i - 1)
                        src = k2[:, i, 0:NLAT] if i < 4 else q2[:, i - 4, :]
                        pe.matmul((B6, B7)[i % 2], cst("swap"), src, start=True, stop=True).then_inc(rope_mm, 1)

            def cd_mid_pe():
                for s in range(2):
                    pe.wait_ge(psum_free[s], CDO // 2)
                pe.wait_ge(lruw_landed, 16)
                pe.wait_ge(rope_done, 8)

                def gates(p_):
                    if p_:
                        pe.wait_ge(p2_ready, 8 * p_)
                    else:
                        pe.wait_ge(cv_ready, 12)
                    for d in range(2):
                        for g in range(2):
                            if d:
                                pe.wait_ge(gate_sig, 4 * p_ + 1 + g)
                            for a, e, _s in SEGS:
                                mm = pe.matmul(G[g][:, a:e], lruw[:, 8 * g + 4 * d + p_, :], xc[:, p_, a:e],
                                               start=True, stop=True)
                            mm.then_inc(gate_mm, 1)

                def scores(a):
                    qt, h = a // 4, a % 4
                    for s in range(2):
                        if a % 4 == 0:
                            pe.wait_ge(gate_sig, 4 * (a // 4) + 3 + s)
                        else:
                            pe.wait_ge(p2_ready, 2 * a + s - 1)
                        hp = slice(64 * s, 64 * s + 64)
                        for b_, e, _s in SEGS:
                            mm = pe.matmul(G[s][:, b_:e], q2[hp, h, P * qt:P * qt + P], k2[hp, h, b_:e], start=True, stop=True)
                        mm.then_inc(s2_done, 1)

                def turn(a):
                    pe.wait_ge(w_done, a + 1)
                    if a:
                        pe.wait_ge(wt_ready, a)
                    for k in range(NT):
                        mm = pe.transpose(NP[:, P * k:P * k + P], wb[:, P * k:P * k + P], cst("ident"))
                    mm.then_inc(tr2_done, 1)

                def values(a):
                    pe.wait_ge(wt_ready, a + 1)
                    if a:
                        pe.wait_ge(on_done, a)
                    h = a % 4
                    for k in range(NT):
                        mm = pe.matmul(B6[:, 0:P], wtb[:, P * k:P * k + P], vtok[:, k, P * h:P * h + P],
                                       start=(k == 0), stop=(k == NT - 1))
                    mm.then_inc(pv2_done, 1)

                for what, i in SCHED:
                    if what == "gates":
                        gates(i)
                    if what == "att":
                        if i < NA2:
                            scores(i)
                        if 1 <= i <= NA2:
                            turn(i - 1)
                            values(i - 1)
                for qt in range(4):
                    pe.wait_ge(on_done, NA2)
                    if qt >= 2:
                        pe.wait_ge(ov_ready, qt - 1)
                    for h in range(4):
                        mm = pe.transpose((B6, B7)[qt % 2][:, P * h:P * h + P], onq[qt][:, P * h:P * h + P], cst("ident"))
                    mm.then_inc(oq_done, 1)

            def cd_out_pe():
                def ready(k):
                    if k == 0:
                        pe.wait_ge(cd_cat, 4)
                    if k == 4:
                        pe.wait_ge(cd_cat2, 4)
                for c in range(CD_OUT_T):
                    gemm(CDO + c, c % 2, (CDO + c) // 2, KC, xh, xl, LSEG, ready if c == 0 else None)

            def cd_pe():
                cd_in_pe()
                cd_mid_pe()
                cd_out_pe()

            pe.wait_ge(sc_ready, 1)
            for b in (0, 2, 4):
                pe.wait_ge(mini_landed[b % 4], 16 * (b // 4 + 1))
                for j in range(4):
                    for k in range(KC):
                        c0 = 2 * (4 * b + j)
                        mm = pe.matmul(G[0][:, c0:c0 + 2], mini[b % 4][:, j, k * P:(k + 1) * P], sc[:, k, :],
                                       start=(k == 0), stop=(k == KC - 1))
                mm.then_inc(mini_mm, 1)
            pe.wait_ge(con_landed, 32)
            norm(0, SEGS)
            ffn(0, 0, BASE["ffn0"], SEGS)
            if upto >= 1:
                ab_pe()
            if upto >= 2:
                norm(2, SEGS)
                ffn(1, 2, BASE["ffn1"], SEGS)
                norm(3, SEGS)
                ffn(2, 3, BASE["ffn2"], SEGS)
                norm(4, SEGS)
            if upto >= 3:
                cd_pe()
                norm(5, LSEG)
                ffn(3, 5, BASE["ffn3"], LSEG)

        def cat_view(buf, gi):
            if gi < 4:
                return buf[:, 0:4, 0:NLAT].rearrange("p c (r w) -> p c r w", w=GRID_W)[:, :, :, 16 * gi:16 * gi + 16]
            return buf[:, 0:4, NLAT + P * (gi - 4):NLAT + P * (gi - 3)]

        @block.scalar
        def _(act):
            def split_hi(t, slot, n, nk):
                act.wait_ge(raw_landed[slot], n * 16 + 16)
                if not (isinstance(t, int) and t < 2):
                    act.wait_ge(mm_done, t - 1)
                act.activation(wh[slot][:, 0:nk * P], raw[slot][:, 0:nk * P], ACT.Copy).then_inc(hi_done, 1)

            def load_mods(it):
                if not (isinstance(it, int) and it == 0):
                    act.wait_ge(mod_sum, it * 3)
                act.dma_start(mraw[:], dr["wmn"][bass.ds(it * 3 + 24, 3)].rearrange("t p n -> p t n")
                              ).then_inc(mod_landed, 16)

            def sum_mods(it):
                for j in range(3):
                    act.wait_ge(mod_prod, it * 3 + (j + 1))
                    if j == 0 and not (isinstance(it, int) and it == 0):
                        act.wait_ge(mod_set, it)
                    act.activation(mraw[:, j, :], mraw[:, j, :], ACT.Copy, accum_out=mcol[:, j, 1:2]
                                   ).then_inc(mod_sum, 1)

            def load_scb(n):
                act.dma_start(scb[:], dr["ccb"]).then_inc(scb_landed, 16)
                act.wait_ge(scb_landed, 16 * n)
                act.activation(scb[:], scb[:], ACT.Silu).then_inc(scb_ready, 1)

            def up(b, hb, look, mods, ns):
                def pair(i, nk, mods=None, more=False):
                    split_hi(i * 2 + (b + 2), 0, i + (b // 2 + 1), nk)
                    act.wait_ge(mm_done, i * 2 + (b + 1))
                    if not (isinstance(i, int) and i == 0 and b == 0):
                        act.wait_ge(psum_free[1], i + b // 2)
                    act.activation(g1s[:, 0:ns], G[0][:, 0:ns], ACT.Silu).then_inc(psum_free[0], 1)
                    split_hi(i * 2 + (b + 3), 1, i + (b // 2 + 1), nk)
                    act.wait_ge(psum_free[1], i + (b // 2 + 1))
                    act.activation(hh[:, bass.ds(i, 1), 0:ns].rearrange("p a n -> p (a n)"), hf[:, 0:ns],
                                   ACT.Copy).then_inc(h_hi, 1)
                    if mods is not None:
                        sum_mods(i + mods)
                        if more:
                            load_mods(i + (mods + 1))

                last = mods is not None and mods + FH - 1 in (20, 40)
                if b == 0:
                    pair(0, KC, mods, True)
                with act.Fori(int(b == 0), FH - 1 - last) as i:
                    pair(i, KC, mods, True)
                if last:
                    pair(FH - 2, KC, mods, False)
                pair(FH - 1, look)

            def square(j, n, chunk, ns):
                if 8 * n + j >= 2:
                    act.wait_ge(ssq_acc, 8 * n + j - 1)
                act.activation(sq[j % 2][:, 0:ns], chunk, ACT.Square).then_inc(sq_done, 1)

            def down(d, look, same, n_sq, ns):
                for i in range(DOWN // 2):
                    for s in range(2):
                        nk = look if i == DOWN // 2 - 1 else same
                        if nk:
                            split_hi(d + 2 * i + s + 2, s, (d + 2 * i + s + 2) // 2, nk)
                        if n_sq is not None:
                            act.wait_ge(psum_free[s], (d + 2 * i + s) // 2 + 1)
                            square(2 * i + s, n_sq, x[:, 2 * i + s, 0:ns], ns)

            def norm(n, ns):
                act.wait_ge(norm_sum, n + 1)
                act.activation(sq[0][:, 0:ns], NP[:, 0:ns], ACT.Ln, bias=eps[:, 0:1], scale=1.0 / D
                               ).then_inc(norm_ln, 1)
                act.wait_ge(norm_ln, n + 1)
                act.activation(rstd[:, 0:ns], sq[0][:, 0:ns], ACT.Exp, scale=-0.5).then_inc(rstd_ready, 1)
                for j in range(KC):
                    act.wait_ge(aff_done, 8 * n + j + 1)
                    act.activation(xh[:, j, 0:ns], yn[j % 2][:, 0:ns], ACT.Copy).then_inc(xn_hi, 1)

            def ffn(f, base, look, n_sq, mods, ns, ns_sq):
                for h in range(2):
                    b = base + h * (UP + DOWN)
                    up(b, (2 * f + h) * FH, FH, None if mods is None else mods + 10 * h, ns)
                    if h == 0:
                        down(b + UP, KC, FH, None, ns)
                    else:
                        down(b + UP, look, FH, n_sq, ns_sq)

            def ab_in_act():
                def rs(i):
                    act.wait_ge(kq_sum, i + 1)
                    if i:
                        act.wait_ge(kq_rs, i)
                    act.activation(ssq[:], NP[:, 0:T], ACT.Ln, bias=eps[:, 0:1], scale=1.0 / HD).then_inc(kq_ln, 1)
                    act.wait_ge(kq_ln, i + 1)
                    if i:
                        act.wait_ge(kq_done, i)
                    act.activation(rstd[:], ssq[:], ACT.Exp, scale=-0.5).then_inc(kq_rs, 1)

                def silu_conv(i):
                    act.wait_ge(conv_done, i + 1)
                    for a, e, o in ((0, NLAT, 0), (NLAT, T, 3)):
                        ins = act.activation(cv[:, i, a:e], cb[i % 2][:, a + o:e + o], ACT.Silu,
                                             bias=pr("scb")[:, i:i + 1])
                    ins.then_inc(cv_ready, 1)

                for c in range(AB_IN_T):
                    t, s = AB + c, c % 2
                    split_hi(t + 2, s, (t + 2) // 2, KC)
                    if c == 3:
                        act.wait_ge(wdt_landed, 16)
                        act.activation(wdh[:], wdt[:], ACT.Copy).then_inc(wdt_hi, 1)
                        act.activation(ea[:, 0, :], pr("alog"), ACT.Exp).then_inc(dt_exp, 1)
                    if 4 <= c < 12:
                        i = c - 4
                        act.wait_ge(psum_free[s], t // 2 + 1)
                        if i >= 2:
                            act.wait_ge(kq_sum, i - 1)
                        act.activation(sq[i % 2][:], kq[:, i, :], ACT.Square).then_inc(kq_sq, 1)
                        if i:
                            rs(i - 1)
                    if c == 12:
                        rs(7)
                        act.wait_ge(pad_zero, 1)
                    if 12 <= c < 20:
                        i = c - 12
                        act.wait_ge(mm_done, t + 1)
                        if i >= 2:
                            act.wait_ge(conv_done, i - 1)
                        act.activation(pad[i % 2][:, 2:2 + NLAT], G[s][:, 0:NLAT], ACT.Copy)
                        act.activation(pad[i % 2][:, 517:517 + NCTX], G[s][:, NLAT:T], ACT.Copy).then_inc(psum_free[s], 1)
                        if i:
                            silu_conv(i - 1)
                    if c == 14:
                        act.wait_ge(dt_abs, 1)
                        act.activation(dte[:], dtu[:], ACT.Exp, scale=-1.0).then_inc(dt_exp, 1)
                    if c == 20:
                        silu_conv(7)
                    if c >= 20:
                        act.wait_ge(mm_done, t + 1)
                        act.activation(zs[:, c - 20, :], G[s][:, 0:T], ACT.Silu).then_inc(psum_free[s], 1)

            def na_act():
                for g in range(10):
                    act.wait_ge(vt_done, g + 1)
                    act.activation(vtile(g), (B6, B7)[g % 2], ACT.Copy).then_inc(vs_ready, 1)

                def expo(u):
                    act.wait_ge(nmax_ready, u + 1)
                    if u >= 2:
                        act.wait_ge(tr_done, u - 1)
                    st = nst[:, u % 4, :]
                    if u < 32:
                        act.activation(nsP[u % 2][:], nsS[u % 2][:], ACT.Exp, bias=st[:, 0:1], accum_out=st[:, 2:3]
                                       ).then_inc(p_ready, 1)
                    else:
                        for w_ in range(2):
                            r = slice(256 * w_, 256 * w_ + 256)
                            ins = act.activation(nsP[u % 2][:, r], G[0][:, 512 * (u % 2) + 256 * w_:512 * (u % 2) + 256 * w_ + 256],
                                                 ACT.Exp, bias=st[:, w_:w_ + 1], accum_out=st[:, 2 + w_:3 + w_])
                        ins.then_inc(p_ready, 1)

                def copy_pt(u):
                    act.wait_ge(tr_done, u + 1)
                    if u >= 2:
                        act.wait_ge(pv_done, u - 1)
                    act.activation(nsT[u % 2][:], G[1][:, 512 * (u % 2):512 * (u % 2) + 512], ACT.Copy).then_inc(pt_ready, 1)

                def out_hi(gi):
                    act.wait_ge(ot_done, gi + 1)
                    src = (B6, B7)[gi % 2].rearrange("p (c t) -> p c t", c=4)
                    act.activation(cat_view(xh, gi), src if gi >= 4 else src.rearrange("p c (r w) -> p c r w", w=16),
                                   ACT.Copy).then_inc(cat_hi, 1)

                for it in range(NU + 4):
                    if it < NU:
                        expo(it)
                    if 0 <= it - 2 < NU:
                        copy_pt(it - 2)
                    if it >= 12 and (it - 12) % 8 == 0 and (it - 12) // 8 < 4:
                        out_hi((it - 12) // 8)
                out_hi(4)
                out_hi(5)

            def ssd_act():
                for q in range(9):
                    act.wait_ge(tk_done, q + 1)
                    dst = xst[:, q, :] if q < 6 else bst[:, 2 * (q - 6):2 * (q - 6) + 2, :].rearrange("p t c -> p (t c)")
                    act.activation(dst, (B6, B7)[q % 2], ACT.Copy).then_inc(tk_ready, 1)
                act.wait_ge(tm_set, 1)
                act.activation(dend[:], tm[:], ACT.Exp).then_inc(dend_set, 1)
                act.activation(cdec[:].rearrange("p t c -> p (t c)"), NP[:, 512:608], ACT.Exp).then_inc(dend_set, 1)
                for u in range(12):
                    st = u % 2
                    act.wait_ge(d_ready, 8 * (u + 1))
                    for d in range(2):
                        act.activation(sL[st][d][:], sL[st][d][:], ACT.Exp).then_inc(l_ready, 1)
                    if u >= 2:
                        act.wait_ge(y_mm, u - 1)
                    for d in range(2):
                        ins = act.activation(sE[st][d][:], G[st][:, 512 * d:512 * d + 512], ACT.Exp)
                    ins.then_inc(e_ready, 1)
                for c in range(4):
                    if c == 0:
                        act.wait_ge(gz_done, 6)
                    if c >= 2:
                        act.wait_ge(gn_sum, c - 1)
                    act.activation(sqg[c % 2][:], gy[:, c, :], ACT.Square).then_inc(gsq_done, 1)
                act.wait_ge(gn_sum, 4)
                act.activation(lng[:], NP[:, 0:T], ACT.Ln, bias=eps[:, 0:1], scale=1.0 / 512).then_inc(gn_ln, 1)
                act.wait_ge(gn_ln, 1)
                act.activation(rsg[:], lng[:], ACT.Exp, scale=-0.5).then_inc(gn_rs, 1)
                for c in range(4):
                    act.wait_ge(vg_ready, c + 1)
                    act.activation(xh[:, 4 + c, :], vg[c % 2][:], ACT.Copy).then_inc(gcat_hi, 1)

            def cd_in_act():
                def rs(i):
                    ns = T if i < 4 else NLAT
                    act.wait_ge(kq_sum, 8 + i + 1)
                    act.wait_ge(kq_rs, 8 + i)
                    act.activation(ssq[:, 0:ns], NP[:, 0:ns], ACT.Ln, bias=eps[:, 0:1], scale=1.0 / HD).then_inc(kq_ln, 1)
                    act.wait_ge(kq_ln, 8 + i + 1)
                    act.wait_ge(kq_done, 8 + i)
                    act.activation(rstd[:, 0:ns], ssq[:, 0:ns], ACT.Exp, scale=-0.5).then_inc(kq_rs, 1)

                def add_bias(i):
                    act.wait_ge(conv_done, 8 + i + 1)
                    for a, e, o in ((0, NLAT, 0), (NLAT, T, 3)):
                        ins = act.activation(xc[:, i, a:e], cb[i % 2][:, a + o:e + o], ACT.Identity,
                                             bias=pr("lcb")[:, i:i + 1])
                    ins.then_inc(cv_ready, 1)

                for c in range(CD_IN_T):
                    t, s = CD + c, c % 2
                    split_hi(t + 2, s, (t + 2) // 2, KC)
                    if c == 2:
                        act.wait_ge(coef_abs, 1)
                        act.activation(coef[:, 1, :], coef[:, 0, :], ACT.Exp, scale=-1.0).then_inc(coef_exp, 1)
                        act.wait_ge(dl_set, 2)
                        act.activation(dl[:, 2:4], dl[:, 0:2], ACT.Exp).then_inc(dl_exp, 1)
                    if 4 <= c < 7:
                        for tt in (2 * c - 8, 2 * c - 7):
                            act.wait_ge(v2_done, tt + 1)
                            act.activation(vtok[:, tt, :], (B6, B7)[tt % 2], ACT.Copy).then_inc(v2_ready, 1)
                    if 4 <= c < 12:
                        i = c - 4
                        act.wait_ge(psum_free[s], t // 2 + 1)
                        if i >= 2:
                            act.wait_ge(kq_sum, 8 + i - 1)
                        if i < 4:
                            act.activation(sq[i % 2][:], k2[:, i, :], ACT.Square).then_inc(kq_sq, 1)
                        else:
                            act.activation(sq[i % 2][:, 0:NLAT], q2[:, i - 4, :], ACT.Square).then_inc(kq_sq, 1)
                        if i:
                            rs(i - 1)
                    if c == 12:
                        rs(7)
                        act.wait_ge(pad_zero, 2)
                    if 12 <= c < 16:
                        i = c - 12
                        act.wait_ge(mm_done, t + 1)
                        if i >= 2:
                            act.wait_ge(conv_done, 8 + i - 1)
                        act.activation(pad[i % 2][:, 2:2 + NLAT], G[s][:, 0:NLAT], ACT.Copy)
                        act.activation(pad[i % 2][:, 517:517 + NCTX], G[s][:, NLAT:T], ACT.Copy).then_inc(psum_free[s], 1)
                        if i:
                            add_bias(i - 1)
                    if c == 16:
                        add_bias(3)
                    if c >= 16:
                        act.wait_ge(mm_done, t + 1)
                        act.activation(gate[:, c - 16, :], G[s][:, 0:NLAT], ACT.Gelu_apprx_tanh).then_inc(psum_free[s], 1)

            def cd_mid_act():
                act.wait_ge(coef_set, 1)

                def gates(p_):
                    for d in range(2):
                        for g, (dst, bias) in enumerate(((lR, "lba"), (lI, "lbx"))):
                            act.wait_ge(gate_mm, 4 * p_ + 2 * d + g + 1)
                            if p_:
                                act.wait_ge(cd_cat, p_)
                            act.activation(dst[d][:], G[g][:, 0:T], ACT.Sigmoid, bias=pr(bias)[:, 4 * d + p_:4 * d + p_ + 1]
                                           ).then_inc(gate_sig, 1)

                def decay(p_):
                    for d in range(2):
                        e = 4 * d + p_
                        act.wait_ge(gate_sig, 4 * p_ + 2 * d + 1)
                        act.activation(lA[d][:], lR[d][:], ACT.Exp, scale=coef[:, 6, e:e + 1]).then_inc(lru_a, 1)
                        act.wait_ge(lru_a, 2 * p_ + d + 1)
                        act.activation(lR[d][:], lR[d][:], ACT.Tanh, scale=coef[:, 7, e:e + 1]).then_inc(lru_t, 1)

                def root(p_):
                    for d in range(2):
                        act.wait_ge(lru_m, 2 * p_ + d + 1)
                        act.activation(lR[d][:], lR[d][:], ACT.Sqrt).then_inc(lru_q, 1)

                def out(p_):
                    act.wait_ge(lru_o, p_ + 1)
                    act.activation(xh[:, p_, 0:NLAT], lX[1][:, 0:NLAT], ACT.Copy).then_inc(lru_hi, 1)

                def att(a):
                    if a < NA2:
                        for s in range(2):
                            act.wait_ge(max2_ready, 2 * a + s + 1)
                            if a:
                                act.wait_ge(w_done, a)
                            act.activation(pb[s][:], G[s][:, 0:T], ACT.Exp, bias=st2[:, a % 2, s:s + 1],
                                           accum_out=st2[:, a % 2, 2 + s:3 + s]).then_inc(p2_ready, 1)
                    if 1 <= a <= NA2:
                        act.wait_ge(tr2_done, a)
                        if a >= 2:
                            act.wait_ge(pv2_done, a - 1)
                        act.activation(wtb[:], NP[:, 0:T], ACT.Copy).then_inc(wt_ready, 1)
                    if 1 <= a <= NA2:
                        b = a - 1
                        act.wait_ge(pv2_done, b + 1)
                        st = st2[:, b % 2, :]
                        act.activation(junk[:], B6[:, 0:P], ACT.Square, accum_out=st[:, 6:7]).then_inc(ss_ready, 1)
                        act.wait_ge(ss_ready, b + 1)
                        act.activation(st[:, 7:8], st[:, 6:7], ACT.Ln, bias=eps[:, 0:1], scale=1.0 / P).then_inc(ss_ln, 1)
                        act.wait_ge(ss_ln, b + 1)
                        act.activation(st[:, 6:7], st[:, 7:8], ACT.Exp, scale=-0.5).then_inc(rr_ready, 1)

                for what, i in SCHED:
                    if what == "gates":
                        gates(i)
                    if what == "act":
                        decay(i)
                    if what == "root":
                        root(i)
                    if what == "out":
                        out(i)
                    if what == "att":
                        att(i)
                for qt in range(4):
                    act.wait_ge(ov_ready, qt + 1)
                    act.activation(xh[:, 4:8, P * qt:P * qt + P], ovb[qt % 2][:].rearrange("p (h t) -> p h t", h=4), ACT.Copy
                                   ).then_inc(oq_hi, 1)

            act.wait_ge(scb0_landed, 16)
            act.activation(scb0[:], scb0[:], ACT.Silu).then_inc(scb0_ready, 1)
            act.wait_ge(con_landed, 32)
            act.activation(sc[:].rearrange("p k s -> p (k s)"), pr("cc"), ACT.Silu).then_inc(sc_ready, 1)
            act.wait_ge(x_landed, 16)
            for j in range(KC):
                square(j, 0, x[:, j, :], T)
            split_hi(0, 0, 0, KC)
            split_hi(1, 1, 0, KC)
            act.wait_ge(eps_set, 1)
            norm(0, T)
            load_mods(0)
            load_scb(1)
            ffn(0, BASE["ffn0"], KC if upto >= 1 else 0, 1 if upto >= 1 else None, 0, T, T)
            if upto >= 1:
                norm(1, T)
                ab_in_act()
                na_act()
                ssd_act()
                down(ABO, KC if upto >= 2 else 0, KC, 2 if upto >= 2 else None, T)
            if upto >= 2:
                norm(2, T)
                load_mods(20)
                load_scb(2)
                ffn(1, BASE["ffn1"], KC, 3, 20, T, T)
                norm(3, T)
                ffn(2, BASE["ffn2"], KC if upto >= 3 else 0, 4 if upto >= 3 else None, None, T, T)
            if upto >= 3:
                norm(4, T)
                cd_in_act()
                cd_mid_act()
                down(CDO, KC, KC, 5, NLAT)
                norm(5, NLAT)
                ffn(3, BASE["ffn3"], 0, None, None, NLAT, NLAT)

        @block.vector
        def _(dve):
            def split_lo(t, slot, nk):
                dve.wait_ge(hi_done, t + 1)
                dve.tensor_tensor(wl[slot][:, 0:nk * P], raw[slot][:, 0:nk * P],
                                  wh[slot][:, 0:nk * P].bitcast(F32), ALU.subtract).then_inc(lo_done, 1)

            def dot(tile, s, scv, out):
                return dve.scalar_tensor_tensor(B67[:], tile, 1.0, scv[:, s, :], ALU.mult, ALU.mult, accum_out=out)

            def dot_mods(it, mods_first):
                dve.wait_ge(mod_landed, it * 16 + 16)
                dve.wait_ge(scb_ready, 1 if mods_first else 2)
                if not (isinstance(it, int) and it == 0):
                    dve.wait_ge(mod_set, it)
                for j in range(3):
                    if j or not (isinstance(it, int) and it == 0):
                        dve.wait_ge(mod_dot, it * 3 + j)
                    dot(mraw[:, j, :], 0, scb, mcol[:, j, 0:1]).then_inc(mod_dot, 1)

            def set_mods(it):
                dve.wait_ge(mod_sum, it * 3 + 3)
                c0 = it * 3 + 24
                dve.tensor_tensor(M[:, bass.ds(c0, 3), :], mcol[:],
                                  pr("bmod")[:, bass.ds(c0, 3)].unsqueeze(2).to_broadcast([P, 3, 2]),
                                  ALU.add).then_inc(mod_set, 1)

            def up(b, hb, look, mods, ns):
                def pair(i, nk):
                    split_lo(i * 2 + (b + 2), 0, nk)
                    if mods is not None and nk == KC:
                        dot_mods(i + mods, mods < 20)
                    dve.wait_ge(mm_done, i * 2 + (b + 2))
                    dve.wait_ge(psum_free[0], i + (b // 2 + 1))
                    if not (isinstance(i, int) and i == 0 and hb == 0):
                        dve.wait_ge(h_ready, i + hb)
                    dve.tensor_tensor(hf[:, 0:ns], g1s[:, 0:ns], G[1][:, 0:ns], ALU.mult).then_inc(psum_free[1], 1)
                    split_lo(i * 2 + (b + 3), 1, nk)
                    dve.wait_ge(h_hi, i + (hb + 1))
                    hs = [t_[:, bass.ds(i, 1), 0:ns].rearrange("p a n -> p (a n)") for t_ in (hl, hh)]
                    dve.tensor_tensor(hs[0], hf[:, 0:ns], hs[1].bitcast(F32), ALU.subtract).then_inc(h_ready, 1)
                    if mods is not None and nk == KC:
                        set_mods(i + mods)

                if b == 0:
                    pair(0, KC)
                with dve.Fori(int(b == 0), FH - 1) as i:
                    pair(i, KC)
                pair(FH - 1, look)

            def down(d, look, same, n, segs):
                for i in range(DOWN // 2):
                    for s in range(2):
                        t = d + 2 * i + s
                        dve.wait_ge(mm_done, t + 1)
                        for a, b, c in segs:
                            j = 2 * i + s
                            ins = dve.scalar_tensor_tensor(x[:, j, a:b], G[s][:, a:b], modG[:, n, j, c:c + 1],
                                                           x[:, j, a:b], ALU.mult, ALU.add)
                        ins.then_inc(psum_free[s], 1)
                        nk = look if i == DOWN // 2 - 1 else same
                        if nk:
                            split_lo(t + 2, s, nk)

            def prep(n, it):
                dve.wait_ge(mod_set, it)
                c0 = (n // 3) * NMT + 3 * KC * (n % 3)
                g = pr("normg")[:, 8 * n:8 * n + 8].unsqueeze(2).to_broadcast([P, KC, 2])
                dve.scalar_tensor_tensor(modA[:, n], M[:, c0 + KC:c0 + 2 * KC, :], 1.0, g, ALU.add, ALU.mult
                                         ).then_inc(prep_done, 1)
                dve.tensor_scalar(modG[:, n], M[:, c0 + 2 * KC:c0 + 3 * KC, :], 1.0 if n % 3 == 1 else 0.5, None,
                                  ALU.mult).then_inc(prep_done, 1)
                dve.wait_ge(prep_done, 2 * (n + 1))

            def norm(n, segs):
                ns = segs[-1][1]
                c0 = (n // 3) * NMT + 3 * KC * (n % 3)

                def rest(j):
                    dve.wait_ge(xn_hi, 8 * n + j + 1)
                    dve.tensor_tensor(xl[:, j, 0:ns], yn[j % 2][:, 0:ns], xh[:, j, 0:ns].bitcast(F32),
                                      ALU.subtract).then_inc(xn_ready, 1)

                for j in range(KC):
                    dve.wait_ge(v_ready, 8 * n + j + 1)
                    if j >= 2:
                        dve.wait_ge(xn_ready, 8 * n + j - 1)
                    for a, b, c in segs:
                        ins = dve.tensor_scalar(yn[j % 2][:, a:b], vn[j % 2][:, a:b], modA[:, n, j, c:c + 1],
                                                M[:, c0 + j, c:c + 1], ALU.mult, ALU.add)
                    ins.then_inc(aff_done, 1)
                    if j >= 1:
                        rest(j - 1)
                rest(KC - 1)

            def ffn(f, n, base, look, mods, segs):
                for h in range(2):
                    b = base + h * (UP + DOWN)
                    up(b, (2 * f + h) * FH, FH, None if mods is None else mods + 10 * h, segs[-1][1])
                    down(b + UP, KC if h == 0 else look, FH, n, segs)

            chained = [0]

            def chain(ins):
                chained[0] += 1
                ins.then_inc(dve_chain, 1)
                dve.wait_ge(dve_chain, chained[0])

            def log1p_exp(e, den, s_, s2, p_):
                chain(dve.tensor_scalar(den, e, 2.0, None, ALU.add))
                chain(dve.reciprocal(den, den))
                chain(dve.tensor_tensor(s_, e, den, ALU.mult))
                chain(dve.tensor_tensor(s2, s_, s_, ALU.mult))
                chain(dve.tensor_scalar(p_, s2, 1.0 / 19, None, ALU.mult))
                for q in (17, 15, 13, 11, 9, 7, 5, 3):
                    chain(dve.scalar_tensor_tensor(p_, p_, 1.0 / q, s2, ALU.add, ALU.mult))
                chain(dve.scalar_tensor_tensor(p_, p_, 1.0, s_, ALU.add, ALU.mult))

            def ab_in_dve():
                dve.wait_ge(con_landed, 32)
                dve.tensor_scalar(qg8[:, 1:2], pr("naqg"), HD ** -0.5, None, ALU.mult).then_inc(qg_set, 1)
                dve.tensor_copy(qg8[:, 0:1], pr("nakg")).then_inc(qg_set, 1)

                def kq_norm(i):
                    dve.wait_ge(kq_rs, i + 1)
                    dve.scalar_tensor_tensor(kq[:, i, :], kq[:, i, :], qg8[:, i // 4:i // 4 + 1], rstd[:],
                                             ALU.mult, ALU.mult).then_inc(kq_done, 1)

                def conv(i):
                    t = AB + 12 + i
                    dve.wait_ge(psum_free[i % 2], t // 2 + 1)
                    if i >= 2:
                        dve.wait_ge(cv_ready, i - 1)
                    src, dst = pad[i % 2], cb[i % 2]
                    for k in range(4):
                        tap = pr("scw")[:, 4 * i + k:4 * i + k + 1]
                        if k == 0:
                            ins = dve.tensor_scalar(dst[:], src[:, 0:771], tap, None, ALU.mult)
                        else:
                            ins = dve.scalar_tensor_tensor(dst[:], src[:, k:k + 771], tap, dst[:], ALU.mult, ALU.add)
                        if k < 3:
                            ins.then_inc(conv_tap, 1)
                            dve.wait_ge(conv_tap, 3 * i + k + 1)
                    ins.then_inc(conv_done, 1)

                for c in range(AB_IN_T):
                    t, s = AB + c, c % 2
                    if c < 12:
                        dve.wait_ge(mm_done, t + 1)
                        dst = vT[:, c, :] if c < 4 else kq[:, c - 4, :]
                        if c < 8:
                            dve.tensor_copy(dst, G[s][:, 0:T]).then_inc(psum_free[s], 1)
                        else:
                            dve.tensor_copy(dst[:, 0:NLAT].rearrange("p (n r c) -> p n r c", n=4, c=16),
                                            G[s][:, 0:NLAT].rearrange("p (r n c) -> p n r c", n=4, c=16))
                            dve.tensor_copy(dst[:, NLAT:T], G[s][:, NLAT:T]).then_inc(psum_free[s], 1)
                    split_lo(t + 2, s, KC)
                    if c == 3:
                        dve.wait_ge(wdt_hi, 1)
                        dve.tensor_tensor(wdl[:], wdt[:], wdh[:].bitcast(F32), ALU.subtract).then_inc(wdt_lo, 1)
                    if c == 4:
                        dve.wait_ge(qg_set, 2)
                        for s_ in range(2):
                            ins = dve.memset(pad[s_][:], 0.0)
                        ins.then_inc(pad_zero, 1)
                    if 5 <= c < 13:
                        kq_norm(c - 5)
                    if c == 12:
                        dve.wait_ge(dt_mm, 1)
                        bias = pr("dtb").unsqueeze(1).to_broadcast([P, NT, 16])
                        chain(dve.tensor_tensor(dt2[:], B6[:, 0:96].rearrange("p (t c) -> p t c", c=16), bias, ALU.add))
                        chain(dve.tensor_scalar(dtp[:], dt2[:], -1.0, None, ALU.mult))
                        dve.tensor_tensor(dtu[:], dt2[:], dtp[:], ALU.max).then_inc(dt_abs, 1)
                        chain(dve.tensor_scalar(dt[:], dt2[:], 0.0, None, ALU.max))
                    if 12 <= c < 20:
                        conv(c - 12)
                    if c == 20:
                        dve.wait_ge(dt_exp, 2)
                        log1p_exp(dte[:], dtu[:], dts[:], dt2[:], dtp[:])
                        chain(dve.scalar_tensor_tensor(dt[:], dtp[:], 2.0, dt[:], ALU.mult, ALU.add))
                        ab_ = ea[:, 0, :].unsqueeze(1).to_broadcast([P, NT, 16])
                        dve.scalar_tensor_tensor(dA[:], dt[:], -1.0, ab_, ALU.mult, ALU.mult).then_inc(dt_set, 1)

            def na_dve():
                dve.wait_ge(cv_ready, 8)
                for s in range(2):
                    dve.memset(bm[s][:, 256:512], 0.0).then_inc(bm_zero, 1)
                dve.wait_ge(bm_zero, 2)
                for g in range(8):
                    if g >= 2:
                        dve.wait_ge(vt_done, g - 1)
                    dve.tensor_copy(vst[g % 2][:].rearrange("p (c r w) -> p c r w", c=4, w=32),
                                    vT[:, :, 256 * (g % 2):256 * (g % 2) + 256].rearrange("p c (r w) -> p c r w", w=GRID_W)[
                                        :, :, :, STRIP0[g // 2]:STRIP0[g // 2] + 32]).then_inc(vst_ready, 1)

                def biased_max(u):
                    dve.wait_ge(s_done, u + 1)
                    st, bank = nst[:, u % 4, :], G[0][:, 512 * (u % 2):512 * (u % 2) + 512]
                    if u == 0:
                        dve.wait_ge(vs_ready, 10)
                    if u < 32:
                        dve.wait_ge(bm_ready, u + 1)
                        if u >= 2:
                            dve.wait_ge(p_ready, u - 1)
                        dve.tensor_tensor(nsS[u % 2][:], bank, bm[u % 2][:], ALU.add).then_inc(na_biased, 1)
                        dve.wait_ge(na_biased, u + 1)
                        dve.tensor_reduce(st[:, 0:1], nsS[u % 2][:], AX.X, ALU.max, negate=True).then_inc(nmax_ready, 1)
                    else:
                        dve.tensor_reduce(st[:, 0:2], bank.rearrange("p (w k) -> p w k", w=2), AX.X, ALU.max, negate=True
                                          ).then_inc(nmax_ready, 1)

                def scale_out(u):
                    h, st = u % 8, nst[:, u % 4, :]
                    nw = 1 if u < 32 else 2
                    dve.wait_ge(p_ready, u + 1)
                    dve.reciprocal(st[:, 4:4 + nw], st[:, 2:2 + nw]).then_inc(rinv_ready, 1)
                    dve.wait_ge(rinv_ready, u + 1)
                    dve.wait_ge(pv_done, u + 1)
                    if h == 0 and u // 8 >= 2:
                        dve.wait_ge(ot_done, min(u // 8 - 1, 4) if u < 32 else 4)
                    for w_ in range(nw):
                        o = NP[:, 512 * (u % 2) + 64 * w_:512 * (u % 2) + 64 * w_ + 64]
                        ins = dve.tensor_scalar(onorm[(u // 8 + w_) % 2][:, 64 * h:64 * h + 64], o, st[:, 4 + w_:5 + w_], None,
                                                ALU.mult)
                    ins.then_inc(o_read, 1)

                def out_lo(gi):
                    dve.wait_ge(cat_hi, gi + 1)
                    src = (B6, B7)[gi % 2].rearrange("p (c t) -> p c t", c=4)
                    if gi < 4:
                        for c in range(4):
                            ins = dve.tensor_tensor(cat_view(xl, gi)[:, c], src[:, c].rearrange("p (r w) -> p r w", w=16),
                                                    cat_view(xh, gi)[:, c].bitcast(F32), ALU.subtract)
                    else:
                        ins = dve.tensor_tensor(cat_view(xl, gi), src, cat_view(xh, gi).bitcast(F32), ALU.subtract)
                    ins.then_inc(na_cat, 1)

                for it in range(NU + 4):
                    if it < NU:
                        biased_max(it)
                    if 0 <= it - 3 < NU:
                        scale_out(it - 3)
                    if it >= 12 and (it - 12) % 8 == 0 and (it - 12) // 8 < 4:
                        out_lo((it - 12) // 8)
                out_lo(4)
                out_lo(5)

            def ssd_dve():
                dve.wait_ge(acs_mm, 1)
                dve.tensor_copy(acs[:].rearrange("p t c -> p (t c)"), NP[:, 0:96]).then_inc(acs_set, 1)
                dve.wait_ge(acs_set, 1)
                dve.tensor_tensor(tm[:].rearrange("p t c -> p (t c)"), NP[:, 512:608], acs[:].rearrange("p t c -> p (t c)"),
                                  ALU.subtract).then_inc(tm_set, 1)
                dve.wait_ge(dend_set, 2)
                dve.tensor_tensor(dend[:], dend[:], dt[:], ALU.mult).then_inc(dw_set, 1)
                for s in range(5):
                    for d in range(2):
                        e = 2 * s + d
                        tt = (FWD_SEQ, BWD_SEQ)[d][s]
                        if s:
                            if e > 2:
                                dve.wait_ge(h_set, e)
                            dve.wait_ge(h_set, e - 1)
                            dve.tensor_tensor(hm[:].rearrange("p (h q) -> p h q", q=64),
                                              hst[d][s - 1].rearrange("p (h q) -> p h q", q=64),
                                              heads(cdec[:, tt, 8 * d:8 * d + 8], 8, 64), ALU.mult).then_inc(hm_set, 1)
                            dve.wait_ge(hm_set, e - 1)
                        dve.wait_ge(st_mm, e + 1)
                        bank = G[1][:, 512 * d:512 * d + 512]
                        if s:
                            dve.tensor_tensor(hst[d][s], hm[:], bank, ALU.add).then_inc(h_set, 1)
                        else:
                            dve.tensor_copy(hst[d][s], bank).then_inc(h_set, 1)

                def decays(u):
                    tt, g, st = u // 2, u % 2, u % 2
                    dve.wait_ge(r_mm, u + 1)
                    if u >= 2:
                        dve.wait_ge(y_mm, u - 1)
                    for d in range(2):
                        dve.tensor_tensor(cbm[st][d][:], (B6, B7)[st][:, 0:P], cst(("trif", "trib")[d]), ALU.mult
                                          ).then_inc(cb_set, 1)
                    for d in range(2):
                        for hh_ in range(4):
                            col = 8 * d + 4 * g + hh_
                            r = slice(P * hh_, P * hh_ + P)
                            dve.tensor_scalar(sL[st][d][:, r], G[st][:, 512 * d + P * hh_:512 * d + P * hh_ + P],
                                              acs[:, tt, col:col + 1], 0.0, ALU.subtract, ALU.min).then_inc(d_ready, 1)

                def weights(u):
                    tt, g, st = u // 2, u % 2, u % 2
                    v3 = lambda ap: ap.rearrange("p (h i) -> p h i", h=4)
                    dve.wait_ge(cb_set, 2 * (u + 1))
                    for d in range(2):
                        dve.wait_ge(l_ready, 2 * u + d + 1)
                        dve.tensor_tensor(v3(sL[st][d][:]), v3(sL[st][d][:]),
                                          cbm[st][d][:].unsqueeze(1).to_broadcast([P, 4, P]), ALU.mult).then_inc(m_ready, 1)
                    dve.wait_ge(e_ready, u + 1)
                    for d in range(2):
                        dve.tensor_tensor(v3(sE[st][d][:]), v3(sE[st][d][:]),
                                          cv[:, 6 + g, P * tt:P * tt + P].unsqueeze(1).to_broadcast([P, 4, P]), ALU.mult
                                          ).then_inc(m_ready, 1)

                def read_y(tt):
                    dve.wait_ge(y_mm, 2 * tt + 2)
                    for c in range(4):
                        ins = dve.scalar_tensor_tensor(gy[:, c, P * tt:P * tt + P], cv[:, c, P * tt:P * tt + P],
                                                       pr("ssdd")[:, c:c + 1],
                                                       NP[:, 512 * (tt % 2) + P * c:512 * (tt % 2) + P * c + P],
                                                       ALU.mult, ALU.add)
                    ins.then_inc(y_read, 1)

                decays(0)
                for u in range(12):
                    weights(u)
                    if u + 1 < 12:
                        decays(u + 1)
                    if u % 2 == 1:
                        read_y(u // 2)
                for c in range(5):
                    if c < 4:
                        dve.wait_ge(gn_rs, 1)
                        if c >= 2:
                            dve.wait_ge(ssd_cat, c - 1)
                        dve.scalar_tensor_tensor(vg[c % 2][:], gy[:, c, :], pr("ssdg")[:, c:c + 1], rsg[:], ALU.mult, ALU.mult
                                                 ).then_inc(vg_ready, 1)
                    if c >= 1:
                        dve.wait_ge(gcat_hi, c)
                        dve.tensor_tensor(xl[:, 3 + c, :], vg[(c - 1) % 2][:], xh[:, 3 + c, :].bitcast(F32), ALU.subtract
                                          ).then_inc(ssd_cat, 1)

            def cd_in_dve():
                chain(dve.tensor_scalar(coef[:, 5, :], pr("lam"), -1.0, None, ALU.mult))
                dve.tensor_tensor(coef[:, 0, :], coef[:, 5, :], pr("lam"), ALU.max).then_inc(coef_abs, 1)
                for q in range(2):
                    dve.scalar_tensor_tensor(t1b[q][:, 0:64], pr("dlam")[:, 128 * q:128 * q + 64], 1.0,
                                             pr("dlam")[:, 128 * q + 64:128 * q + 128], ALU.mult, ALU.mult,
                                             accum_out=dl[:, q:q + 1]).then_inc(dl_set, 1)
                chain(dve.tensor_scalar(qg2[:, 1:2], pr("dqg"), HD ** -0.5, None, ALU.mult))
                chain(dve.tensor_copy(qg2[:, 0:1], pr("dkg")))
                dve.tensor_scalar(dg[:, 0:1], pr("subg"), 1.0 - LAM_INIT, None, ALU.mult).then_inc(dg_set, 1)

                def kq_norm(i):
                    dve.wait_ge(kq_rs, 8 + i + 1)
                    ap = k2[:, i, :] if i < 4 else q2[:, i - 4, :]
                    dve.scalar_tensor_tensor(ap, ap, qg2[:, i // 4:i // 4 + 1], rstd[:, 0:T if i < 4 else NLAT],
                                             ALU.mult, ALU.mult).then_inc(kq_done, 1)

                def rotate(i):
                    dve.wait_ge(rope_mm, i + 1)
                    dve.wait_ge(rope_landed, 16)
                    if i:
                        dve.wait_ge(rope_done, i)
                    dve.tensor_tensor(t2b[:], (B6, B7)[i % 2], rope[:, 1, :], ALU.mult).then_inc(t2_set, 1)
                    dve.wait_ge(t2_set, i + 1)
                    dve.wait_ge(t1_ready, i + 1)
                    ap = k2[:, i, 0:NLAT] if i < 4 else q2[:, i - 4, :]
                    dve.tensor_tensor(ap, t1b[i % 2][:], t2b[:], ALU.add).then_inc(rope_done, 1)

                def conv(i):
                    t = CD + 12 + i
                    dve.wait_ge(psum_free[i % 2], t // 2 + 1)
                    if i >= 2:
                        dve.wait_ge(cv_ready, 8 + i - 1)
                    src, dst = pad[i % 2], cb[i % 2]
                    for k in range(4):
                        tap = pr("lcw")[:, 4 * i + k:4 * i + k + 1]
                        if k == 0:
                            ins = dve.tensor_scalar(dst[:], src[:, 0:771], tap, None, ALU.mult)
                        else:
                            ins = dve.scalar_tensor_tensor(dst[:], src[:, k:k + 771], tap, dst[:], ALU.mult, ALU.add)
                        if k < 3:
                            ins.then_inc(conv_tap, 1)
                            dve.wait_ge(conv_tap, 24 + 3 * i + k + 1)
                    ins.then_inc(conv_done, 1)

                for c in range(CD_IN_T):
                    t, s = CD + c, c % 2
                    if c < 12:
                        dve.wait_ge(mm_done, t + 1)
                        if c < 8:
                            dve.tensor_copy(vT2[:, c, :] if c < 4 else k2[:, c - 4, :], G[s][:, 0:T]).then_inc(psum_free[s], 1)
                        else:
                            dve.tensor_copy(q2[:, c - 8, :], G[s][:, 0:NLAT]).then_inc(psum_free[s], 1)
                    split_lo(t + 2, s, KC)
                    if c == 3:
                        dve.wait_ge(coef_exp, 1)
                        log1p_exp(coef[:, 1, :], coef[:, 2, :], coef[:, 3, :], coef[:, 4, :], coef[:, 6, :])
                        chain(dve.tensor_scalar(coef[:, 5, :], coef[:, 5, :], 0.0, None, ALU.max))
                        chain(dve.scalar_tensor_tensor(coef[:, 7, :], coef[:, 6, :], 2.0, coef[:, 5, :], ALU.mult, ALU.add))
                        chain(dve.tensor_scalar(coef[:, 6, :], coef[:, 7, :], -8.0, None, ALU.mult))
                        dve.tensor_scalar(coef[:, 7, :], coef[:, 7, :], 8.0, None, ALU.mult).then_inc(coef_set, 1)
                        dve.wait_ge(dl_exp, 1)
                        chain(dve.tensor_tensor(dl[:, 4:5], dl[:, 3:4], dl[:, 2:3], ALU.subtract))
                        dve.tensor_scalar(dl[:, 5:6], dl[:, 4:5], -LAM_INIT, None, ALU.add).then_inc(dlam_set, 1)
                    if c == 4:
                        for s_ in range(2):
                            ins = dve.memset(pad[s_][:], 0.0)
                        ins.then_inc(pad_zero, 1)
                    if 5 <= c < 13:
                        kq_norm(c - 5)
                    if 8 <= c < 16:
                        rotate(c - 8)
                    if 12 <= c < 16:
                        conv(c - 12)

            def cd_mid_dve():
                def decay(p_):
                    for d in range(2):
                        e = 2 * p_ + d
                        dve.wait_ge(lru_t, e + 1)
                        dve.tensor_tensor(lX[d][:], lA[d][:], lA[d][:], ALU.mult).then_inc(lru_a2, 1)
                        dve.wait_ge(lru_a2, e + 1)
                        dve.scalar_tensor_tensor(lR[d][:], lX[d][:], 1.0, lR[d][:], ALU.add, ALU.mult).then_inc(lru_m, 1)

                def scan(p_):
                    for d in range(2):
                        e = 2 * p_ + d
                        dve.wait_ge(lru_q, e + 1)
                        dve.wait_ge(lru_ix, e + 1)
                        dve.tensor_tensor(lI[d][:], lI[d][:], lR[d][:], ALU.mult).then_inc(lru_b, 1)
                        dve.wait_ge(lru_b, e + 1)
                        A_, B_, X_ = lA[d], lI[d], lX[d]
                        if d == 0:
                            dve.tensor_tensor_scan(X_[:, NLAT:T], A_[:, NLAT:T], B_[:, NLAT:T], 0.0, ALU.mult, ALU.add
                                                   ).then_inc(scan_c, 1)
                            dve.wait_ge(scan_c, e + 1)
                            dve.tensor_tensor_scan(hsum[:, p_, :], A_[:, 0:NLAT], B_[:, 0:NLAT], X_[:, T - 1:T],
                                                   ALU.mult, ALU.add).then_inc(scan_l, 1)
                        else:
                            dve.tensor_tensor_scan(X_[:, T - 1:NLAT - 1:-1], A_[:, T - 1:NLAT - 1:-1],
                                                   B_[:, T - 1:NLAT - 1:-1], 0.0, ALU.mult, ALU.add).then_inc(scan_c, 1)
                            dve.wait_ge(scan_c, e + 1)
                            dve.tensor_tensor_scan(X_[:, NLAT - 1::-1], A_[:, NLAT - 1::-1], B_[:, NLAT - 1::-1],
                                                   X_[:, NLAT:NLAT + 1], ALU.mult, ALU.add).then_inc(scan_l, 1)
                    dve.wait_ge(scan_l, 2 * p_ + 2)
                    dve.tensor_tensor(hsum[:, p_, :], hsum[:, p_, :], lX[1][:, 0:NLAT], ALU.add).then_inc(lru_h, 1)
                    dve.wait_ge(lru_h, p_ + 1)
                    dve.tensor_tensor(lX[1][:, 0:NLAT], hsum[:, p_, :], gate[:, p_, :], ALU.mult).then_inc(lru_o, 1)

                def out(p_):
                    dve.wait_ge(lru_hi, p_ + 1)
                    dve.tensor_tensor(xl[:, p_, 0:NLAT], lX[1][:, 0:NLAT], xh[:, p_, 0:NLAT].bitcast(F32), ALU.subtract
                                      ).then_inc(cd_cat, 1)

                def att(a):
                    if 1 <= a <= NA2:
                        b = a - 1
                        st = st2[:, b % 2, :]
                        dve.wait_ge(p2_ready, 2 * b + 2)
                        dve.reciprocal(st[:, 4:6], st[:, 2:4]).then_inc(rinv2, 1)
                        dve.wait_ge(rinv2, 2 * b + 1)
                        dve.tensor_scalar(st[:, 5:6], st[:, 5:6], dl[:, 5:6], None, ALU.mult).then_inc(rinv2, 1)
                        dve.wait_ge(rinv2, 2 * b + 2)
                        if b:
                            dve.wait_ge(tr2_done, b)
                        dve.tensor_scalar(wb[:], pb[1][:], st[:, 5:6], None, ALU.mult).then_inc(w_part, 1)
                        dve.wait_ge(w_part, b + 1)
                        dve.scalar_tensor_tensor(wb[:], pb[0][:], st[:, 4:5], wb[:], ALU.mult, ALU.add).then_inc(w_done, 1)
                    if 2 <= a <= NA2 + 1:
                        b = a - 2
                        dve.wait_ge(rr_ready, b + 1)
                        dve.tensor_scalar(onq[b // 4][:, P * (b % 4):P * (b % 4) + P], B6[:, 0:P], st2[:, b % 2, 6:7], None,
                                          ALU.mult).then_inc(on_done, 1)
                    if a < NA2:
                        for s in range(2):
                            dve.wait_ge(s2_done, 2 * a + s + 1)
                            dve.tensor_reduce(st2[:, a % 2, s:s + 1], G[s][:, 0:T], AX.X, ALU.max, negate=True
                                              ).then_inc(max2_ready, 1)

                dve.wait_ge(dlam_set, 1)
                for what, i in SCHED:
                    if what == "act":
                        decay(i)
                    if what == "root":
                        scan(i)
                    if what == "out":
                        out(i)
                    if what == "att":
                        att(i)
                dve.wait_ge(dg_set, 1)
                for qt in range(5):
                    if qt < 4:
                        dve.wait_ge(oq_done, qt + 1)
                        if qt >= 2:
                            dve.wait_ge(cd_cat2, qt - 1)
                        dve.tensor_scalar(ovb[qt % 2][:], (B6, B7)[qt % 2], dg[:, 0:1], None, ALU.mult).then_inc(ov_ready, 1)
                    if qt:
                        q = qt - 1
                        dve.wait_ge(oq_hi, qt)
                        dve.tensor_tensor(xl[:, 4:8, P * q:P * q + P], ovb[q % 2][:].rearrange("p (h t) -> p h t", h=4),
                                          xh[:, 4:8, P * q:P * q + P].bitcast(F32), ALU.subtract).then_inc(cd_cat2, 1)

            dve.memset(eps[:], EPS).then_inc(eps_set, 1)
            dve.wait_ge(con_landed, 32)
            split_lo(0, 0, KC)
            split_lo(1, 1, KC)
            dve.wait_ge(scb0_ready, 1)
            for q, b in enumerate((1, 3, 5)):
                dve.wait_ge(mini_landed[b % 4], 16 * (b // 4 + 1))
                for j in range(4):
                    for s in range(2):
                        if q + j + s:
                            dve.wait_ge(mini_dot, 8 * q + 2 * j + s)
                        dot(mini[b % 4][:, j, :], s, scb0, M[:, 4 * b + j, s:s + 1]).then_inc(mini_dot, 1)
            dve.wait_ge(mini_mm, 3)
            dve.wait_ge(mini_dot, 24)
            for b in range(6):
                src = M[:, 4 * b:4 * b + 4, :] if b % 2 else G[0][:, 8 * b:8 * b + 8].rearrange("p (t s) -> p t s", s=2)
                dve.tensor_tensor(M[:, 4 * b:4 * b + 4, :], src,
                                  pr("bmod")[:, 4 * b:4 * b + 4].unsqueeze(2).to_broadcast([P, 4, 2]), ALU.add
                                  ).then_inc(mini_set, 1)
            dve.wait_ge(mini_set, 6)
            prep(0, 0)
            norm(0, SEGS)
            ffn(0, 0, BASE["ffn0"], KC if upto >= 1 else 0, 0, SEGS)
            if upto >= 1:
                prep(1, 20)
                norm(1, SEGS)
                ab_in_dve()
                na_dve()
                ssd_dve()
                down(ABO, KC if upto >= 2 else 0, KC, 1, SEGS)
            if upto >= 2:
                prep(2, 20)
                norm(2, SEGS)
                ffn(1, 2, BASE["ffn1"], KC, 20, SEGS)
                prep(3, 40)
                norm(3, SEGS)
                ffn(2, 3, BASE["ffn2"], KC if upto >= 3 else 0, None, SEGS)
            if upto >= 3:
                prep(4, 40)
                norm(4, SEGS)
                cd_in_dve()
                cd_mid_dve()
                down(CDO, KC, KC, 4, LSEG)
                prep(5, 40)
                norm(5, LSEG)
                ffn(3, 5, BASE["ffn3"], 0, None, LSEG)

        @block.gpsimd
        def _(pool):
            def add_squares(n, ns):
                for j in range(KC):
                    pool.wait_ge(sq_done, 8 * n + j + 1)
                    if j == 0:
                        pool.tensor_copy(ssq[:, 0:ns], sq[0][:, 0:ns]).then_inc(ssq_acc, 1)
                    else:
                        pool.wait_ge(ssq_acc, 8 * n + j)
                        pool.tensor_tensor(ssq[:, 0:ns], ssq[:, 0:ns], sq[j % 2][:, 0:ns], ALU.add
                                           ).then_inc(ssq_acc, 1)

            def norm(n, ns):
                add_squares(n, ns)
                pool.wait_ge(rstd_ready, n + 1)
                for j in range(KC):
                    if j >= 2:
                        pool.wait_ge(aff_done, 8 * n + j - 1)
                    pool.tensor_tensor(vn[j % 2][:, 0:ns], x[:, j, 0:ns], rstd[:, 0:ns], ALU.mult
                                       ).then_inc(v_ready, 1)

            def prod_mods(it0):
                with pool.Fori(0, FH - 1) as i:
                    for j in range(3):
                        pool.wait_ge(mod_dot, i * 3 + (3 * it0 + j + 1))
                        pool.tensor_tensor(mraw[:, j, :], mraw[:, j, :], scb[:, 1, :], ALU.mult).then_inc(mod_prod, 1)

            def ab_pool():
                pool.wait_ge(rb_landed, 16 * ROWS)
                pool.wait_ge(mask_landed, 16)
                pool.wait_ge(bm_zero, 2)
                for u in range(32):
                    n, h = u // 8, u % 8
                    if u >= 2:
                        pool.wait_ge(na_biased, u - 1)
                    row = rb[:, h, 16 - STRIP_OFF[n]:48 - STRIP_OFF[n]]
                    win = bass.AP(tensor=row.tensor, offset=row.offset, ap=[row.ap[0], [RPB_ROW, ROWS], [1, 32]])
                    pool.tensor_tensor(bm[u % 2][:, 0:256].rearrange("p (r c) -> p r c", c=32), win,
                                       namask[:, (0, 1, 1, 2)[n], :].rearrange("p (r c) -> p r c", c=32), ALU.add
                                       ).then_inc(bm_ready, 1)
                pool.wait_ge(dw_set, 1)
                pool.wait_ge(tk_ready, 9)
                for e in range(10):
                    d, tt = e % 2, (FWD_SEQ, BWD_SEQ)[e % 2][e // 2]
                    if e >= 2:
                        pool.wait_ge(st_mm, e - 1)
                    pool.tensor_tensor(xw[e % 2][:].rearrange("p (h q) -> p h q", q=64),
                                       xst[:, tt, :].rearrange("p (h q) -> p h q", q=64),
                                       heads(dend[:, tt, 8 * d:8 * d + 8], 8, 64), ALU.mult).then_inc(xw_ready, 1)

                def gate(tt):
                    pool.wait_ge(y_read, tt + 1)
                    tk = slice(P * tt, P * tt + P)
                    pool.tensor_tensor(gy[:, :, tk], gy[:, :, tk], zs[:, :, tk], ALU.mult).then_inc(gz_done, 1)

                for u in range(12):
                    tt, g, st = u // 2, u % 2, u % 2
                    if u == 0:
                        pool.wait_ge(na_cat, 6)
                    if u >= 2:
                        pool.wait_ge(y_mm, u - 1)
                    for d in range(2):
                        pool.tensor_tensor(xdt[st][d][:].rearrange("p (h q) -> p h q", q=64),
                                           xst[:, tt, 256 * g:256 * g + 256].rearrange("p (h q) -> p h q", q=64),
                                           heads(dt[:, tt, 8 * d + 4 * g:8 * d + 4 * g + 4], 4, 64), ALU.mult
                                           ).then_inc(xdt_ready, 1)
                    if g == 1 and tt >= 1:
                        gate(tt - 1)
                gate(5)

            def cd_pool():
                pool.wait_ge(rope_landed, 16)
                for i in range(8):
                    pool.wait_ge(kq_done, 8 + i + 1)
                    pool.wait_ge(dl_set, 2)
                    if i >= 2:
                        pool.wait_ge(rope_done, i - 1)
                    src = k2[:, i, 0:NLAT] if i < 4 else q2[:, i - 4, :]
                    pool.tensor_tensor(t1b[i % 2][:], src, rope[:, 0, :], ALU.mult).then_inc(t1_ready, 1)
                for e in range(8):
                    p_, d = e // 2, e % 2
                    pool.wait_ge(gate_sig, 2 * e + 2)
                    pool.tensor_tensor(lI[d][:], lI[d][:], xc[:, p_, :], ALU.mult).then_inc(lru_ix, 1)

            norm(0, T)
            prod_mods(0)
            prod_mods(10)
            if upto >= 1:
                norm(1, T)
                ab_pool()
            if upto >= 2:
                norm(2, T)
                prod_mods(20)
                prod_mods(30)
                norm(3, T)
            if upto >= 3:
                norm(4, T)
                cd_pool()
                norm(5, NLAT)


def host_arrays(a):
    f = np.float32

    def tiles(w_, cols=None):
        k, n = w_.shape
        return np.ascontiguousarray(w_.reshape(k // P, P, n // P, P).transpose(2, 1, 0, 3)).reshape(n // P, P, k)

    def vec(v):
        return np.asarray(v).reshape(-1, P).T

    out = {}
    xt = np.concatenate([a["x"][0], a["ctx"][0]], axis=0).T
    out["x"] = np.ascontiguousarray(xt.reshape(KC, P, T).transpose(1, 0, 2))
    out["wmn"] = np.stack([a["w_mod"][i].T.reshape(NMT, P, D) for i in range(2)]).reshape(2 * NMT, P, D)
    wk = tiles(a["w_mod"][0][:, 0:24 * P]).reshape(6, 4, P, D)
    out["wmk"] = wk[0::2].reshape(12, P, D)
    out["ccb"] = np.broadcast_to(np.stack([a["c"][0], a["c_ctx"]])[None], (P, 2, D))
    w13, w2 = [], []
    for i in range(2):
        for h in range(2):
            t1, t3 = tiles(a["ffn_w1"][i, h]), tiles(a["ffn_w3"][i, h])
            w13.append(np.stack([t1, t3], 1).reshape(2 * FC, P, D))
            for q in range(2):
                w2.append(tiles(a["ffn_w2"][i, h][q * FH * P:(q + 1) * FH * P]))
    out["w13"], out["w2"] = np.concatenate(w13), np.concatenate(w2)

    abw, gw = a["ab_w_in"][0], 512
    order = [(2 * gw, 3 * gw), (gw, 2 * gw), (0, gw), (4 * gw, 6 * gw), (3 * gw, 4 * gw)]
    out["abin"] = np.concatenate([tiles(abw[:, p:q]) for p, q in order])
    out["wdt"] = np.ascontiguousarray(abw[:, 6 * gw:].reshape(KC, P, 16).transpose(1, 0, 2)).reshape(P, KC * 16)
    out["about"] = tiles(a["ab_w_out"][0])
    cdw = a["cd_w_in"][0]
    order = [(4 * gw, 5 * gw), (3 * gw, 4 * gw), (2 * gw, 3 * gw), (gw, 2 * gw), (0, gw)]
    out["cdin"] = np.concatenate([tiles(cdw[:, p:q]) for p, q in order])
    out["cdout"] = tiles(a["cd_w_out"][0])
    bd = np.zeros((2, 2, 4, P, P), f)
    for g, n in enumerate(("lru_wa", "lru_wx")):
        for b in range(2):
            bd[g, :, :, 64 * b:64 * b + 64, 64 * b:64 * b + 64] = a[n][0].reshape(2, 4, 2, 64, 64)[:, :, b]
    out["lruw"] = np.ascontiguousarray(bd.reshape(16, P, P).transpose(1, 0, 2)).reshape(P, 16 * P)
    table = np.zeros(RPB_LEN + 16, f)
    table[RPB_PAD:RPB_PAD + 8 * RPB_HEAD] = np.asarray(a["na_rpb"][0]).reshape(-1)
    out["rpb"] = np.stack([np.roll(table, c)[:RPB_LEN] for c in range(16)])

    def rep(v):
        return np.broadcast_to(np.asarray(v).reshape(1, -1), (P, np.asarray(v).size))

    def two(v):
        return np.concatenate([v, v]).reshape(P, 1)

    par = {
        "bmod": vec(a["b_mod"].reshape(-1)), "normg": vec(a["norm_g"].reshape(-1)),
        "naqg": two(a["na_q_g"][0]), "nakg": two(a["na_k_g"][0]),
        "scw": a["ssd_conv_w"][0].reshape(4, 8, P).transpose(2, 1, 0).reshape(P, 32),
        "scb": vec(a["ssd_conv_b"][0]), "dtb": rep(a["ssd_dt_bias"][0]), "alog": rep(a["ssd_a_log"][0]),
        "ssdd": np.repeat(a["ssd_d"][0], 64).reshape(4, P).T, "ssdg": vec(a["ssd_norm_g"][0]),
        "lcw": a["lru_conv_w"][0].reshape(4, 4, P).transpose(2, 1, 0).reshape(P, 16),
        "lcb": vec(a["lru_conv_b"][0]), "lba": vec(a["lru_ba"][0].reshape(-1)),
        "lbx": vec(a["lru_bx"][0].reshape(-1)), "lam": vec(a["lru_lambda"][0].reshape(-1)),
        "dqg": two(a["diff_q_g"][0]), "dkg": two(a["diff_k_g"][0]), "subg": vec(a["diff_subln_g"][0]),
        "dlam": rep(a["diff_lambda"][0]),
        "cc": np.stack([vec(a["c"][0]), vec(a["c_ctx"])], 2).reshape(P, 16),
    }
    out["par"] = np.concatenate([par[n] for n in PCOL], axis=1)

    i = np.arange(P)
    swap = np.zeros((P, P), f)
    swap[i[0::2] + 1, i[0::2]] = -1.0
    swap[i[0::2], i[0::2] + 1] = 1.0
    con = {"ident": np.eye(P, dtype=f), "ones": np.ones((P, P), f),
           "blk": (i[:, None] // 64 == i[None] // 64).astype(f),
           "trif": (i[:, None] <= i[None]).astype(f), "trib": (i[:, None] >= i[None]).astype(f), "swap": swap}
    out["con"] = np.concatenate([con[n] for n in CCOL], axis=1)
    t = np.arange(NLAT)
    inv = (10000.0 ** (-np.arange(16, dtype=f) / 16)).astype(f)
    ang = np.concatenate([(t // GRID_W).astype(f)[:, None] * inv, (t % GRID_W).astype(f)[:, None] * inv], 1)
    pair = (i % 64) // 2
    out["rope"] = np.stack([np.cos(ang).T[pair], np.sin(ang).T[pair]], 1).astype(f)
    kc, qc = np.arange(32), np.arange(16)
    mask = np.zeros((3, P, ROWS, 32), f)
    for v, blk_ in enumerate((0, 1, 3)):
        q0 = np.clip(16 * blk_ + qc - 8, 0, GRID_W - 16)
        col = STRIP0[blk_] + kc
        ok = (col[None] >= q0[:, None]) & (col[None] < q0[:, None] + 16)
        mask[v] = np.where(np.tile(ok, (ROWS, 1))[:, None, :], 0.0, -1e30)
    out["mask"] = np.ascontiguousarray(mask.reshape(3, P, 256).transpose(1, 0, 2))
    return {k: np.ascontiguousarray(v, dtype=f) for k, v in out.items()}


def kernel(**inputs):
    import concourse.bacc as bacc
    from concourse.bass_utils import run_bass_kernel_spmd

    arrays = host_arrays({k: np.asarray(v) for k, v in inputs.items()})
    nc = bacc.Bacc("TRN2", target_bir_lowering=False, num_devices=1, dynamic_dma_scratch_size=1024)
    dr = {k: nc.dram_tensor("in_" + k, v.shape, F32, kind="ExternalInput").ap() for k, v in arrays.items()}
    dr["out"] = nc.dram_tensor("out_t", (P, KC, NLAT), F32, kind="ExternalOutput").ap()
    build(nc, dr)
    r = run_bass_kernel_spmd(nc, [{"in_" + k: v for k, v in arrays.items()}], core_ids=[0])
    o = r.results[0]["out_t"]
    return np.ascontiguousarray(o.transpose(2, 1, 0)).reshape(1, NLAT, D)
```

```python
from contextlib import ExitStack

import numpy as np

import concourse.bass as bass
import concourse.mybir as mybir
from concourse.alu_op_type import AluOpType as ALU

F32 = mybir.dt.float32
F32R = mybir.dt.float32r
ACT = mybir.ActivationFunctionType
AX = mybir.AxisListType

P = 128
D = 1024
NLAT, NCTX = 512, 256
T = NLAT + NCTX
KC = D // P
DFF = 2816
FC = DFF // P
FH = FC // 2
NMT = 9 * KC
EPS = 1e-6
HD = 64
NT = T // P
LT = NLAT // P
GRID_W, ROWS = 64, 8
SEGS = ((0, NLAT, 0), (NLAT, T, 1))
LSEG = ((0, NLAT, 0),)
STRIP0 = (0, 8, 24, 32)
STRIP_OFF = (0, 8, 8, 16)
PE_MINI = (1, 3, 5, 7, 9, 11, 13)
DVE_MINI = (0, 2, 4, 6, 8, 10, 12, 14, 15)
NWARM = 5
MINI_GROUPS = ((0, 1, 2), (3, 4, 5, 6), (7, 8, 9, 10), (11, 12, 13), (14, 15))
RPB_PAD = 32
RPB_ROW = 31
RPB_HEAD = 15 * 31
RPB_RUN = 7 * RPB_ROW + 32 + 16
RPB_LEN = RPB_PAD + 8 * RPB_HEAD + 48
LAM_INIT = 0.8 - 0.6 * float(np.exp(-0.3))
FWD_SEQ = (4, 5, 0, 1, 2, 3)
BWD_SEQ = (5, 4, 3, 2, 1, 0)

AB_IN_T, AB_OUT_T, CD_IN_T, CD_OUT_T = 24, 8, 20, 8
UP, DOWN = 2 * FH, KC
FFN_T = 2 * (UP + DOWN)
BASE = {}
_t = 0
for _name, _n in (("ffn0", FFN_T), ("ab_in", AB_IN_T), ("ab_out", AB_OUT_T), ("ffn1", FFN_T),
                  ("ffn2", FFN_T), ("cd_in", CD_IN_T), ("cd_out", CD_OUT_T), ("ffn3", FFN_T)):
    BASE[_name] = _t
    _t += _n
N_TILES = _t

PCOL = {}
_c = 0
for _name, _n in (("bmod", 2 * NMT), ("normg", 6 * KC), ("naqg", 1), ("nakg", 1), ("scw", 32), ("scb", 8),
                  ("dtb", 16), ("alog", 16), ("ssdd", 4), ("ssdg", 4), ("lcw", 16), ("lcb", 4), ("lba", 8),
                  ("lbx", 8), ("lam", 8), ("dqg", 1), ("dkg", 1), ("subg", 1), ("dlam", 256), ("cc", 16)):
    PCOL[_name] = (_c, _c + _n)
    _c += _n
NPAR = _c
CCOL = {n: (i * P, (i + 1) * P) for i, n in enumerate(("ident", "ones", "blk", "trif", "trib", "swap"))}
NCON = 6 * P


def build(nc, dr):
    ctx = ExitStack()
    with ctx:
        arena0 = 2048

        def at(name, shape, word, dt=F32):
            return nc.alloc_sbuf_tensor_at(name, shape, dt, offset=arena0 + 4 * word)

        w = 0
        x = at("x", [P, KC, T], w); w += KC * T
        XH = w
        xh = at("xh", [P, KC, T], w, F32R); w += KC * T
        XL = w
        xl = at("xl", [P, KC, T], w, F32R); w += KC * T
        H = w
        hh = at("hh", [P, FH, T], w, F32R); w += FH * T
        hl = at("hl", [P, FH, T], w, F32R); w += FH * T
        MR = w
        mraw = at("mraw", [P, 3, D], w); w += 3 * D
        raw = [at(f"raw{s}", [P, FH * P], w + s * FH * P) for s in range(2)]; w += 2 * FH * P
        wh = [at(f"wh{s}", [P, FH * P], w + s * FH * P, F32R) for s in range(2)]; w += 2 * FH * P
        wl = [at(f"wl{s}", [P, FH * P], w + s * FH * P, F32R) for s in range(2)]; w += 2 * FH * P
        TB = w
        tmp = [at(f"tmp{s}", [P, T], w + s * T) for s in range(4)]; w += 4 * T + 32
        g1s, hf = tmp[0], tmp[1]
        vn = (tmp[0], tmp[1])
        yn = (tmp[2], tmp[3])
        SQ = w
        sq = [at(f"sq{s}", [P, T], w + s * T) for s in range(2)]; w += 2 * T
        ssq = at("ssq", [P, T], w); w += T
        rstd = at("rstd", [P, T], w); w += T
        con = at("con", [P, NCON], w); w += NCON
        par = at("par", [P, NPAR], w); w += (NPAR + 7) // 8 * 8
        M = at("M", [P, 2 * NMT, 2], w); w += 4 * NMT
        modA = at("modA", [P, 6, KC, 2], w); w += 6 * KC * 2
        modG = at("modG", [P, 6, KC, 2], w); w += 6 * KC * 2
        sc = at("sc", [P, KC, 2], w); w += 2 * KC
        blkr = at("blkr", [P, P], w, F32R); w += P
        eps = at("eps", [P, 1], w); w += 8
        mcol = at("mcol", [P, 3, 2], w); w += 8
        FREE = w
        LIMIT = (229368 - arena0) // 4

        def cst(n):
            return con[:, CCOL[n][0]:CCOL[n][1]]

        def pr(n):
            return par[:, PCOL[n][0]:PCOL[n][1]]

        mini = [at(f"mini{j}", [P, D], XH + j * D) for j in range(2 * KC)]
        gmini = [at(f"gmini{s}", [P, 4, D], H + 4 * D + s * 8 * D) for s in range(2)]
        scb0 = at("scb0", [P, 2, D], MR)
        scb = at("scb", [P, 2, D], SQ)

        w = H
        kq = at("kq", [P, 8, T], w); w += 8 * T
        zs = at("zs", [P, 4, T], w); w += 4 * T
        cv = at("cv", [P, 8, T], w); w += 8 * T
        dtT = at("dtT", [16, T], H + 8 * T)
        VT0 = w
        vT = at("vT", [P, 4, T], w); w += 4 * T
        assert w <= MR + 3 * D
        ABX = w
        pad = [at(f"pad{s}", [P, 774], TB + s * 776) for s in range(2)]
        cb = [at(f"cb{s}", [P, 771], TB + (2 + s) * 776) for s in range(2)]
        sqh, sql = at("sqh", [P, T], TB + 2 * 776, F32R), at("sql", [P, T], TB + 3 * 776, F32R)
        vsa = at("vsa", [P, 6, 512], XH + 4 * T)
        vsb = at("vsb", [P, 4, 512], XL + 4 * T)
        nsS = [at(f"nsS{s}", [P, 512], VT0 + s * 512) for s in range(2)]
        nsP = [at(f"nsP{s}", [P, 512], VT0 + 1024 + s * 512) for s in range(2)]
        nsT = [at(f"nsT{s}", [P, 512], VT0 + 2048 + s * 512) for s in range(2)]
        rb = at("rb", [P, 8, RPB_RUN], SQ)
        bm = [at(f"bm{s}", [P, 512], TB + s * 512) for s in range(2)]
        namask = at("namask", [P, 3, 256], TB + 1024)
        onorm = [at(f"onorm{s}", [P, 512], TB + 1792 + s * 512) for s in range(2)]
        vst = [at(f"vst{s}", [P, 512], ABX + s * 512) for s in range(2)]
        nst = at("nst", [P, 4, 8], TB + 2816)
        xst = at("xst", [P, NT, 512], H)
        bst = at("bst", [P, NT, 256], H + 3072)
        xw = [at(f"xw{s}", [P, 512], H + 4608 + s * 512) for s in range(2)]
        hm = at("hm", [P, 512], H + 5632)
        hsa = at("hsa", [P, 6, 512], XH + 4 * T)
        hsb = at("hsb", [P, 4, 512], XL + 4 * T)
        hst = [[hsa[:, s, :] for s in range(5)], [hsa[:, 5, :]] + [hsb[:, s, :] for s in range(4)]]
        gy = at("gy", [P, 4, T], VT0)
        SET = (TB, SQ)
        sL = [[at(f"sL{s}{d}", [P, 512], SET[s] + 512 * d) for d in range(2)] for s in range(2)]
        sE = [[at(f"sE{s}{d}", [P, 512], SET[s] + 1024 + 512 * d) for d in range(2)] for s in range(2)]
        xdt = [[at(f"xdt{s}{d}", [P, 256], SET[s] + 2048 + 256 * d) for d in range(2)] for s in range(2)]
        cbm = [[at(f"cbm{s}{d}", [P, 128], SET[s] + 2560 + 128 * d) for d in range(2)] for s in range(2)]
        sqg = [at(f"sqg{s}", [P, T], SQ + s * T) for s in range(2)]
        lng, rsg = at("lng", [P, T], TB), at("rsg", [P, T], TB + T)
        vg = [at(f"vg{s}", [P, T], TB + (2 + s) * T) for s in range(2)]

        w = H
        k2 = at("k2", [P, 4, T], w); w += 4 * T
        q2 = at("q2", [P, 4, NLAT], w); w += 4 * NLAT
        LR = w
        vT2 = at("vT2", [P, 4, T], w); w += 4 * T
        vtok = at("vtok", [P, NT, 512], w); w += NT * 512
        xc = at("xc", [P, 4, T], w); w += 4 * T
        gate = at("gate", [P, 4, NLAT], w); w += 4 * NLAT
        hsum = at("hsum", [P, 4, NLAT], w); w += 4 * NLAT
        rope = at("rope", [P, 2, NLAT], w); w += 2 * NLAT
        assert w <= MR + 3 * D
        lruw = at("lruw", [P, 16, P], SQ)
        lR, lA, lI, lX = ([at(f"{n}{d}", [P, T], (LR, XH + 4 * T)[d] + q * T) for d in range(2)]
                          for q, n in enumerate(("lR", "lA", "lI", "lX")))
        ATT = (TB, XL + 4 * T)
        pb = [[at(f"pb{q}{s}", [P, T], ATT[q] + s * T) for s in range(2)] for q in range(2)]
        wb = [at(f"wb{q}", [P, T], ATT[q] + 2 * T) for q in range(2)]
        wtb = [at(f"wtb{q}", [P, T], ATT[q] + 3 * T) for q in range(2)]
        ovb = [at(f"ovb{s}", [P, 512], TB + s * T) for s in range(2)]

        fw = [FREE]

        def small(name, shape, dt=F32):
            n = 1
            for s_ in shape[1:]:
                n *= s_
            t_ = at(name, shape, fw[0], dt)
            fw[0] += (n + 7) // 8 * 8
            assert fw[0] <= LIMIT, (name, fw[0], LIMIT)
            return t_

        assert FREE <= LIMIT
        wdt, wdh, wdl = small("wdt", [P, P]), small("wdh", [P, P], F32R), small("wdl", [P, P], F32R)
        TH = [P, NT, 16]
        dtu, dte, dts, dt2, dtp, dt, dA, ea = (small(n, TH) for n in ("dtu", "dte", "dts", "dt2", "dtp", "dt", "dA", "ea"))
        acs, tm, dend, cdec = (small(n, TH) for n in ("acs", "tm", "dend", "cdec"))
        qg8 = small("qg8", [P, 2])

        G = [ctx.enter_context(nc.psum_tensor(f"G{s}", [P, 1024], F32)) for s in range(2)]
        NP = ctx.enter_context(nc.psum_tensor("NP", [P, 1024], F32))
        B67 = ctx.enter_context(nc.psum_tensor("B67", [P, 1024], F32))
        B6, B7 = B67[:, 0:512], B67[:, 512:1024]

        def sem(name):
            return ctx.enter_context(nc.semaphore(name))

        par_landed, con_landed, x_landed, out_stored = sem("par_landed"), sem("con_landed"), sem("x_landed"), sem("out_stored")
        raw_landed = [sem("raw_landed0"), sem("raw_landed1")]
        hi_done, lo_done, mm_done = sem("hi_done"), sem("lo_done"), sem("mm_done")
        psum_free = [sem("psum_free0"), sem("psum_free1")]
        h_hi, h_ready = sem("h_hi"), sem("h_ready")
        mini_landed = [sem(f"mini_landed{q}") for q in range(len(MINI_GROUPS))]
        gmini_landed, gate_prep = sem("gmini_landed"), sem("gate_prep")
        mini_mm, mini_dot, mini_set = sem("mini_mm"), sem("mini_dot"), sem("mini_set")
        mod_landed, mod_dot, mod_prod, mod_sum, mod_set = (sem("mod_landed"), sem("mod_dot"), sem("mod_prod"),
                                                           sem("mod_sum"), sem("mod_set"))
        scb0_landed, scb0_ready, scb_landed, scb_ready = (sem("scb0_landed"), sem("scb0_ready"), sem("scb_landed"),
                                                          sem("scb_ready"))
        sc_ready, eps_set, prep_done = sem("sc_ready"), sem("eps_set"), sem("prep_done")
        sq_done, ssq_acc, norm_sum, norm_ln, rstd_ready = (sem("sq_done"), sem("ssq_acc"), sem("norm_sum"),
                                                           sem("norm_ln"), sem("rstd_ready"))
        v_ready, aff_done, xn_hi, xn_ready = sem("v_ready"), sem("aff_done"), sem("xn_hi"), sem("xn_ready")

        fw[0] = FREE
        t1b = [small(f"t1b{s}", [P, NLAT]) for s in range(2)]
        t2b = small("t2b", [P, NLAT])
        coef = small("coef", [P, 8, 8])
        dl = small("dl", [P, 8])
        dg = small("dg", [P, 4])
        st2 = small("st2", [P, 4, 8])
        hsq, hrs = small("hsq", [P, 3, 16]), small("hrs", [P, 16])
        qg2 = small("qg2", [P, 2])
        fw[0] = FREE
        onq = [at(f"onq{s}", [P, 512], SQ + 2048 + 512 * s) for s in range(2)]
        onq += [small(f"onq{s + 2}", [P, 512]) for s in range(2)]
        junk = small("junk", [P, P])

        wdt_landed, wdt_hi, wdt_lo, dt_mm, dt_copied, dt_turned, dt_abs, dt_exp, dt_set, dve_chain = (
            sem(n) for n in ("wdt_landed", "wdt_hi", "wdt_lo", "dt_mm", "dt_copied", "dt_turned", "dt_abs", "dt_exp", "dt_set", "dve_chain"))
        sql_set, kq_sq, kq_sum, kq_ln, kq_rs, kq_done = (sem(n) for n in ("sql_set", "kq_sq", "kq_sum", "kq_ln", "kq_rs", "kq_done"))
        pad_zero, conv_tap, conv_done, cv_ready = (sem(n) for n in ("pad_zero", "conv_tap", "conv_done", "cv_ready"))
        rb_landed, mask_landed, bm_zero, bm_ready = (sem(n) for n in ("rb_landed", "mask_landed", "bm_zero", "bm_ready"))
        vst_ready = sem("vst_ready")
        vt_done, vs_ready, s_done, na_biased, nmax_ready, p_ready, tr_done, pt_ready, pv_done, inv_ready, o_read = (
            sem(n) for n in ("vt_done", "vs_ready", "s_done", "na_biased", "nmax_ready", "p_ready", "tr_done", "pt_ready",
                             "pv_done", "inv_ready", "o_read"))
        ot_done, cat_hi, na_cat = sem("ot_done"), sem("cat_hi"), sem("na_cat")
        tk_done, tk_ready, acs_mm, acs_set, tm_set, dend_set, dw_set, xw_ready, st_mm, hm_set, h_set = (
            sem(n) for n in ("tk_done", "tk_ready", "acs_mm", "acs_set", "tm_set", "dend_set", "dw_set", "xw_ready",
                             "st_mm", "hm_set", "h_set"))
        r_mm, d_ready, l_ready, e_ready, m_ready, xdt_ready, y_mm, y_read, gz_done = (
            sem(n) for n in ("r_mm", "d_ready", "l_ready", "e_ready", "m_ready", "xdt_ready", "y_mm", "y_read", "gz_done"))
        cb_set, gsq_done, gn_sum, gn_ln, gn_rs, vg_ready, gcat_hi, ssd_cat = (
            sem(n) for n in ("cb_set", "gsq_done", "gn_sum", "gn_ln", "gn_rs", "vg_ready", "gcat_hi", "ssd_cat"))

        names = ("rope_landed lruw_landed coef_exp coef_set dl_set dl_exp dlam_set dg_set v2_done v2_ready rope_mm "
                 "t1_ready t2_set rope_done gate_mm gate_sig lru_a lru_t lru_a2 lru_m lru_ix lru_q lru_b scan_c scan_l "
                 "lru_h lru_o lru_hi cd_cat s2_done max2_ready p2_ready w_done tr2_done wt_ready pv2_done "
                 "ss_ready ss_ln rr_ready onr_done on_done oq_done ov_ready oq_hi cd_cat2")
        (rope_landed, lruw_landed, coef_exp, coef_set, dl_set, dl_exp, dlam_set, dg_set, v2_done, v2_ready, rope_mm,
         t1_ready, t2_set, rope_done, gate_mm, gate_sig, lru_a, lru_t, lru_a2, lru_m, lru_ix, lru_q, lru_b, scan_c, scan_l,
         lru_h, lru_o, lru_hi, cd_cat, s2_done, max2_ready, p2_ready, w_done, tr2_done, wt_ready, pv2_done,
         ss_ready, ss_ln, rr_ready, onr_done, on_done, oq_done, ov_ready, oq_hi, cd_cat2) = (sem(n) for n in names.split())
        CD, CDO = BASE["cd_in"], BASE["cd_out"]
        NA2 = 16
        SCHED = []
        for p_ in range(5):
            if p_ < 4:
                SCHED += [("gates", p_)]
            SCHED += [("att", 4 * p_)]
            SCHED += ([("gated", p_ - 1)] if p_ else []) + ([("decay", p_)] if p_ < 4 else [])
            SCHED += [("att", 4 * p_ + 1)]
            SCHED += ([("hi", p_ - 1)] if p_ else []) + ([("comp", p_)] if p_ < 4 else [])
            SCHED += [("att", 4 * p_ + 2)]
            SCHED += ([("lo", p_ - 1)] if p_ else []) + ([("root", p_)] if p_ < 4 else [])
            SCHED += [("att", 4 * p_ + 3)]
            SCHED += [("scan", p_)] if p_ < 4 else []

        AB = BASE["ab_in"]
        ABO = BASE["ab_out"]
        NU = 40

        def strip(ap, n, width, c0):
            return ap.rearrange("p (r w) -> p r w", w=GRID_W)[:, :, c0:c0 + width]

        def vtile(g):
            return vsa[:, g, :] if g < 6 else vsb[:, g - 6, :]

        def heads(col, n, width):
            return col.unsqueeze(2).to_broadcast([P, n, width])

        def group(j):
            return [j in g for g in MINI_GROUPS].index(True)

        block = ctx.enter_context(nc.Block())

        @block.sync
        def _(sp):
            def load(t, slot, src, nk):
                if not (isinstance(t, int) and t < 2):
                    sp.wait_ge(lo_done, t - 1)
                sp.dma_start(raw[slot][:, 0:nk * P], src).then_inc(raw_landed[slot], 16)

            def load_tiles(base, count, dram, nk, row0=0):
                with sp.Fori(0, count // 2) as i:
                    for s in range(2):
                        src = dram[bass.ds(i * 2 + (row0 + s), 1)].rearrange("a p n -> (a p) n")
                        if base == 0:
                            sp.wait_ge(lo_done, i * 2 + (s + 1))
                            src = dram[bass.ds(i * 2 + (row0 + s + 2), 1)].rearrange("a p n -> (a p) n")
                            sp.dma_start(raw[s][:, 0:nk * P], src).then_inc(raw_landed[s], 16)
                        else:
                            load(i * 2 + (base + s), s, src, nk)

            def load_ffn(f, base):
                for h in range(2):
                    b = base + h * (UP + DOWN)
                    r = (f * 2 + h) * UP
                    if b == 0:
                        load_tiles(0, UP - 2, dr["w13"], KC, r)
                    else:
                        load_tiles(b, UP, dr["w13"], KC, r)
                    load_tiles(b + UP, DOWN, dr["w2"], FH, (f * 2 + h) * DOWN)

            sp.dma_start(par[:], dr["par"]).then_inc(par_landed, 16)
            sp.dma_start(scb0[:], dr["ccb"]).then_inc(scb0_landed, 16)
            sp.dma_start(x[:], dr["x"]).then_inc(x_landed, 16)
            for j in range(2 * KC):
                src = dr["wmk"][PE_MINI.index(j)] if j in PE_MINI else dr["wmn"][j]
                sp.dma_start(mini[j][:], src).then_inc(mini_landed[group(j)], 16)
                if j == KC:
                    sp.dma_start(con[:], dr["con"]).then_inc(con_landed, 16)
                if j in (10, 12):
                    s = j // 2 - 5
                    sp.dma_start(raw[s][:, 0:D], dr["w13"][s]).then_inc(raw_landed[s], 16)
            for s in range(2):
                sp.dma_start(gmini[s][:], dr["wmn"][16 + 4 * s:20 + 4 * s].rearrange("t p n -> p t n")).then_inc(gmini_landed, 16)
            sp.dma_start(wdt[:], dr["wdt"]).then_inc(wdt_landed, 16)
            load_ffn(0, BASE["ffn0"])
            load_tiles(AB, AB_IN_T, dr["abin"], KC)
            sp.wait_ge(kq_done, 8)
            for r in range(ROWS):
                base = dr["rpb"]
                src = bass.AP(tensor=base.tensor, offset=RPB_PAD + (7 - r) * RPB_ROW - 1,
                              ap=[[RPB_LEN, 16], [RPB_HEAD, 8], [1, RPB_RUN]])
                sp.dma_start(rb[16 * r:16 * r + 16, :, :], src).then_inc(rb_landed, 16)
            sp.wait_ge(cv_ready, 8)
            sp.dma_start(namask[:], dr["mask"]).then_inc(mask_landed, 16)
            load_tiles(ABO, AB_OUT_T, dr["about"], KC)
            load_ffn(1, BASE["ffn1"])
            load_ffn(2, BASE["ffn2"])
            load_tiles(CD, 2, dr["cdin"], KC)
            sp.wait_ge(psum_free[0], CD // 2)
            sp.wait_ge(psum_free[1], CD // 2)
            sp.dma_start(rope[:], dr["rope"]).then_inc(rope_landed, 16)
            load_tiles(CD + 2, CD_IN_T - 2, dr["cdin"], KC, 2)
            sp.wait_ge(kq_done, 16)
            sp.dma_start(lruw[:].rearrange("p a n -> p (a n)"), dr["lruw"]).then_inc(lruw_landed, 16)
            load_tiles(CDO, CD_OUT_T, dr["cdout"], KC)
            load_ffn(3, BASE["ffn3"])
            for j in range(KC):
                sp.wait_ge(psum_free[j % 2], (N_TILES - KC + j) // 2 + 1)
                sp.dma_start(dr["out"][:, j, :], x[:, j, 0:NLAT]).then_inc(out_stored, 16)
            sp.wait_ge(out_stored, 16 * KC)

        @block.tensor
        def _(pe):
            def weights_ready(t, slot, n):
                pe.wait_ge(lo_done, t + 1)
                if not (isinstance(n, int) and n == 0):
                    pe.wait_ge(psum_free[slot], n)

            def gemm_step(slot, k, nk, rh, rl, segs):
                W, L = wh[slot][:, k * P:(k + 1) * P], wl[slot][:, k * P:(k + 1) * P]
                for a, b, _s in segs:
                    pe.matmul(G[slot][:, a:b], W, rh[:, k, a:b], start=(k == 0), stop=False)
                for a, b, _s in segs:
                    pe.matmul(G[slot][:, a:b], W, rl[:, k, a:b], start=False, stop=False)
                for a, b, _s in segs:
                    mm = pe.matmul(G[slot][:, a:b], L, rh[:, k, a:b], start=False, stop=(k == nk - 1))
                return mm

            def gemm(t, slot, n, nk, rh, rl, segs, ready=None):
                weights_ready(t, slot, n)
                for k in range(nk):
                    if ready is not None:
                        ready(k)
                    mm = gemm_step(slot, k, nk, rh, rl, segs)
                mm.then_inc(mm_done, 1)

            def gemm_pair(t, rh, rl, segs, ready):
                for s in range(2):
                    weights_ready(t + s, s, t // 2)
                for k in range(KC):
                    ready(k)
                    for s in range(2):
                        mm = gemm_step(s, k, KC, rh, rl, segs)
                        if k == KC - 1:
                            mm.then_inc(mm_done, 1)

            def norm(n, segs, t=None):
                pe.wait_ge(ssq_acc, 7 * (n + 1))
                for a, b, _s in segs:
                    pe.matmul(NP[:, a:b], cst("ones"), ssq[:, a:b], start=True, stop=False)
                pe.wait_ge(sq_done, 8 * (n + 1))
                for a, b, _s in segs:
                    mm = pe.matmul(NP[:, a:b], cst("ones"), sq[1][:, a:b], start=False, stop=True)
                mm.then_inc(norm_sum, 1)
                if t is not None:
                    pe.wait_ge(psum_free[1], t // 2)
                    for _ in range(NWARM):
                        pe.matmul(G[1][:, 0:512], cst("ones"), con[:, 0:512], start=True, stop=True)

            def ffn(f, n, base, segs):
                for h in range(2):
                    b = base + h * (UP + DOWN)
                    hb = (2 * f + h) * FH

                    def xn(k):
                        pe.wait_ge(xn_ready, 8 * n + k + 1)

                    def hid(k):
                        pe.wait_ge(h_ready, hb + k + 1)

                    def pair(i):
                        for s in range(2):
                            gemm(i * 2 + (b + s), s, i + b // 2, KC, xh, xl, segs)

                    if h == 0:
                        gemm_pair(b, xh, xl, segs, xn)
                    with pe.Fori(int(h == 0), FH) as i:
                        pair(i)
                    d = b + UP
                    with pe.Fori(0, DOWN // 2) as i:
                        for s in range(2):
                            gemm(i * 2 + (d + s), s, i + d // 2, FH, hh, hl, segs, hid if s == 0 else None)

            def ab_in_pe():
                b = AB
                for c in range(AB_IN_T):
                    if c == 0:
                        gemm_pair(b, xh, xl, SEGS, lambda k: pe.wait_ge(xn_ready, 8 + k + 1))
                    if c >= 2:
                        gemm(b + c, c % 2, (b + c) // 2, KC, xh, xl, SEGS)
                    i = c - 5
                    if 0 <= i < 8:
                        pe.wait_ge(sql_set, i + 1)
                        if i:
                            pe.wait_ge(kq_ln, i)
                        for a, e, _s in SEGS:
                            pe.matmul(NP[:, a:e], blkr[:], sqh[:, a:e], start=True, stop=False)
                            mm = pe.matmul(NP[:, a:e], blkr[:], sql[:, a:e], start=False, stop=True)
                        mm.then_inc(kq_sum, 1)
                    if c == 10:
                        pe.wait_ge(wdt_lo, 1)
                        for k in range(KC):
                            wk = slice(16 * k, 16 * k + 16)
                            for W, X in ((wdh, xh), (wdh, xl), (wdl, xh)):
                                for a, e, _s in SEGS:
                                    mm = pe.matmul(B67[0:16, a:e], W[:, wk], X[:, k, a:e], start=(k == 0 and X is xh and W is wdh),
                                                   stop=(k == KC - 1 and W is wdl))
                        mm.then_inc(dt_mm, 1)
                    if c == 11:
                        pe.wait_ge(dt_copied, 1)
                        for tt in range(NT):
                            mm = pe.transpose(B6[:, 16 * tt:16 * tt + 16], dtT[:, P * tt:P * tt + P], cst("ident")[0:16, 0:16])
                        mm.then_inc(dt_turned, 1)

            def na_pe():
                for s in range(2):
                    pe.wait_ge(psum_free[s], ABO // 2)
                pe.wait_ge(dt_abs, 1)
                for g in range(10):
                    if g >= 2:
                        pe.wait_ge(vs_ready, g - 1)
                    if g < 8:
                        pe.wait_ge(vst_ready, g + 1)
                    bank = (B6, B7)[g % 2]
                    for c in range(4):
                        src = (vst[g % 2][:, P * c:P * c + P] if g < 8
                               else vT[:, c, NLAT + P * (g - 8):NLAT + P * (g - 7)])
                        mm = pe.transpose(bank[:, P * c:P * c + P], src, cst("ident"))
                    mm.then_inc(vt_done, 1)

                def scores(u):
                    h, bank = u % 8, G[0][:, 512 * (u % 2):512 * (u % 2) + 512]
                    hp = slice(64 * (h % 2), 64 * (h % 2) + 64)
                    kk, qq = kq[hp, h // 2, :], kq[hp, 4 + h // 2, :]
                    if 2 <= u < 34:
                        pe.wait_ge(na_biased, u - 1)
                    if u >= 34:
                        pe.wait_ge(p_ready, u - 1)
                    if u < 32:
                        n = u // 8
                        q = qq[:, P * n:P * n + P]
                        pe.matmul(bank[:, 0:256].rearrange("p (r c) -> p r c", c=32), q,
                                  strip(kk[:, 0:NLAT], 8, 32, STRIP0[n]), start=True, stop=True)
                        mm = pe.matmul(bank[:, 256:512], q, kk[:, NLAT:T], start=True, stop=True)
                    else:
                        for w_ in range(2):
                            mm = pe.matmul(bank[:, 256 * w_:256 * w_ + 256], qq[:, NLAT + P * w_:NLAT + P * w_ + P],
                                           kk[:, NLAT:T], start=True, stop=True)
                    mm.then_inc(s_done, 1)

                def turn(u):
                    pe.wait_ge(p_ready, u + 1)
                    if u >= 2:
                        pe.wait_ge(pt_ready, u - 1)
                    for c in range(4):
                        mm = pe.transpose(G[1][:, 512 * (u % 2) + P * c:512 * (u % 2) + P * c + P],
                                          nsP[u % 2][:, P * c:P * c + P], cst("ident"))
                    mm.then_inc(tr_done, 1)

                def values(u):
                    h = u % 8
                    o = NP[:, 512 * (u % 2):512 * (u % 2) + 128]
                    pe.wait_ge(pt_ready, u + 1)
                    if u >= 2:
                        pe.wait_ge(o_read, u - 1)
                    for c in range(4):
                        if u < 32:
                            g, w_, first, last = (2 * (u // 8) + c if c < 2 else 6 + c), 0, c == 0, c == 3
                        else:
                            g, w_, first, last = 8 + c % 2, c // 2, c % 2 == 0, c % 2 == 1
                        mm = pe.matmul(o[:, 64 * w_:64 * w_ + 64], nsT[u % 2][:, P * c:P * c + P],
                                       vtile(g)[:, 64 * h:64 * h + 64], start=first, stop=last)
                    mm.then_inc(pv_done, 1)

                def turn_out(gi):
                    pe.wait_ge(o_read, min(8 * gi + 8, NU))
                    if gi >= 2:
                        pe.wait_ge(na_cat, gi - 1)
                    else:
                        pe.wait_ge(vs_ready, 10)
                    for c in range(4):
                        mm = pe.transpose((B6, B7)[gi % 2][:, P * c:P * c + P], onorm[gi % 2][:, P * c:P * c + P],
                                          cst("ident"))
                    mm.then_inc(ot_done, 1)

                pe.wait_ge(kq_done, 8)
                for it in range(NU + 4):
                    if it < NU:
                        scores(it)
                    if it < 4:
                        pe.wait_ge(vs_ready, 10)
                        for _ in range(2):
                            pe.matmul(B7[:, 0:384], cst("ident"), con[:, 0:384], start=True, stop=True)
                    if 0 <= it - 2 < NU:
                        turn(it - 2)
                    if 0 <= it - 3 < NU:
                        values(it - 3)
                    if it >= 11 and (it - 11) % 8 == 0 and (it - 11) // 8 < 4:
                        turn_out((it - 11) // 8)
                turn_out(4)
                turn_out(5)

            def ssd_pe():
                pe.wait_ge(cv_ready, 8)
                for q in range(9):
                    if q < 2:
                        pe.wait_ge(na_cat, 5 + q)
                    else:
                        pe.wait_ge(tk_ready, q - 1)
                    for c in range(4):
                        tt = q if q < 6 else 2 * (q - 6) + c // 2
                        src = cv[:, c if q < 6 else 4 + c % 2, P * tt:P * tt + P]
                        mm = pe.transpose((B6, B7)[q % 2][:, P * c:P * c + P], src, cst("ident"))
                    mm.then_inc(tk_done, 1)
                pe.wait_ge(dt_set, 1)
                pe.wait_ge(o_read, NU)
                aout = NP[:, 0:96].rearrange("p (t c) -> p t c", c=16)
                pe.matmul(aout[:, :, 0:8], cst("trif"), dA[:, :, 0:8], start=True, stop=True)
                pe.matmul(aout[:, :, 8:16], cst("trib"), dA[:, :, 8:16], start=True, stop=True)
                pe.matmul(NP[:, 512:608], cst("ones"), dA[:].rearrange("p t c -> p (t c)"), start=True, stop=True
                          ).then_inc(acs_mm, 1)
                pe.wait_ge(tk_ready, 9)
                pe.wait_ge(pt_ready, NU)
                for s in range(5):
                    for d in range(2):
                        e = 2 * s + d
                        tt = (FWD_SEQ, BWD_SEQ)[d][s]
                        pe.wait_ge(xw_ready, e + 1)
                        if s:
                            pe.wait_ge(h_set, e - 1)
                        for g in range(2):
                            mm = pe.matmul(G[1][:, 512 * d + 256 * g:512 * d + 256 * g + 256],
                                           bst[:, tt, P * g:P * g + P], xw[e % 2][:, 256 * g:256 * g + 256],
                                           start=True, stop=True)
                        mm.then_inc(st_mm, 1)

                def prep_y(u):
                    tt, g, st = u // 2, u % 2, u % 2
                    if u < 2:
                        if u == 0:
                            pe.wait_ge(tk_ready, 9)
                            pe.wait_ge(p_ready, NU)
                        else:
                            pe.wait_ge(h_set, 10)
                    else:
                        pe.wait_ge(e_ready, 2 * (u - 1))
                        pe.wait_ge(cb_set, 2 * (u - 1))
                    tk = slice(P * tt, P * tt + P)
                    pe.matmul((B6, B7)[st][:, 0:P], cv[:, 4 + g, tk], cv[:, 6 + g, tk], start=True, stop=True)
                    for d in range(2):
                        for hh_ in range(4):
                            col = 8 * d + 4 * g + hh_
                            mm = pe.matmul(G[st][:, 512 * d + P * hh_:512 * d + P * hh_ + P],
                                           dA[:, tt, col:col + 1].to_broadcast([P, P]), cst(("trif", "trib")[d]),
                                           start=True, stop=True)
                    mm.then_inc(r_mm, 1)

                def y(u):
                    tt, g, st = u // 2, u % 2, u % 2
                    pe.wait_ge(m_ready, 2 * (u + 1))
                    pe.wait_ge(xdt_ready, 4 * (u + 1))
                    if u == 0:
                        pe.wait_ge(tm_set, 1)
                        pe.wait_ge(dend_set, 2)
                        pe.wait_ge(h_set, 10)
                    if g == 0 and tt >= 2:
                        pe.wait_ge(y_read, tt - 1)
                    for hh_ in range(4):
                        h = 4 * g + hh_
                        o = NP[64 * (h % 2):64 * (h % 2) + 64, 512 * (tt % 2) + P * (h // 2):512 * (tt % 2) + P * (h // 2) + P]
                        terms = [(xdt[st][d][:, 64 * hh_:64 * hh_ + 64], sL[st][d]) for d in range(2)]
                        for d in range(2):
                            pos = (FWD_SEQ, BWD_SEQ)[d].index(tt)
                            if pos:
                                terms.append((hst[d][pos - 1][:, 64 * h:64 * h + 64], sE[st][d]))
                        for q, (lh, rh_) in enumerate(terms):
                            mm = pe.matmul(o, lh, rh_[:, P * hh_:P * hh_ + P], start=(q == 0), stop=(q == len(terms) - 1))
                    mm.then_inc(y_mm, 1)

                prep_y(0)
                for u in range(12):
                    if u + 1 < 12:
                        prep_y(u + 1)
                    y(u)
                pe.wait_ge(y_read, 6)
                for c in range(4):
                    pe.wait_ge(gsq_done, c + 1)
                    for a, e, _s in SEGS:
                        mm = pe.matmul(NP[:, a:e], cst("ones"), sqg[c % 2][:, a:e], start=(c == 0), stop=(c == 3))
                    mm.then_inc(gn_sum, 1)

            def ab_out_pe():
                def ready(k):
                    if k == 0:
                        pe.wait_ge(na_cat, 6)
                    if k >= 4:
                        pe.wait_ge(ssd_cat, k - 3)
                pe.wait_ge(e_ready, 24)
                gemm_pair(ABO, xh, xl, SEGS, ready)
                for c in range(2, AB_OUT_T):
                    gemm(ABO + c, c % 2, (ABO + c) // 2, KC, xh, xl, SEGS)

            def ab_pe():
                norm(1, SEGS, AB)
                ab_in_pe()
                na_pe()
                ssd_pe()
                ab_out_pe()

            def cd_in_pe():
                for c in range(CD_IN_T):
                    if c == 0:
                        gemm_pair(CD, xh, xl, SEGS, lambda k: pe.wait_ge(xn_ready, 32 + k + 1))
                    if c >= 2:
                        gemm(CD + c, c % 2, (CD + c) // 2, KC, xh, xl, LSEG if 8 <= c < 12 or c >= 16 else SEGS)
                    if 4 <= c < 7:
                        for tt in (2 * c - 8, 2 * c - 7):
                            if tt >= 2:
                                pe.wait_ge(v2_ready, tt - 1)
                            if tt == 0:
                                for s in range(2):
                                    pe.wait_ge(psum_free[s], (CD + 4) // 2)
                            for q in range(4):
                                mm = pe.transpose((B6, B7)[tt % 2][:, P * q:P * q + P], vT2[:, q, P * tt:P * tt + P],
                                                  cst("ident"))
                            mm.then_inc(v2_done, 1)
                    i = c - 5
                    if 0 <= i < 8:
                        pe.wait_ge(kq_ln, 8 + i)
                        if i < 4:
                            pe.wait_ge(sql_set, 8 + i + 1)
                            for a, e, _s in SEGS:
                                pe.matmul(NP[:, a:e], blkr[:], sqh[:, a:e], start=True, stop=False)
                                mm = pe.matmul(NP[:, a:e], blkr[:], sql[:, a:e], start=False, stop=True)
                        else:
                            pe.wait_ge(kq_sq, 16 + 4 + i + 1)
                            mm = pe.matmul(NP[:, 0:NLAT], cst("blk"), sq[i % 2][:, 0:NLAT], start=True, stop=True)
                        mm.then_inc(kq_sum, 1)
                    i = c - 7
                    if 0 <= i < 8:
                        pe.wait_ge(kq_done, 8 + i + 1)
                        if i < 2:
                            pe.wait_ge(v2_ready, 6)
                        else:
                            pe.wait_ge(t2_set, i - 1)
                        src = k2[:, i, 0:NLAT] if i < 4 else q2[:, i - 4, :]
                        pe.matmul((B6, B7)[i % 2], cst("swap"), src, start=True, stop=True).then_inc(rope_mm, 1)

            def cd_mid_pe():
                for s in range(2):
                    pe.wait_ge(psum_free[s], CDO // 2)
                pe.wait_ge(lruw_landed, 16)
                pe.wait_ge(rope_done, 8)

                def gates(p_):
                    if p_:
                        pe.wait_ge(p2_ready, 8 * p_)
                    else:
                        pe.wait_ge(cv_ready, 12)
                    for d in range(2):
                        for g in range(2):
                            if d:
                                pe.wait_ge(gate_sig, 4 * p_ + 1 + g)
                            for a, e, _s in SEGS:
                                mm = pe.matmul(G[g][:, a:e], lruw[:, 8 * g + 4 * d + p_, :], xc[:, p_, a:e],
                                               start=True, stop=True)
                            mm.then_inc(gate_mm, 1)

                def scores(a):
                    qt, h = a // 4, a % 4
                    for s in range(2):
                        if a % 4 == 0:
                            pe.wait_ge(gate_sig, 4 * (a // 4) + 3 + s)
                        else:
                            pe.wait_ge(p2_ready, 2 * a + s - 1)
                        hp = slice(64 * s, 64 * s + 64)
                        for b_, e, _s in SEGS:
                            mm = pe.matmul(G[s][:, b_:e], q2[hp, h, P * qt:P * qt + P], k2[hp, h, b_:e], start=True, stop=True)
                        mm.then_inc(s2_done, 1)

                def turn(a):
                    pe.wait_ge(w_done, a + 1)
                    if a:
                        pe.wait_ge(wt_ready, a)
                    for k in range(NT):
                        mm = pe.transpose(NP[:, P * k:P * k + P], wb[a % 2][:, P * k:P * k + P], cst("ident"))
                    mm.then_inc(tr2_done, 1)

                def values(a):
                    pe.wait_ge(wt_ready, a + 1)
                    if a >= 2:
                        pe.wait_ge(on_done, a - 1)
                    h = a % 4
                    for k in range(NT):
                        mm = pe.matmul((B6, B7)[a % 2][:, 0:P], wtb[a % 2][:, P * k:P * k + P],
                                       vtok[:, k, P * h:P * h + P], start=(k == 0), stop=(k == NT - 1))
                    mm.then_inc(pv2_done, 1)

                for what, i in SCHED:
                    if what == "gates":
                        gates(i)
                    if what == "att":
                        if i < NA2:
                            scores(i)
                        if 2 <= i <= NA2 + 1:
                            turn(i - 2)
                        if 3 <= i <= NA2 + 2:
                            values(i - 3)
                for qt in range(4):
                    pe.wait_ge(onr_done, qt + 1)
                    if qt >= 2:
                        pe.wait_ge(ov_ready, qt - 1)
                    for h in range(4):
                        mm = pe.transpose((B6, B7)[qt % 2][:, P * h:P * h + P], onq[qt][:, P * h:P * h + P], cst("ident"))
                    mm.then_inc(oq_done, 1)

            def cd_out_pe():
                def ready(k):
                    if k == 0:
                        pe.wait_ge(cd_cat, 4)
                    if k == 4:
                        pe.wait_ge(cd_cat2, 4)
                gemm_pair(CDO, xh, xl, LSEG, ready)
                for c in range(2, CD_OUT_T):
                    gemm(CDO + c, c % 2, (CDO + c) // 2, KC, xh, xl, LSEG)

            def cd_pe():
                cd_in_pe()
                cd_mid_pe()
                cd_out_pe()

            pe.wait_ge(sc_ready, 1)
            for j in PE_MINI:
                if j == 11:
                    pe.wait_ge(con_landed, 16)
                    norm(0, SEGS)
                pe.wait_ge(mini_landed[group(j)], 16 * len(MINI_GROUPS[group(j)]))
                for k in range(KC):
                    mm = pe.matmul(G[0][:, 2 * j:2 * j + 2], mini[j][:, k * P:(k + 1) * P], sc[:, k, :],
                                   start=(k == 0), stop=(k == KC - 1))
            mm.then_inc(mini_mm, 1)
            ffn(0, 0, BASE["ffn0"], SEGS)
            ab_pe()
            norm(2, SEGS, BASE["ffn1"])
            ffn(1, 2, BASE["ffn1"], SEGS)
            norm(3, SEGS, BASE["ffn2"])
            ffn(2, 3, BASE["ffn2"], SEGS)
            norm(4, SEGS, CD)
            cd_pe()
            norm(5, LSEG, BASE["ffn3"])
            ffn(3, 5, BASE["ffn3"], LSEG)

        def cat_view(buf, gi):
            if gi < 4:
                return buf[:, 0:4, 0:NLAT].rearrange("p c (r w) -> p c r w", w=GRID_W)[:, :, :, 16 * gi:16 * gi + 16]
            return buf[:, 0:4, NLAT + P * (gi - 4):NLAT + P * (gi - 3)]

        @block.scalar
        def _(act):
            def split_hi(t, slot, n, nk):
                act.wait_ge(raw_landed[slot], n * 16 + 16)
                if not (isinstance(t, int) and t < 2):
                    act.wait_ge(mm_done, t - 1)
                act.activation(wh[slot][:, 0:nk * P], raw[slot][:, 0:nk * P], ACT.Copy).then_inc(hi_done, 1)

            def load_mods(it):
                if not (isinstance(it, int) and it == 0):
                    act.wait_ge(mod_sum, it * 3)
                act.dma_start(mraw[:], dr["wmn"][bass.ds(it * 3 + 24, 3)].rearrange("t p n -> p t n")
                              ).then_inc(mod_landed, 16)

            def sum_mods(it):
                for j in range(3):
                    act.wait_ge(mod_prod, it * 3 + (j + 1))
                    if j == 0 and not (isinstance(it, int) and it == 0):
                        act.wait_ge(mod_set, it)
                    act.activation(mraw[:, j, :], mraw[:, j, :], ACT.Copy, accum_out=mcol[:, j, 1:2]
                                   ).then_inc(mod_sum, 1)

            def load_scb(n):
                act.dma_start(scb[:], dr["ccb"]).then_inc(scb_landed, 16)
                act.wait_ge(scb_landed, 16 * n)
                act.activation(scb[:], scb[:], ACT.Silu).then_inc(scb_ready, 1)

            def up(b, hb, look, mods, ns):
                def pair(i, nk, mods=None, more=False):
                    split_hi(i * 2 + (b + 2), 0, i + (b // 2 + 1), nk)
                    act.wait_ge(mm_done, i * 2 + (b + 1))
                    if not (isinstance(i, int) and i == 0 and b == 0):
                        act.wait_ge(psum_free[1], i + b // 2)
                    act.activation(g1s[:, 0:ns], G[0][:, 0:ns], ACT.Silu).then_inc(psum_free[0], 1)
                    split_hi(i * 2 + (b + 3), 1, i + (b // 2 + 1), nk)
                    act.wait_ge(psum_free[1], i + (b // 2 + 1))
                    act.activation(hh[:, bass.ds(i, 1), 0:ns].rearrange("p a n -> p (a n)"), hf[:, 0:ns],
                                   ACT.Copy).then_inc(h_hi, 1)
                    if mods is not None:
                        sum_mods(i + mods)
                        if more:
                            load_mods(i + (mods + 1))

                last = mods is not None and mods + FH - 1 in (20, 40)
                if b == 0:
                    pair(0, KC, mods, True)
                with act.Fori(int(b == 0), FH - 1 - last) as i:
                    pair(i, KC, mods, True)
                if last:
                    pair(FH - 2, KC, mods, False)
                pair(FH - 1, look)

            def square(j, n, chunk, ns):
                if j >= 2:
                    act.wait_ge(ssq_acc, 7 * n + j - 1)
                elif n and j == 0:
                    act.wait_ge(ssq_acc, 7 * n)
                elif n:
                    act.wait_ge(norm_sum, n)
                act.activation(sq[j % 2][:, 0:ns], chunk, ACT.Square).then_inc(sq_done, 1)

            def down(d, look, same, n_sq, ns):
                for i in range(DOWN // 2):
                    for s in range(2):
                        nk = look if i == DOWN // 2 - 1 else same
                        if nk:
                            split_hi(d + 2 * i + s + 2, s, (d + 2 * i + s + 2) // 2, nk)
                        if n_sq is not None:
                            act.wait_ge(psum_free[s], (d + 2 * i + s) // 2 + 1)
                            square(2 * i + s, n_sq, x[:, 2 * i + s, 0:ns], ns)

            def norm(n, ns):
                act.wait_ge(norm_sum, n + 1)
                act.activation(sq[0][:, 0:ns], NP[:, 0:ns], ACT.Ln, bias=eps[:, 0:1], scale=1.0 / D
                               ).then_inc(norm_ln, 1)
                act.wait_ge(norm_ln, n + 1)
                act.activation(rstd[:, 0:ns], sq[0][:, 0:ns], ACT.Exp, scale=-0.5).then_inc(rstd_ready, 1)
                for j in range(KC):
                    act.wait_ge(aff_done, 8 * n + j + 1)
                    act.activation(xh[:, j, 0:ns], yn[j % 2][:, 0:ns], ACT.Copy).then_inc(xn_hi, 1)

            def ffn(f, base, look, n_sq, mods, ns, ns_sq):
                for h in range(2):
                    b = base + h * (UP + DOWN)
                    up(b, (2 * f + h) * FH, FH, None if mods is None else mods + 10 * h, ns)
                    if h == 0:
                        down(b + UP, KC, FH, None, ns)
                    else:
                        down(b + UP, look, FH, n_sq, ns_sq)

            def ab_in_act():
                def rs(i):
                    act.wait_ge(kq_sum, i + 1)
                    if i:
                        act.wait_ge(kq_rs, i)
                    act.activation(ssq[:], NP[:, 0:T], ACT.Ln, bias=eps[:, 0:1], scale=1.0 / HD).then_inc(kq_ln, 1)
                    act.wait_ge(kq_ln, i + 1)
                    if i:
                        act.wait_ge(kq_done, i)
                    act.activation(rstd[:], ssq[:], ACT.Exp, scale=-0.5).then_inc(kq_rs, 1)

                def silu_conv(i):
                    act.wait_ge(conv_done, i + 1)
                    for a, e, o in ((0, NLAT, 0), (NLAT, T, 3)):
                        ins = act.activation(cv[:, i, a:e], cb[i % 2][:, a + o:e + o], ACT.Silu,
                                             bias=pr("scb")[:, i:i + 1])
                    ins.then_inc(cv_ready, 1)

                for c in range(AB_IN_T):
                    t, s = AB + c, c % 2
                    split_hi(t + 2, s, (t + 2) // 2, KC)
                    if c == 3:
                        act.wait_ge(wdt_landed, 16)
                        act.activation(wdh[:], wdt[:], ACT.Copy).then_inc(wdt_hi, 1)
                        act.activation(ea[:, 0, :], pr("alog"), ACT.Exp).then_inc(dt_exp, 1)
                    if 4 <= c < 12:
                        i = c - 4
                        act.wait_ge(psum_free[s], t // 2 + 1)
                        if i >= 2:
                            act.wait_ge(kq_sum, i - 1)
                        act.activation(sq[i % 2][:], kq[:, i, :], ACT.Square).then_inc(kq_sq, 1)
                        if i == 0:
                            act.activation(blkr[:], cst("blk"), ACT.Copy)
                        if i:
                            rs(i - 1)
                        act.wait_ge(kq_sq, 2 * i + 1)
                        act.activation(sqh[:], sq[i % 2][:], ACT.Copy).then_inc(kq_sq, 1)
                    if c == 12:
                        rs(7)
                        act.wait_ge(pad_zero, 1)
                    if 12 <= c < 20:
                        i = c - 12
                        act.wait_ge(mm_done, t + 1)
                        if i >= 2:
                            act.wait_ge(conv_done, i - 1)
                        act.activation(pad[i % 2][:, 2:2 + NLAT], G[s][:, 0:NLAT], ACT.Copy)
                        act.activation(pad[i % 2][:, 517:517 + NCTX], G[s][:, NLAT:T], ACT.Copy).then_inc(psum_free[s], 1)
                        if i:
                            silu_conv(i - 1)
                    if c == 14:
                        act.wait_ge(dt_abs, 1)
                        act.activation(dte[:], dtu[:], ACT.Exp, scale=-1.0).then_inc(dt_exp, 1)
                    if c == 20:
                        silu_conv(7)
                    if c >= 20:
                        act.wait_ge(mm_done, t + 1)
                        act.activation(zs[:, c - 20, :], G[s][:, 0:T], ACT.Silu).then_inc(psum_free[s], 1)

            def na_act():
                for g in range(10):
                    act.wait_ge(vt_done, g + 1)
                    act.activation(vtile(g), (B6, B7)[g % 2], ACT.Copy).then_inc(vs_ready, 1)

                def expo(u):
                    act.wait_ge(nmax_ready, u + 1)
                    if u >= 2:
                        act.wait_ge(tr_done, u - 1)
                    st = nst[:, u % 4, :]
                    if u < 32:
                        act.activation(nsP[u % 2][:], nsS[u % 2][:], ACT.Exp, bias=st[:, 0:1], accum_out=st[:, 2:3]
                                       ).then_inc(p_ready, 1)
                    else:
                        for w_ in range(2):
                            r = slice(256 * w_, 256 * w_ + 256)
                            ins = act.activation(nsP[u % 2][:, r], G[0][:, 512 * (u % 2) + 256 * w_:512 * (u % 2) + 256 * w_ + 256],
                                                 ACT.Exp, bias=st[:, w_:w_ + 1], accum_out=st[:, 2 + w_:3 + w_])
                        ins.then_inc(p_ready, 1)

                def copy_pt(u):
                    act.wait_ge(tr_done, u + 1)
                    if u >= 2:
                        act.wait_ge(pv_done, u - 1)
                    act.activation(nsT[u % 2][:], G[1][:, 512 * (u % 2):512 * (u % 2) + 512], ACT.Copy).then_inc(pt_ready, 1)

                def out_hi(gi):
                    act.wait_ge(ot_done, gi + 1)
                    src = (B6, B7)[gi % 2].rearrange("p (c t) -> p c t", c=4)
                    act.activation(cat_view(xh, gi), src if gi >= 4 else src.rearrange("p c (r w) -> p c r w", w=16),
                                   ACT.Copy).then_inc(cat_hi, 1)

                for it in range(NU + 4):
                    if it < NU:
                        expo(it)
                    if 0 <= it - 2 < NU:
                        copy_pt(it - 2)
                    if it >= 12 and (it - 12) % 8 == 0 and (it - 12) // 8 < 4:
                        out_hi((it - 12) // 8)
                out_hi(4)
                out_hi(5)

            def ssd_act():
                for q in range(9):
                    act.wait_ge(tk_done, q + 1)
                    dst = xst[:, q, :] if q < 6 else bst[:, 2 * (q - 6):2 * (q - 6) + 2, :].rearrange("p t c -> p (t c)")
                    act.activation(dst, (B6, B7)[q % 2], ACT.Copy).then_inc(tk_ready, 1)
                act.wait_ge(tm_set, 1)
                act.activation(dend[:], tm[:], ACT.Exp).then_inc(dend_set, 1)
                act.activation(cdec[:].rearrange("p t c -> p (t c)"), NP[:, 512:608], ACT.Exp).then_inc(dend_set, 1)
                for u in range(12):
                    st = u % 2
                    if u >= 2:
                        act.wait_ge(y_mm, u - 1)
                    for d in range(2):
                        act.wait_ge(d_ready, 8 * u + 4 * (d + 1))
                        act.activation(sE[st][d][:], G[st][:, 512 * d:512 * d + 512], ACT.Exp).then_inc(e_ready, 1)
                    for d in range(2):
                        act.activation(sL[st][d][:], sL[st][d][:], ACT.Exp).then_inc(l_ready, 1)
                for c in range(4):
                    if c == 0:
                        act.wait_ge(gz_done, 6)
                    if c >= 2:
                        act.wait_ge(gn_sum, c - 1)
                    act.activation(sqg[c % 2][:], gy[:, c, :], ACT.Square).then_inc(gsq_done, 1)
                act.wait_ge(gn_sum, 4)
                act.activation(lng[:], NP[:, 0:T], ACT.Ln, bias=eps[:, 0:1], scale=1.0 / 512).then_inc(gn_ln, 1)
                act.wait_ge(gn_ln, 1)
                act.activation(rsg[:], lng[:], ACT.Exp, scale=-0.5).then_inc(gn_rs, 1)
                for c in range(4):
                    act.wait_ge(vg_ready, c + 1)
                    act.activation(xh[:, 4 + c, :], vg[c % 2][:], ACT.Copy).then_inc(gcat_hi, 1)

            def cd_in_act():
                def rs(i):
                    ns = T if i < 4 else NLAT
                    act.wait_ge(kq_sum, 8 + i + 1)
                    act.wait_ge(kq_rs, 8 + i)
                    act.activation(ssq[:, 0:ns], NP[:, 0:ns], ACT.Ln, bias=eps[:, 0:1], scale=1.0 / HD).then_inc(kq_ln, 1)
                    act.wait_ge(kq_ln, 8 + i + 1)
                    act.wait_ge(kq_done, 8 + i)
                    act.activation(rstd[:, 0:ns], ssq[:, 0:ns], ACT.Exp, scale=-0.5).then_inc(kq_rs, 1)

                def add_bias(i):
                    act.wait_ge(conv_done, 8 + i + 1)
                    for a, e, o in ((0, NLAT, 0), (NLAT, T, 3)):
                        ins = act.activation(xc[:, i, a:e], cb[i % 2][:, a + o:e + o], ACT.Identity,
                                             bias=pr("lcb")[:, i:i + 1])
                    ins.then_inc(cv_ready, 1)

                for c in range(CD_IN_T):
                    t, s = CD + c, c % 2
                    split_hi(t + 2, s, (t + 2) // 2, KC)
                    if c == 2:
                        act.wait_ge(dl_set, 1)
                        act.activation(coef[:, 1, :], coef[:, 0, :], ACT.Exp, scale=-1.0).then_inc(coef_exp, 1)
                        act.wait_ge(dl_set, 3)
                        act.activation(dl[:, 2:4], dl[:, 0:2], ACT.Exp).then_inc(dl_exp, 1)
                    if 4 <= c < 7:
                        for tt in (2 * c - 8, 2 * c - 7):
                            act.wait_ge(v2_done, tt + 1)
                            act.activation(vtok[:, tt, :], (B6, B7)[tt % 2], ACT.Copy).then_inc(v2_ready, 1)
                    if 4 <= c < 12:
                        i = c - 4
                        act.wait_ge(psum_free[s], t // 2 + 1)
                        if i >= 2:
                            act.wait_ge(kq_sum, 8 + i - 1)
                        if i < 4:
                            act.activation(sq[i % 2][:], k2[:, i, :], ACT.Square).then_inc(kq_sq, 1)
                        else:
                            act.activation(sq[i % 2][:, 0:NLAT], q2[:, i - 4, :], ACT.Square).then_inc(kq_sq, 1)
                        if i:
                            rs(i - 1)
                        if i < 4:
                            act.wait_ge(kq_sq, 16 + 2 * i + 1)
                            act.activation(sqh[:], sq[i % 2][:], ACT.Copy).then_inc(kq_sq, 1)
                    if c == 12:
                        rs(7)
                        act.wait_ge(pad_zero, 2)
                    if 12 <= c < 16:
                        i = c - 12
                        act.wait_ge(mm_done, t + 1)
                        if i >= 2:
                            act.wait_ge(conv_done, 8 + i - 1)
                        act.activation(pad[i % 2][:, 2:2 + NLAT], G[s][:, 0:NLAT], ACT.Copy)
                        act.activation(pad[i % 2][:, 517:517 + NCTX], G[s][:, NLAT:T], ACT.Copy).then_inc(psum_free[s], 1)
                        if i:
                            add_bias(i - 1)
                    if c == 16:
                        add_bias(3)
                    if c >= 16:
                        act.wait_ge(mm_done, t + 1)
                        act.activation(gate[:, c - 16, :], G[s][:, 0:NLAT], ACT.Gelu_apprx_tanh).then_inc(psum_free[s], 1)

            def cd_mid_act():
                act.wait_ge(coef_set, 1)

                def gates(p_):
                    for d in range(2):
                        for g, (dst, bias) in enumerate(((lR, "lba"), (lI, "lbx"))):
                            act.wait_ge(gate_mm, 4 * p_ + 2 * d + g + 1)
                            if p_:
                                act.wait_ge(lru_h, p_)
                            act.activation(dst[d][:], G[g][:, 0:T], ACT.Sigmoid, bias=pr(bias)[:, 4 * d + p_:4 * d + p_ + 1]
                                           ).then_inc(gate_sig, 1)

                def decay(p_):
                    for d in range(2):
                        e = 4 * d + p_
                        act.wait_ge(gate_sig, 4 * p_ + 2 * d + 1)
                        act.activation(lA[d][:], lR[d][:], ACT.Exp, scale=coef[:, 6, e:e + 1]).then_inc(lru_a, 1)
                        act.wait_ge(lru_a, 2 * p_ + d + 1)
                        act.activation(lR[d][:], lR[d][:], ACT.Tanh, scale=coef[:, 7, e:e + 1]).then_inc(lru_t, 1)

                def root(p_):
                    for d in range(2):
                        act.wait_ge(lru_m, 2 * p_ + d + 1)
                        act.activation(lR[d][:], lR[d][:], ACT.Sqrt).then_inc(lru_q, 1)

                def hi(p_):
                    act.wait_ge(lru_o, p_ + 1)
                    act.activation(xh[:, p_, 0:NLAT], hsum[:, p_, :], ACT.Copy).then_inc(lru_hi, 1)

                def att(a):
                    if a < NA2:
                        for s in range(2):
                            act.wait_ge(max2_ready, 2 * a + s + 1)
                            if a >= 2:
                                act.wait_ge(w_done, a - 1)
                            act.activation(pb[a % 2][s][:], G[s][:, 0:T], ACT.Exp, bias=st2[:, a % 4, s:s + 1],
                                           accum_out=st2[:, a % 4, 2 + s:3 + s]).then_inc(p2_ready, 1)
                    if 2 <= a <= NA2 + 1:
                        act.wait_ge(tr2_done, a - 1)
                        if a >= 4:
                            act.wait_ge(pv2_done, a - 3)
                        act.activation(wtb[a % 2][:], NP[:, 0:T], ACT.Copy).then_inc(wt_ready, 1)
                    if a >= 4:
                        b = a - 4
                        act.wait_ge(on_done, b + 1)
                        if b:
                            act.wait_ge(ss_ready, b)
                        act.activation(junk[:], onq[b // 4][:, P * (b % 4):P * (b % 4) + P], ACT.Square,
                                       accum_out=hsq[:, 0, b:b + 1]).then_inc(ss_ready, 1)

                for what, i in SCHED:
                    if what == "gates":
                        gates(i)
                    if what == "decay":
                        decay(i)
                    if what == "root":
                        root(i)
                    if what == "hi":
                        hi(i)
                    if what == "att":
                        att(i)
                act.wait_ge(ss_ready, NA2)
                act.activation(hsq[:, 1, :], hsq[:, 0, :], ACT.Ln, bias=eps[:, 0:1], scale=1.0 / P).then_inc(ss_ln, 1)
                act.wait_ge(ss_ln, 1)
                act.activation(hrs[:], hsq[:, 1, :], ACT.Exp, scale=-0.5).then_inc(rr_ready, 1)
                for qt in range(4):
                    act.wait_ge(ov_ready, qt + 1)
                    act.activation(xh[:, 4:8, P * qt:P * qt + P], ovb[qt % 2][:].rearrange("p (h t) -> p h t", h=4), ACT.Copy
                                   ).then_inc(oq_hi, 1)

            act.wait_ge(scb0_landed, 16)
            act.activation(scb0[:], scb0[:], ACT.Silu).then_inc(scb0_ready, 1)
            act.wait_ge(par_landed, 16)
            act.activation(sc[:].rearrange("p k s -> p (k s)"), pr("cc"), ACT.Silu).then_inc(sc_ready, 1)
            act.wait_ge(x_landed, 16)
            for j in range(KC):
                square(j, 0, x[:, j, :], T)
            split_hi(0, 0, 0, KC)
            split_hi(1, 1, 0, KC)
            act.wait_ge(eps_set, 1)
            norm(0, T)
            load_mods(0)
            load_scb(1)
            ffn(0, BASE["ffn0"], KC, 1, 0, T, T)
            norm(1, T)
            ab_in_act()
            na_act()
            ssd_act()
            down(ABO, KC, KC, 2, T)
            norm(2, T)
            load_mods(20)
            load_scb(2)
            ffn(1, BASE["ffn1"], KC, 3, 20, T, T)
            norm(3, T)
            ffn(2, BASE["ffn2"], KC, 4, None, T, T)
            norm(4, T)
            cd_in_act()
            cd_mid_act()
            down(CDO, KC, KC, 5, NLAT)
            norm(5, NLAT)
            ffn(3, BASE["ffn3"], 0, None, None, NLAT, NLAT)

        @block.vector
        def _(dve):
            chained = [0]

            def chain(ins):
                chained[0] += 1
                ins.then_inc(dve_chain, 1)
                dve.wait_ge(dve_chain, chained[0])

            def split_lo(t, slot, nk):
                dve.wait_ge(hi_done, t + 1)
                dve.tensor_tensor(wl[slot][:, 0:nk * P], raw[slot][:, 0:nk * P],
                                  wh[slot][:, 0:nk * P].bitcast(F32), ALU.subtract).then_inc(lo_done, 1)

            def dot(tile, s, scv, out):
                return dve.scalar_tensor_tensor(B67[:], tile, 1.0, scv[:, s, :], ALU.mult, ALU.mult, accum_out=out)

            def dot_mods(it, mods_first):
                dve.wait_ge(mod_landed, it * 16 + 16)
                dve.wait_ge(scb_ready, 1 if mods_first else 2)
                if not (isinstance(it, int) and it == 0):
                    dve.wait_ge(mod_set, it)
                for j in range(3):
                    if j or not (isinstance(it, int) and it == 0):
                        dve.wait_ge(mod_dot, it * 3 + j)
                    dot(mraw[:, j, :], 0, scb, mcol[:, j, 0:1]).then_inc(mod_dot, 1)

            def set_mods(it):
                dve.wait_ge(mod_sum, it * 3 + 3)
                c0 = it * 3 + 24
                dve.tensor_tensor(M[:, bass.ds(c0, 3), :], mcol[:],
                                  pr("bmod")[:, bass.ds(c0, 3)].unsqueeze(2).to_broadcast([P, 3, 2]),
                                  ALU.add).then_inc(mod_set, 1)

            def up(b, hb, look, mods, ns):
                def pair(i, nk):
                    split_lo(i * 2 + (b + 2), 0, nk)
                    if mods is not None and nk == KC:
                        dot_mods(i + mods, mods < 20)
                    dve.wait_ge(mm_done, i * 2 + (b + 2))
                    dve.wait_ge(psum_free[0], i + (b // 2 + 1))
                    if not (isinstance(i, int) and i == 0 and hb == 0):
                        dve.wait_ge(h_ready, i + hb)
                    dve.tensor_tensor(hf[:, 0:ns], g1s[:, 0:ns], G[1][:, 0:ns], ALU.mult).then_inc(psum_free[1], 1)
                    split_lo(i * 2 + (b + 3), 1, nk)
                    dve.wait_ge(h_hi, i + (hb + 1))
                    hs = [t_[:, bass.ds(i, 1), 0:ns].rearrange("p a n -> p (a n)") for t_ in (hl, hh)]
                    dve.tensor_tensor(hs[0], hf[:, 0:ns], hs[1].bitcast(F32), ALU.subtract).then_inc(h_ready, 1)
                    if mods is not None and nk == KC:
                        set_mods(i + mods)

                if b == 0:
                    for i in range(4):
                        pair(i, KC)
                        gate_dots(i)
                with dve.Fori(4 * (b == 0), FH - 1) as i:
                    pair(i, KC)
                pair(FH - 1, look)

            def down(d, look, same, n, segs):
                for i in range(DOWN // 2):
                    for s in range(2):
                        t = d + 2 * i + s
                        dve.wait_ge(mm_done, t + 1)
                        for a, b, c in segs:
                            j = 2 * i + s
                            ins = dve.scalar_tensor_tensor(x[:, j, a:b], G[s][:, a:b], modG[:, n, j, c:c + 1],
                                                           x[:, j, a:b], ALU.mult, ALU.add)
                        ins.then_inc(psum_free[s], 1)
                        nk = look if i == DOWN // 2 - 1 else same
                        if nk:
                            split_lo(t + 2, s, nk)

            def prep(n, it):
                dve.wait_ge(mod_set, it)
                c0 = (n // 3) * NMT + 3 * KC * (n % 3)
                g = pr("normg")[:, 8 * n:8 * n + 8].unsqueeze(2).to_broadcast([P, KC, 2])
                dve.scalar_tensor_tensor(modA[:, n], M[:, c0 + KC:c0 + 2 * KC, :], 1.0, g, ALU.add, ALU.mult
                                         ).then_inc(prep_done, 1)
                if n:
                    gate_of(n)
                    dve.wait_ge(gate_prep, n + 1)
                dve.wait_ge(prep_done, n + 1)

            def gate_of(n):
                c0 = (n // 3) * NMT + 3 * KC * (n % 3)
                dve.tensor_scalar(modG[:, n], M[:, c0 + 2 * KC:c0 + 3 * KC, :], 1.0 if n % 3 == 1 else 0.5, None,
                                  ALU.mult).then_inc(gate_prep, 1)

            def gate_dots(i):
                n0 = 2 * len(DVE_MINI)
                if i == 0:
                    dve.wait_ge(gmini_landed, 32)
                dve.wait_ge(mod_dot, 3 * (i + 1))
                for q in (2 * i, 2 * i + 1):
                    for s in range(2):
                        dve.wait_ge(mini_dot, n0 + 2 * q + s)
                        dot(gmini[q // 4][:, q % 4, :], s, scb, M[:, 16 + q, s:s + 1]).then_inc(mini_dot, 1)
                dve.wait_ge(mini_dot, n0 + 4 * i + 4)
                if i == 3:
                    dve.tensor_tensor(M[:, 16:24, :], M[:, 16:24, :], pr("bmod")[:, 16:24].unsqueeze(2).to_broadcast([P, KC, 2]),
                                      ALU.add).then_inc(mini_set, 1)
                    dve.wait_ge(mini_set, 4)
                    gate_of(0)
                    dve.wait_ge(gate_prep, 1)

            def norm(n, segs):
                ns = segs[-1][1]
                c0 = (n // 3) * NMT + 3 * KC * (n % 3)

                def rest(j):
                    dve.wait_ge(xn_hi, 8 * n + j + 1)
                    dve.tensor_tensor(xl[:, j, 0:ns], yn[j % 2][:, 0:ns], xh[:, j, 0:ns].bitcast(F32),
                                      ALU.subtract).then_inc(xn_ready, 1)

                dve.wait_ge(rstd_ready, n + 1)
                chain(dve.tensor_tensor(vn[0][:, 0:ns], x[:, 0, 0:ns], rstd[:, 0:ns], ALU.mult))
                for j in range(KC):
                    if j:
                        dve.wait_ge(v_ready, 7 * n + j)
                    if j >= 2:
                        dve.wait_ge(xn_ready, 8 * n + j - 1)
                    for a, b, c in segs:
                        ins = dve.tensor_scalar(yn[j % 2][:, a:b], vn[j % 2][:, a:b], modA[:, n, j, c:c + 1],
                                                M[:, c0 + j, c:c + 1], ALU.mult, ALU.add)
                    ins.then_inc(aff_done, 1)
                    if j >= 1:
                        rest(j - 1)
                rest(KC - 1)

            def ffn(f, n, base, look, mods, segs):
                for h in range(2):
                    b = base + h * (UP + DOWN)
                    up(b, (2 * f + h) * FH, FH, None if mods is None else mods + 10 * h, segs[-1][1])
                    down(b + UP, KC if h == 0 else look, FH, n, segs)

            def log1p_exp(e, den, s_, s2, p_):
                chain(dve.tensor_scalar(den, e, 2.0, None, ALU.add))
                chain(dve.reciprocal(den, den))
                chain(dve.tensor_tensor(s_, e, den, ALU.mult))
                chain(dve.tensor_tensor(s2, s_, s_, ALU.mult))
                chain(dve.tensor_scalar(p_, s2, 1.0 / 19, None, ALU.mult))
                for q in (17, 15, 13, 11, 9, 7, 5, 3):
                    chain(dve.scalar_tensor_tensor(p_, p_, 1.0 / q, s2, ALU.add, ALU.mult))
                chain(dve.scalar_tensor_tensor(p_, p_, 1.0, s_, ALU.add, ALU.mult))

            def ab_in_dve():
                dve.wait_ge(con_landed, 16)
                chain(dve.tensor_scalar(qg8[:, 1:2], pr("naqg"), HD ** -0.5, None, ALU.mult))
                chain(dve.tensor_copy(qg8[:, 0:1], pr("nakg")))

                def kq_norm(i):
                    dve.wait_ge(kq_rs, i + 1)
                    dve.scalar_tensor_tensor(kq[:, i, :], kq[:, i, :], qg8[:, i // 4:i // 4 + 1], rstd[:],
                                             ALU.mult, ALU.mult).then_inc(kq_done, 1)

                def conv(i):
                    t = AB + 12 + i
                    dve.wait_ge(psum_free[i % 2], t // 2 + 1)
                    if i >= 2:
                        dve.wait_ge(cv_ready, i - 1)
                    src, dst = pad[i % 2], cb[i % 2]
                    for k in range(4):
                        tap = pr("scw")[:, 4 * i + k:4 * i + k + 1]
                        if k == 0:
                            ins = dve.tensor_scalar(dst[:], src[:, 0:771], tap, None, ALU.mult)
                        else:
                            ins = dve.scalar_tensor_tensor(dst[:], src[:, k:k + 771], tap, dst[:], ALU.mult, ALU.add)
                        if k < 3:
                            ins.then_inc(conv_tap, 1)
                            dve.wait_ge(conv_tap, 3 * i + k + 1)
                    ins.then_inc(conv_done, 1)

                for c in range(AB_IN_T):
                    t, s = AB + c, c % 2
                    if c == 11:
                        dve.wait_ge(dt_mm, 1)
                        dve.tensor_copy(dtT[:], B67[0:16, 0:T]).then_inc(dt_copied, 1)
                    if 5 <= c < 13:
                        i = c - 5
                        dve.wait_ge(kq_sq, 2 * i + 2)
                        dve.tensor_tensor(sql[:], sq[i % 2][:], sqh[:].bitcast(F32), ALU.subtract).then_inc(sql_set, 1)
                    if c < 12:
                        dve.wait_ge(mm_done, t + 1)
                        dst = vT[:, c, :] if c < 4 else kq[:, c - 4, :]
                        if c < 8:
                            dve.tensor_copy(dst, G[s][:, 0:T]).then_inc(psum_free[s], 1)
                        else:
                            dve.tensor_copy(dst[:, 0:NLAT].rearrange("p (n r c) -> p n r c", n=4, c=16),
                                            G[s][:, 0:NLAT].rearrange("p (r n c) -> p n r c", n=4, c=16))
                            dve.tensor_copy(dst[:, NLAT:T], G[s][:, NLAT:T]).then_inc(psum_free[s], 1)
                    split_lo(t + 2, s, KC)
                    if c == 3:
                        dve.wait_ge(wdt_hi, 1)
                        dve.tensor_tensor(wdl[:], wdt[:], wdh[:].bitcast(F32), ALU.subtract).then_inc(wdt_lo, 1)
                    if c == 4:
                        for s_ in range(2):
                            ins = dve.memset(pad[s_][:], 0.0)
                        ins.then_inc(pad_zero, 1)
                    if 5 <= c < 13:
                        kq_norm(c - 5)
                    if c == 12:
                        dve.wait_ge(dt_turned, 1)
                        bias = pr("dtb").unsqueeze(1).to_broadcast([P, NT, 16])
                        chain(dve.tensor_tensor(dt2[:], B6[:, 0:96].rearrange("p (t c) -> p t c", c=16), bias, ALU.add))
                        chain(dve.tensor_scalar(dtp[:], dt2[:], -1.0, None, ALU.mult))
                        dve.tensor_tensor(dtu[:], dt2[:], dtp[:], ALU.max).then_inc(dt_abs, 1)
                        chain(dve.tensor_scalar(dt[:], dt2[:], 0.0, None, ALU.max))
                    if 12 <= c < 20:
                        conv(c - 12)
                    if c == 20:
                        dve.wait_ge(dt_exp, 2)
                        log1p_exp(dte[:], dtu[:], dts[:], dt2[:], dtp[:])
                        chain(dve.scalar_tensor_tensor(dt[:], dtp[:], 2.0, dt[:], ALU.mult, ALU.add))
                        ab_ = ea[:, 0, :].unsqueeze(1).to_broadcast([P, NT, 16])
                        dve.scalar_tensor_tensor(dA[:], dt[:], -1.0, ab_, ALU.mult, ALU.mult).then_inc(dt_set, 1)

            def na_dve():
                dve.wait_ge(cv_ready, 8)
                for s in range(2):
                    dve.memset(bm[s][:, 256:512], 0.0).then_inc(bm_zero, 1)
                dve.wait_ge(bm_zero, 2)
                for g in range(8):
                    if g >= 2:
                        dve.wait_ge(vt_done, g - 1)
                    dve.tensor_copy(vst[g % 2][:].rearrange("p (c r w) -> p c r w", c=4, w=32),
                                    vT[:, :, 256 * (g % 2):256 * (g % 2) + 256].rearrange("p c (r w) -> p c r w", w=GRID_W)[
                                        :, :, :, STRIP0[g // 2]:STRIP0[g // 2] + 32]).then_inc(vst_ready, 1)

                def biased_max(u):
                    dve.wait_ge(s_done, u + 1)
                    st, bank = nst[:, u % 4, :], G[0][:, 512 * (u % 2):512 * (u % 2) + 512]
                    if u == 0:
                        dve.wait_ge(vs_ready, 10)
                    if u < 32:
                        dve.wait_ge(bm_ready, u + 1)
                        if u >= 2:
                            dve.wait_ge(p_ready, u - 1)
                        dve.tensor_tensor(nsS[u % 2][:], bank, bm[u % 2][:], ALU.add).then_inc(na_biased, 1)
                        dve.wait_ge(na_biased, u + 1)
                        dve.tensor_reduce(st[:, 0:1], nsS[u % 2][:], AX.X, ALU.max, negate=True).then_inc(nmax_ready, 1)
                    else:
                        dve.tensor_reduce(st[:, 0:2], bank.rearrange("p (w k) -> p w k", w=2), AX.X, ALU.max, negate=True
                                          ).then_inc(nmax_ready, 1)

                def scale_out(u):
                    h, st = u % 8, nst[:, u % 4, :]
                    nw = 1 if u < 32 else 2
                    dve.wait_ge(p_ready, u + 1)
                    dve.reciprocal(st[:, 4:4 + nw], st[:, 2:2 + nw]).then_inc(inv_ready, 1)
                    dve.wait_ge(inv_ready, u + 1)
                    dve.wait_ge(pv_done, u + 1)
                    if h == 0 and u // 8 >= 2:
                        dve.wait_ge(ot_done, min(u // 8 - 1, 4) if u < 32 else 4)
                    for w_ in range(nw):
                        o = NP[:, 512 * (u % 2) + 64 * w_:512 * (u % 2) + 64 * w_ + 64]
                        ins = dve.tensor_scalar(onorm[(u // 8 + w_) % 2][:, 64 * h:64 * h + 64], o, st[:, 4 + w_:5 + w_], None,
                                                ALU.mult)
                    ins.then_inc(o_read, 1)

                def out_lo(gi):
                    dve.wait_ge(cat_hi, gi + 1)
                    src = (B6, B7)[gi % 2].rearrange("p (c t) -> p c t", c=4)
                    if gi < 4:
                        for c in range(4):
                            ins = dve.tensor_tensor(cat_view(xl, gi)[:, c], src[:, c].rearrange("p (r w) -> p r w", w=16),
                                                    cat_view(xh, gi)[:, c].bitcast(F32), ALU.subtract)
                    else:
                        ins = dve.tensor_tensor(cat_view(xl, gi), src, cat_view(xh, gi).bitcast(F32), ALU.subtract)
                    ins.then_inc(na_cat, 1)

                for it in range(NU + 4):
                    if it < NU:
                        biased_max(it)
                    if 0 <= it - 3 < NU:
                        scale_out(it - 3)
                    if it >= 13 and (it - 13) % 8 == 0 and (it - 13) // 8 < 4:
                        out_lo((it - 13) // 8)
                out_lo(4)
                out_lo(5)

            def ssd_dve():
                dve.wait_ge(acs_mm, 1)
                dve.tensor_copy(acs[:].rearrange("p t c -> p (t c)"), NP[:, 0:96]).then_inc(acs_set, 1)
                dve.wait_ge(acs_set, 1)
                dve.tensor_tensor(tm[:].rearrange("p t c -> p (t c)"), NP[:, 512:608], acs[:].rearrange("p t c -> p (t c)"),
                                  ALU.subtract).then_inc(tm_set, 1)
                dve.wait_ge(dend_set, 2)
                dve.tensor_tensor(dend[:], dend[:], dt[:], ALU.mult).then_inc(dw_set, 1)
                for s in range(5):
                    for d in range(2):
                        e = 2 * s + d
                        tt = (FWD_SEQ, BWD_SEQ)[d][s]
                        if s:
                            if e > 2:
                                dve.wait_ge(h_set, e)
                            dve.wait_ge(h_set, e - 1)
                            dve.tensor_tensor(hm[:].rearrange("p (h q) -> p h q", q=64),
                                              hst[d][s - 1].rearrange("p (h q) -> p h q", q=64),
                                              heads(cdec[:, tt, 8 * d:8 * d + 8], 8, 64), ALU.mult).then_inc(hm_set, 1)
                            dve.wait_ge(hm_set, e - 1)
                        dve.wait_ge(st_mm, e + 1)
                        bank = G[1][:, 512 * d:512 * d + 512]
                        if s:
                            dve.tensor_tensor(hst[d][s], hm[:], bank, ALU.add).then_inc(h_set, 1)
                        else:
                            dve.tensor_copy(hst[d][s], bank).then_inc(h_set, 1)

                def decays(u):
                    tt, g, st = u // 2, u % 2, u % 2
                    dve.wait_ge(r_mm, u + 1)
                    if u >= 2:
                        dve.wait_ge(y_mm, u - 1)
                    for d in range(2):
                        dve.tensor_tensor(cbm[st][d][:], (B6, B7)[st][:, 0:P], cst(("trif", "trib")[d]), ALU.mult
                                          ).then_inc(cb_set, 1)
                    for d in range(2):
                        for hh_ in range(4):
                            col = 8 * d + 4 * g + hh_
                            r = slice(P * hh_, P * hh_ + P)
                            dve.tensor_scalar(sL[st][d][:, r], G[st][:, 512 * d + P * hh_:512 * d + P * hh_ + P],
                                              acs[:, tt, col:col + 1], 0.0, ALU.subtract, ALU.min).then_inc(d_ready, 1)

                def weights(u):
                    tt, g, st = u // 2, u % 2, u % 2
                    v3 = lambda ap: ap.rearrange("p (h i) -> p h i", h=4)
                    dve.wait_ge(cb_set, 2 * (u + 1))
                    for d in range(2):
                        dve.wait_ge(l_ready, 2 * u + d + 1)
                        dve.tensor_tensor(v3(sL[st][d][:]), v3(sL[st][d][:]),
                                          cbm[st][d][:].unsqueeze(1).to_broadcast([P, 4, P]), ALU.mult).then_inc(m_ready, 1)

                def read_y(tt):
                    dve.wait_ge(y_mm, 2 * tt + 2)
                    for c in range(4):
                        ins = dve.scalar_tensor_tensor(gy[:, c, P * tt:P * tt + P], cv[:, c, P * tt:P * tt + P],
                                                       pr("ssdd")[:, c:c + 1],
                                                       NP[:, 512 * (tt % 2) + P * c:512 * (tt % 2) + P * c + P],
                                                       ALU.mult, ALU.add)
                    ins.then_inc(y_read, 1)

                decays(0)
                for u in range(12):
                    weights(u)
                    if u + 1 < 12:
                        decays(u + 1)
                    if u % 2 == 1:
                        read_y(u // 2)
                for c in range(5):
                    if c < 4:
                        dve.wait_ge(gn_rs, 1)
                        if c >= 2:
                            dve.wait_ge(ssd_cat, c - 1)
                        dve.scalar_tensor_tensor(vg[c % 2][:], gy[:, c, :], pr("ssdg")[:, c:c + 1], rsg[:], ALU.mult, ALU.mult
                                                 ).then_inc(vg_ready, 1)
                    if c >= 1:
                        dve.wait_ge(gcat_hi, c)
                        dve.tensor_tensor(xl[:, 3 + c, :], vg[(c - 1) % 2][:], xh[:, 3 + c, :].bitcast(F32), ALU.subtract
                                          ).then_inc(ssd_cat, 1)

            def cd_in_dve():
                chain(dve.tensor_scalar(coef[:, 5, :], pr("lam"), -1.0, None, ALU.mult))
                dve.tensor_tensor(coef[:, 0, :], coef[:, 5, :], pr("lam"), ALU.max).then_inc(dl_set, 1)
                for q in range(2):
                    dve.scalar_tensor_tensor(t1b[q][:, 0:64], pr("dlam")[:, 128 * q:128 * q + 64], 1.0,
                                             pr("dlam")[:, 128 * q + 64:128 * q + 128], ALU.mult, ALU.mult,
                                             accum_out=dl[:, q:q + 1]).then_inc(dl_set, 1)
                chain(dve.tensor_scalar(qg2[:, 1:2], pr("dqg"), HD ** -0.5, None, ALU.mult))
                chain(dve.tensor_copy(qg2[:, 0:1], pr("dkg")))
                dve.tensor_scalar(dg[:, 0:1], pr("subg"), 1.0 - LAM_INIT, None, ALU.mult).then_inc(dg_set, 1)

                def kq_norm(i):
                    dve.wait_ge(kq_rs, 8 + i + 1)
                    ap = k2[:, i, :] if i < 4 else q2[:, i - 4, :]
                    dve.scalar_tensor_tensor(ap, ap, qg2[:, i // 4:i // 4 + 1], rstd[:, 0:T if i < 4 else NLAT],
                                             ALU.mult, ALU.mult).then_inc(kq_done, 1)

                def rotate(i):
                    dve.wait_ge(rope_mm, i + 1)
                    dve.wait_ge(rope_landed, 16)
                    if i:
                        dve.wait_ge(rope_done, i)
                    dve.tensor_tensor(t2b[:], (B6, B7)[i % 2], rope[:, 1, :], ALU.mult).then_inc(t2_set, 1)
                    dve.wait_ge(t2_set, i + 1)
                    dve.wait_ge(t1_ready, i + 1)
                    ap = k2[:, i, 0:NLAT] if i < 4 else q2[:, i - 4, :]
                    dve.tensor_tensor(ap, t1b[i % 2][:], t2b[:], ALU.add).then_inc(rope_done, 1)

                def conv(i):
                    t = CD + 12 + i
                    dve.wait_ge(psum_free[i % 2], t // 2 + 1)
                    if i >= 2:
                        dve.wait_ge(cv_ready, 8 + i - 1)
                    src, dst = pad[i % 2], cb[i % 2]
                    for k in range(4):
                        tap = pr("lcw")[:, 4 * i + k:4 * i + k + 1]
                        if k == 0:
                            ins = dve.tensor_scalar(dst[:], src[:, 0:771], tap, None, ALU.mult)
                        else:
                            ins = dve.scalar_tensor_tensor(dst[:], src[:, k:k + 771], tap, dst[:], ALU.mult, ALU.add)
                        if k < 3:
                            ins.then_inc(conv_tap, 1)
                            dve.wait_ge(conv_tap, 24 + 3 * i + k + 1)
                    ins.then_inc(conv_done, 1)

                for c in range(CD_IN_T):
                    t, s = CD + c, c % 2
                    if 5 <= c < 9:
                        i = c - 5
                        dve.wait_ge(kq_sq, 16 + 2 * i + 2)
                        dve.tensor_tensor(sql[:], sq[i % 2][:], sqh[:].bitcast(F32), ALU.subtract).then_inc(sql_set, 1)
                    if c < 12:
                        dve.wait_ge(mm_done, t + 1)
                        if c < 8:
                            dve.tensor_copy(vT2[:, c, :] if c < 4 else k2[:, c - 4, :], G[s][:, 0:T]).then_inc(psum_free[s], 1)
                        else:
                            dve.tensor_copy(q2[:, c - 8, :], G[s][:, 0:NLAT]).then_inc(psum_free[s], 1)
                    split_lo(t + 2, s, KC)
                    if c == 3:
                        dve.wait_ge(coef_exp, 1)
                        log1p_exp(coef[:, 1, :], coef[:, 2, :], coef[:, 3, :], coef[:, 4, :], coef[:, 6, :])
                        chain(dve.tensor_scalar(coef[:, 5, :], coef[:, 5, :], 0.0, None, ALU.max))
                        chain(dve.scalar_tensor_tensor(coef[:, 7, :], coef[:, 6, :], 2.0, coef[:, 5, :], ALU.mult, ALU.add))
                        chain(dve.tensor_scalar(coef[:, 6, :], coef[:, 7, :], -8.0, None, ALU.mult))
                        dve.tensor_scalar(coef[:, 7, :], coef[:, 7, :], 8.0, None, ALU.mult).then_inc(coef_set, 1)
                        dve.wait_ge(dl_exp, 1)
                        chain(dve.tensor_tensor(dl[:, 4:5], dl[:, 3:4], dl[:, 2:3], ALU.subtract))
                        dve.tensor_scalar(dl[:, 5:6], dl[:, 4:5], -LAM_INIT, None, ALU.add).then_inc(dlam_set, 1)
                    if c == 4:
                        for s_ in range(2):
                            ins = dve.memset(pad[s_][:], 0.0)
                        ins.then_inc(pad_zero, 1)
                    if 5 <= c < 13:
                        kq_norm(c - 5)
                    if 8 <= c < 16:
                        rotate(c - 8)
                    if 12 <= c < 16:
                        conv(c - 12)

            def cd_mid_dve():
                def comp(p_):
                    for d in range(2):
                        e = 2 * p_ + d
                        dve.wait_ge(lru_t, e + 1)
                        dve.wait_ge(lru_a2, e + 1)
                        dve.scalar_tensor_tensor(lR[d][:], lX[d][:], 1.0, lR[d][:], ALU.add, ALU.mult).then_inc(lru_m, 1)

                def scan(p_):
                    for d in range(2):
                        e = 2 * p_ + d
                        dve.wait_ge(lru_b, e + 1)
                        A_, B_, X_ = lA[d], lI[d], lX[d]
                        if d == 0:
                            dve.tensor_tensor_scan(X_[:, NLAT:T], A_[:, NLAT:T], B_[:, NLAT:T], 0.0, ALU.mult, ALU.add
                                                   ).then_inc(scan_c, 1)
                            dve.wait_ge(scan_c, e + 1)
                            dve.tensor_tensor_scan(hsum[:, p_, :], A_[:, 0:NLAT], B_[:, 0:NLAT], X_[:, T - 1:T],
                                                   ALU.mult, ALU.add).then_inc(scan_l, 1)
                        else:
                            dve.tensor_tensor_scan(X_[:, T - 1:NLAT - 1:-1], A_[:, T - 1:NLAT - 1:-1],
                                                   B_[:, T - 1:NLAT - 1:-1], 0.0, ALU.mult, ALU.add).then_inc(scan_c, 1)
                            dve.wait_ge(scan_c, e + 1)
                            dve.tensor_tensor_scan(X_[:, NLAT - 1::-1], A_[:, NLAT - 1::-1], B_[:, NLAT - 1::-1],
                                                   X_[:, NLAT:NLAT + 1], ALU.mult, ALU.add).then_inc(scan_l, 1)
                    dve.wait_ge(scan_l, 2 * p_ + 2)
                    dve.tensor_tensor(hsum[:, p_, :], hsum[:, p_, :], lX[1][:, 0:NLAT], ALU.add).then_inc(lru_h, 1)

                def gated(p_):
                    dve.wait_ge(lru_h, p_ + 1)
                    dve.tensor_tensor(hsum[:, p_, :], hsum[:, p_, :], gate[:, p_, :], ALU.mult).then_inc(lru_o, 1)

                def lo(p_):
                    dve.wait_ge(lru_hi, p_ + 1)
                    dve.tensor_tensor(xl[:, p_, 0:NLAT], hsum[:, p_, :], xh[:, p_, 0:NLAT].bitcast(F32), ALU.subtract
                                      ).then_inc(cd_cat, 1)

                def att(a):
                    if a >= 4:
                        b = a - 4
                        dve.wait_ge(pv2_done, b + 1)
                        dve.tensor_scalar(onq[b // 4][:, P * (b % 4):P * (b % 4) + P], (B6, B7)[b % 2][:, 0:P],
                                          st2[:, b % 4, 4:5], None, ALU.mult).then_inc(on_done, 1)
                    if a < NA2:
                        for s in range(2):
                            dve.wait_ge(s2_done, 2 * a + s + 1)
                            dve.tensor_reduce(st2[:, a % 4, s:s + 1], G[s][:, 0:T], AX.X, ALU.max, negate=True
                                              ).then_inc(max2_ready, 1)
                    if 1 <= a <= NA2:
                        b = a - 1
                        st = st2[:, b % 4, :]
                        dve.wait_ge(p2_ready, 2 * b + 2)
                        if b >= 4:
                            dve.wait_ge(on_done, b - 3)
                        dve.reciprocal(st[:, 4:6], st[:, 2:4]).then_inc(inv_ready, 1)
                        dve.wait_ge(inv_ready, NU + 2 * b + 1)
                        dve.scalar_tensor_tensor(st[:, 6:7], st[:, 5:6], dl[:, 5:6], st[:, 2:3], ALU.mult, ALU.mult
                                                 ).then_inc(inv_ready, 1)
                        dve.wait_ge(inv_ready, NU + 2 * b + 2)
                        if b >= 2:
                            dve.wait_ge(tr2_done, b - 1)
                        dve.scalar_tensor_tensor(wb[b % 2][:], pb[b % 2][1][:], st[:, 6:7], pb[b % 2][0][:], ALU.mult, ALU.add
                                                 ).then_inc(w_done, 1)

                dve.wait_ge(dlam_set, 1)
                for what, i in SCHED:
                    if what == "comp":
                        comp(i)
                    if what == "scan":
                        scan(i)
                    if what == "gated":
                        gated(i)
                    if what == "lo":
                        lo(i)
                    if what == "att":
                        att(i)
                dve.wait_ge(dg_set, 1)
                dve.wait_ge(rr_ready, 1)
                for qt in range(4):
                    ap = onq[qt][:].rearrange("p (h d) -> p h d", h=4)
                    dve.tensor_tensor(ap, ap, heads(hrs[:, 4 * qt:4 * qt + 4], 4, P), ALU.mult).then_inc(onr_done, 1)
                for qt in range(5):
                    if qt < 4:
                        dve.wait_ge(oq_done, qt + 1)
                        if qt >= 2:
                            dve.wait_ge(cd_cat2, qt - 1)
                        dve.tensor_scalar(ovb[qt % 2][:], (B6, B7)[qt % 2], dg[:, 0:1], None, ALU.mult).then_inc(ov_ready, 1)
                    if qt:
                        q = qt - 1
                        dve.wait_ge(oq_hi, qt)
                        dve.tensor_tensor(xl[:, 4:8, P * q:P * q + P], ovb[q % 2][:].rearrange("p (h t) -> p h t", h=4),
                                          xh[:, 4:8, P * q:P * q + P].bitcast(F32), ALU.subtract).then_inc(cd_cat2, 1)

            dve.memset(eps[:], EPS).then_inc(eps_set, 1)
            dve.wait_ge(scb0_ready, 1)
            for q, j in enumerate(DVE_MINI):
                dve.wait_ge(mini_landed[group(j)], 16 * len(MINI_GROUPS[group(j)]))
                for s in range(2):
                    if q + s:
                        dve.wait_ge(mini_dot, 2 * q + s)
                    dot(mini[j][:], s, scb0, M[:, j, s:s + 1]).then_inc(mini_dot, 1)
                if q in (6, 7):
                    split_lo(q - 6, q - 6, KC)
            dve.wait_ge(par_landed, 16)
            dve.wait_ge(mini_mm, 1)
            dve.wait_ge(mini_dot, 2 * len(DVE_MINI))
            pairs = G[0][:, 0:4 * KC].rearrange("p (t s) -> p t s", s=2)
            for js, src in ((slice(1, 14, 2), pairs), (slice(0, 15, 2), M), (slice(15, 16), M)):
                n_ = len(range(16)[js])
                dve.tensor_tensor(M[:, js, :], src[:, js, :], pr("bmod")[:, js].unsqueeze(2).to_broadcast([P, n_, 2]), ALU.add
                                  ).then_inc(mini_set, 1)
            dve.wait_ge(mini_set, 3)
            prep(0, 0)
            norm(0, SEGS)
            ffn(0, 0, BASE["ffn0"], KC, 0, SEGS)
            prep(1, 20)
            norm(1, SEGS)
            ab_in_dve()
            na_dve()
            ssd_dve()
            down(ABO, KC, KC, 1, SEGS)
            prep(2, 20)
            norm(2, SEGS)
            ffn(1, 2, BASE["ffn1"], KC, 20, SEGS)
            prep(3, 40)
            norm(3, SEGS)
            ffn(2, 3, BASE["ffn2"], KC, None, SEGS)
            prep(4, 40)
            norm(4, SEGS)
            cd_in_dve()
            cd_mid_dve()
            down(CDO, KC, KC, 4, LSEG)
            prep(5, 40)
            norm(5, LSEG)
            ffn(3, 5, BASE["ffn3"], 0, None, LSEG)

        @block.gpsimd
        def _(pool):
            def add_squares(n, ns):
                for j in range(KC - 1):
                    pool.wait_ge(sq_done, 8 * n + j + 1)
                    if j == 0:
                        pool.tensor_copy(ssq[:, 0:ns], sq[0][:, 0:ns]).then_inc(ssq_acc, 1)
                    else:
                        pool.wait_ge(ssq_acc, 7 * n + j)
                        pool.tensor_tensor(ssq[:, 0:ns], ssq[:, 0:ns], sq[j % 2][:, 0:ns], ALU.add
                                           ).then_inc(ssq_acc, 1)

            def norm(n, ns):
                add_squares(n, ns)
                pool.wait_ge(rstd_ready, n + 1)
                for j in range(1, KC):
                    if j >= 2:
                        pool.wait_ge(aff_done, 8 * n + j - 1)
                    pool.tensor_tensor(vn[j % 2][:, 0:ns], x[:, j, 0:ns], rstd[:, 0:ns], ALU.mult
                                       ).then_inc(v_ready, 1)

            def prod_mods(it0):
                with pool.Fori(0, FH - 1) as i:
                    for j in range(3):
                        pool.wait_ge(mod_dot, i * 3 + (3 * it0 + j + 1))
                        pool.tensor_tensor(mraw[:, j, :], mraw[:, j, :], scb[:, 1, :], ALU.mult).then_inc(mod_prod, 1)

            def ab_pool():
                pool.wait_ge(rb_landed, 16 * ROWS)
                pool.wait_ge(mask_landed, 16)
                pool.wait_ge(bm_zero, 2)
                for u in range(32):
                    n, h = u // 8, u % 8
                    if u >= 2:
                        pool.wait_ge(na_biased, u - 1)
                    row = rb[:, h, 16 - STRIP_OFF[n]:48 - STRIP_OFF[n]]
                    win = bass.AP(tensor=row.tensor, offset=row.offset, ap=[row.ap[0], [RPB_ROW, ROWS], [1, 32]])
                    pool.tensor_tensor(bm[u % 2][:, 0:256].rearrange("p (r c) -> p r c", c=32), win,
                                       namask[:, (0, 1, 1, 2)[n], :].rearrange("p (r c) -> p r c", c=32), ALU.add
                                       ).then_inc(bm_ready, 1)
                pool.wait_ge(dw_set, 1)
                pool.wait_ge(tk_ready, 9)
                for e in range(10):
                    d, tt = e % 2, (FWD_SEQ, BWD_SEQ)[e % 2][e // 2]
                    if e >= 2:
                        pool.wait_ge(st_mm, e - 1)
                    pool.tensor_tensor(xw[e % 2][:].rearrange("p (h q) -> p h q", q=64),
                                       xst[:, tt, :].rearrange("p (h q) -> p h q", q=64),
                                       heads(dend[:, tt, 8 * d:8 * d + 8], 8, 64), ALU.mult).then_inc(xw_ready, 1)

                def gate(tt):
                    pool.wait_ge(y_read, tt + 1)
                    tk = slice(P * tt, P * tt + P)
                    pool.tensor_tensor(gy[:, :, tk], gy[:, :, tk], zs[:, :, tk], ALU.mult).then_inc(gz_done, 1)

                for u in range(12):
                    tt, g, st = u // 2, u % 2, u % 2
                    if u == 0:
                        pool.wait_ge(na_cat, 6)
                    if u >= 2:
                        pool.wait_ge(y_mm, u - 1)
                    for d in range(2):
                        pool.tensor_tensor(xdt[st][d][:].rearrange("p (h q) -> p h q", q=64),
                                           xst[:, tt, 256 * g:256 * g + 256].rearrange("p (h q) -> p h q", q=64),
                                           heads(dt[:, tt, 8 * d + 4 * g:8 * d + 4 * g + 4], 4, 64), ALU.mult
                                           ).then_inc(xdt_ready, 1)
                    for d in range(2):
                        pool.wait_ge(e_ready, 2 * u + d + 1)
                        v = sE[st][d][:].rearrange("p (h i) -> p h i", h=4)
                        pool.tensor_tensor(v, v, cv[:, 6 + g, P * tt:P * tt + P].unsqueeze(1).to_broadcast([P, 4, P]), ALU.mult
                                           ).then_inc(xdt_ready, 1)
                    if g == 1 and tt >= 1:
                        gate(tt - 1)
                gate(5)

            def cd_pool():
                pool.wait_ge(rope_landed, 16)
                for i in range(8):
                    pool.wait_ge(kq_done, 8 + i + 1)
                    pool.wait_ge(dl_set, 3)
                    if i >= 2:
                        pool.wait_ge(rope_done, i - 1)
                    src = k2[:, i, 0:NLAT] if i < 4 else q2[:, i - 4, :]
                    pool.tensor_tensor(t1b[i % 2][:], src, rope[:, 0, :], ALU.mult).then_inc(t1_ready, 1)
                for p_ in range(4):
                    for d in range(2):
                        pool.wait_ge(gate_sig, 4 * p_ + 2 * d + 2)
                        pool.tensor_tensor(lI[d][:], lI[d][:], xc[:, p_, :], ALU.mult).then_inc(lru_ix, 1)
                    for d in range(2):
                        pool.wait_ge(lru_a, 2 * p_ + d + 1)
                        pool.tensor_tensor(lX[d][:], lA[d][:], lA[d][:], ALU.mult).then_inc(lru_a2, 1)
                    for d in range(2):
                        pool.wait_ge(lru_q, 2 * p_ + d + 1)
                        pool.wait_ge(lru_ix, 2 * p_ + d + 1)
                        pool.tensor_tensor(lI[d][:], lI[d][:], lR[d][:], ALU.mult).then_inc(lru_b, 1)

            norm(0, T)
            prod_mods(0)
            prod_mods(10)
            norm(1, T)
            ab_pool()
            norm(2, T)
            prod_mods(20)
            prod_mods(30)
            norm(3, T)
            norm(4, T)
            cd_pool()
            norm(5, NLAT)


def host_arrays(a):
    f = np.float32

    def tiles(w_, cols=None):
        k, n = w_.shape
        return np.ascontiguousarray(w_.reshape(k // P, P, n // P, P).transpose(2, 1, 0, 3)).reshape(n // P, P, k)

    def vec(v):
        return np.asarray(v).reshape(-1, P).T

    out = {}
    xt = np.concatenate([a["x"][0], a["ctx"][0]], axis=0).T
    out["x"] = np.ascontiguousarray(xt.reshape(KC, P, T).transpose(1, 0, 2))
    out["wmn"] = np.stack([a["w_mod"][i].T.reshape(NMT, P, D) for i in range(2)]).reshape(2 * NMT, P, D)
    out["wmk"] = tiles(a["w_mod"][0][:, 0:16 * P])[list(PE_MINI)]
    out["ccb"] = np.broadcast_to(np.stack([a["c"][0], a["c_ctx"]])[None], (P, 2, D))
    w13, w2 = [], []
    for i in range(2):
        for h in range(2):
            t1, t3 = tiles(a["ffn_w1"][i, h]), tiles(a["ffn_w3"][i, h])
            w13.append(np.stack([t1, t3], 1).reshape(2 * FC, P, D))
            for q in range(2):
                w2.append(tiles(a["ffn_w2"][i, h][q * FH * P:(q + 1) * FH * P]))
    out["w13"], out["w2"] = np.concatenate(w13), np.concatenate(w2)

    abw, gw = a["ab_w_in"][0], 512
    order = [(2 * gw, 3 * gw), (gw, 2 * gw), (0, gw), (4 * gw, 6 * gw), (3 * gw, 4 * gw)]
    out["abin"] = np.concatenate([tiles(abw[:, p:q]) for p, q in order])
    out["wdt"] = np.ascontiguousarray(abw[:, 6 * gw:].reshape(KC, P, 16).transpose(1, 0, 2)).reshape(P, KC * 16)
    out["about"] = tiles(a["ab_w_out"][0])
    cdw = a["cd_w_in"][0]
    order = [(4 * gw, 5 * gw), (3 * gw, 4 * gw), (2 * gw, 3 * gw), (gw, 2 * gw), (0, gw)]
    out["cdin"] = np.concatenate([tiles(cdw[:, p:q]) for p, q in order])
    out["cdout"] = tiles(a["cd_w_out"][0])
    bd = np.zeros((2, 2, 4, P, P), f)
    for g, n in enumerate(("lru_wa", "lru_wx")):
        for b in range(2):
            bd[g, :, :, 64 * b:64 * b + 64, 64 * b:64 * b + 64] = a[n][0].reshape(2, 4, 2, 64, 64)[:, :, b]
    out["lruw"] = np.ascontiguousarray(bd.reshape(16, P, P).transpose(1, 0, 2)).reshape(P, 16 * P)
    table = np.zeros(RPB_LEN + 16, f)
    table[RPB_PAD:RPB_PAD + 8 * RPB_HEAD] = np.asarray(a["na_rpb"][0]).reshape(-1)
    out["rpb"] = np.stack([np.roll(table, c)[:RPB_LEN] for c in range(16)])

    def rep(v):
        return np.broadcast_to(np.asarray(v).reshape(1, -1), (P, np.asarray(v).size))

    def two(v):
        return np.concatenate([v, v]).reshape(P, 1)

    par = {
        "bmod": vec(a["b_mod"].reshape(-1)), "normg": vec(a["norm_g"].reshape(-1)),
        "naqg": two(a["na_q_g"][0]), "nakg": two(a["na_k_g"][0]),
        "scw": a["ssd_conv_w"][0].reshape(4, 8, P).transpose(2, 1, 0).reshape(P, 32),
        "scb": vec(a["ssd_conv_b"][0]), "dtb": rep(a["ssd_dt_bias"][0]), "alog": rep(a["ssd_a_log"][0]),
        "ssdd": np.repeat(a["ssd_d"][0], 64).reshape(4, P).T, "ssdg": vec(a["ssd_norm_g"][0]),
        "lcw": a["lru_conv_w"][0].reshape(4, 4, P).transpose(2, 1, 0).reshape(P, 16),
        "lcb": vec(a["lru_conv_b"][0]), "lba": vec(a["lru_ba"][0].reshape(-1)),
        "lbx": vec(a["lru_bx"][0].reshape(-1)), "lam": vec(a["lru_lambda"][0].reshape(-1)),
        "dqg": two(a["diff_q_g"][0]), "dkg": two(a["diff_k_g"][0]), "subg": vec(a["diff_subln_g"][0]),
        "dlam": rep(a["diff_lambda"][0]),
        "cc": np.stack([vec(a["c"][0]), vec(a["c_ctx"])], 2).reshape(P, 16),
    }
    out["par"] = np.concatenate([par[n] for n in PCOL], axis=1)

    i = np.arange(P)
    swap = np.zeros((P, P), f)
    swap[i[0::2] + 1, i[0::2]] = -1.0
    swap[i[0::2], i[0::2] + 1] = 1.0
    con = {"ident": np.eye(P, dtype=f), "ones": np.ones((P, P), f),
           "blk": (i[:, None] // 64 == i[None] // 64).astype(f),
           "trif": (i[:, None] <= i[None]).astype(f), "trib": (i[:, None] >= i[None]).astype(f), "swap": swap}
    out["con"] = np.concatenate([con[n] for n in CCOL], axis=1)
    t = np.arange(NLAT)
    inv = (10000.0 ** (-np.arange(16, dtype=f) / 16)).astype(f)
    ang = np.concatenate([(t // GRID_W).astype(f)[:, None] * inv, (t % GRID_W).astype(f)[:, None] * inv], 1)
    pair = (i % 64) // 2
    out["rope"] = np.stack([np.cos(ang).T[pair], np.sin(ang).T[pair]], 1).astype(f)
    kc, qc = np.arange(32), np.arange(16)
    mask = np.zeros((3, P, ROWS, 32), f)
    for v, blk_ in enumerate((0, 1, 3)):
        q0 = np.clip(16 * blk_ + qc - 8, 0, GRID_W - 16)
        col = STRIP0[blk_] + kc
        ok = (col[None] >= q0[:, None]) & (col[None] < q0[:, None] + 16)
        mask[v] = np.where(np.tile(ok, (ROWS, 1))[:, None, :], 0.0, -1e30)
    out["mask"] = np.ascontiguousarray(mask.reshape(3, P, 256).transpose(1, 0, 2))
    return {k: np.ascontiguousarray(v, dtype=f) for k, v in out.items()}


def kernel(**inputs):
    import concourse.bacc as bacc
    from concourse.bass_utils import run_bass_kernel_spmd

    arrays = host_arrays({k: np.asarray(v) for k, v in inputs.items()})
    nc = bacc.Bacc("TRN2", target_bir_lowering=False, num_devices=1, dynamic_dma_scratch_size=1024)
    dr = {k: nc.dram_tensor("in_" + k, v.shape, F32, kind="ExternalInput").ap() for k, v in arrays.items()}
    dr["out"] = nc.dram_tensor("out_t", (P, KC, NLAT), F32, kind="ExternalOutput").ap()
    build(nc, dr)
    r = run_bass_kernel_spmd(nc, [{"in_" + k: v for k, v in arrays.items()}], core_ids=[0])
    o = r.results[0]["out_t"]
    return np.ascontiguousarray(o.transpose(2, 1, 0)).reshape(1, NLAT, D)
```
